# Optimizing a Trainium2 kernel written in Bass

```python
import jax, jax.numpy as jnp
from jax import lax
import numpy as np

D_MODEL = 1024
BATCH = 1
SEQ = 1024
DEPTH = 1
DEC_BATCH = 8
DEC_SEQ = 4
PAST_LEN = 8192
PAGE_SIZE = 128

HEAD_DIM = 64
N_HEADS = 8
D_ATTN = N_HEADS * HEAD_DIM
D_CONV = D_MODEL - D_ATTN
CONV_WIDTH = 3
WINDOWS = (128, 512, 2048)
DILATIONS = (1, 4, 16)
MAX_WINDOW = max(WINDOWS)
Q_BLOCK = 128
D_IN = 3 * D_ATTN + 3 * D_CONV
D_FF = -(-8 * D_MODEL // (3 * 256)) * 256
RMS_EPS = 1e-6
ATTN_SCALE = HEAD_DIM ** -0.5
NEG_INF = -1e30

kernel_name = "hymba_longnet_shortconv_step"

def rms_norm(x, g):
    xf = x.astype(jnp.float32)
    y = xf * lax.rsqrt(jnp.mean(xf * xf, axis=-1, keepdims=True) + RMS_EPS)
    return (y * g.astype(jnp.float32)).astype(x.dtype)

def alibi_slopes():
    return jnp.exp2(-8.0 * jnp.arange(1, N_HEADS + 1, dtype=jnp.float32) / N_HEADS)

def _project(xn, w_in):
    b, t, _ = xn.shape
    z = xn @ w_in
    q, k, v, hc, gb, gc = jnp.split(
        z, [D_ATTN, 2 * D_ATTN, 3 * D_ATTN, 3 * D_ATTN + D_CONV, 3 * D_ATTN + 2 * D_CONV], axis=-1)
    heads = lambda a: a.reshape(b, t, N_HEADS, HEAD_DIM)
    return heads(q), heads(k), heads(v), hc, gb, gc

def _short_conv(u_ext, w_conv, t):
    acc = w_conv[0] * u_ext[:, 0:t]
    for i in range(1, CONV_WIDTH):
        acc = acc + w_conv[i] * u_ext[:, i:i + t]
    return acc

def _dilated_prompt(q, k, v, window, dilation, slopes):
    b, s, h, hd = q.shape
    nk = window // dilation
    n_sub = s // dilation
    nb = -(-n_sub // Q_BLOCK)
    lp = nb * Q_BLOCK

    def classes(a, front):
        a = a.reshape(b, n_sub, dilation, h, hd).transpose(0, 2, 1, 3, 4)
        return jnp.pad(a, ((0, 0), (0, 0), (front, lp - n_sub), (0, 0), (0, 0)))

    qb = classes(q, 0).reshape(b, dilation, nb, Q_BLOCK, h, hd)
    kidx = jnp.arange(nb)[:, None] * Q_BLOCK + jnp.arange(Q_BLOCK + nk)[None, :]
    kb = jnp.take(classes(k, nk), kidx, axis=2)
    vb = jnp.take(classes(v, nk), kidx, axis=2)
    s_qk = jnp.einsum('brnqhd,brnkhd->brnhqk', qb, kb) * ATTN_SCALE
    dist = jnp.arange(Q_BLOCK)[:, None] + nk - jnp.arange(Q_BLOCK + nk)[None, :]
    key_sub = kidx - nk
    valid = (dist >= 0)[None] & (dist <= nk)[None] & (key_sub >= 0)[:, None, :]
    bias = -slopes[:, None, None] * (dilation * dist).astype(jnp.float32)[None]
    s_qk = jnp.where(valid[None, None, :, None], s_qk + bias, NEG_INF)
    m = s_qk.max(-1)
    p = jnp.exp(s_qk - m[..., None])
    l = p.sum(-1)
    o = jnp.einsum('brnhqk,brnkhd->brnqhd', p, vb) / jnp.swapaxes(l, -1, -2)[..., None]

    def back(a):
        a = a.reshape((b, dilation, lp) + a.shape[4:])[:, :, :n_sub]
        return jnp.swapaxes(a, 1, 2).reshape((b, s) + a.shape[3:])

    return back(jnp.swapaxes(m, -1, -2)), back(jnp.swapaxes(l, -1, -2)), back(o)

def _dilated_sample(q, k_all, v_all, n_past, window, dilation, slopes):
    t = q.shape[1]
    nk = window // dilation
    j = jnp.arange(nk + 1)
    idx = n_past + jnp.arange(t)[:, None] - dilation * j[None, :]
    valid = idx >= 0
    idx = jnp.maximum(idx, 0)
    kg = k_all[:, idx]
    vg = v_all[:, idx]
    s_qk = (jnp.einsum('bthd,btjhd->bhtj', q, kg) * ATTN_SCALE
            - slopes[:, None, None] * (dilation * j).astype(jnp.float32))
    s_qk = jnp.where(valid, s_qk, NEG_INF)
    m = s_qk.max(-1)
    p = jnp.exp(s_qk - m[..., None])
    l = p.sum(-1)
    o = jnp.einsum('bhtj,btjhd->bthd', p, vg) / jnp.swapaxes(l, 1, 2)[..., None]
    return jnp.swapaxes(m, 1, 2), jnp.swapaxes(l, 1, 2), o

def _merge_branches(parts):
    m = jnp.stack([p[0] for p in parts])
    l = jnp.stack([p[1] for p in parts])
    o = jnp.stack([p[2] for p in parts])
    w = l * jnp.exp(m - m.max(0, keepdims=True))
    return (w[..., None] * o).sum(0) / w.sum(0)[..., None]

def _finish(x, attn_o, conv_o, w_out, norm_ffn_g, w_gate, w_up, w_down):
    b, t, _ = x.shape
    mix = jnp.concatenate([attn_o.reshape(b, t, D_ATTN).astype(x.dtype), conv_o], axis=-1)
    h = x + mix @ w_out
    hn = rms_norm(h, norm_ffn_g)
    return h + (jax.nn.silu(hn @ w_gate) * (hn @ w_up)) @ w_down

def _layer_prompt(x, norm_mix_g, w_in, w_conv, w_out, norm_ffn_g, w_gate, w_up, w_down):
    t = x.shape[1]
    xn = rms_norm(x, norm_mix_g)
    q, k, v, hc, gb, gc = _project(xn, w_in)
    slopes = alibi_slopes()
    qf, kf, vf = q.astype(jnp.float32), k.astype(jnp.float32), v.astype(jnp.float32)
    parts = [_dilated_prompt(qf, kf, vf, w, d, slopes) for w, d in zip(WINDOWS, DILATIONS)]
    attn_o = _merge_branches(parts)
    u = gc * hc
    u_ext = jnp.pad(u, ((0, 0), (CONV_WIDTH - 1, 0), (0, 0)))
    conv_o = gb * _short_conv(u_ext, w_conv, t)
    y = _finish(x, attn_o, conv_o, w_out, norm_ffn_g, w_gate, w_up, w_down)
    keep = min(MAX_WINDOW, t)
    return y, k[:, t - keep:], v[:, t - keep:], u_ext[:, -(CONV_WIDTH - 1):]

def _layer_sample(x, k_buf, v_buf, conv_buf, norm_mix_g, w_in, w_conv, w_out,
                  norm_ffn_g, w_gate, w_up, w_down):
    t = x.shape[1]
    xn = rms_norm(x, norm_mix_g)
    q, k, v, hc, gb, gc = _project(xn, w_in)
    slopes = alibi_slopes()
    n_past = k_buf.shape[1]
    k_all = jnp.concatenate([k_buf.astype(k.dtype), k], axis=1).astype(jnp.float32)
    v_all = jnp.concatenate([v_buf.astype(v.dtype), v], axis=1).astype(jnp.float32)
    qf = q.astype(jnp.float32)
    parts = [_dilated_sample(qf, k_all, v_all, n_past, w, d, slopes)
             for w, d in zip(WINDOWS, DILATIONS)]
    attn_o = _merge_branches(parts)
    u = gc * hc
    u_ext = jnp.concatenate([conv_buf.astype(u.dtype), u], axis=1)
    conv_o = gb * _short_conv(u_ext, w_conv, t)
    y = _finish(x, attn_o, conv_o, w_out, norm_ffn_g, w_gate, w_up, w_down)
    return y, k, v, u_ext[:, -(CONV_WIDTH - 1):]

def setup_inputs(seed: int = 0) -> dict:
    key = jax.random.key(seed)
    ks = jax.random.split(key, 16)
    f32 = jnp.float32
    n_buf = min(MAX_WINDOW, PAST_LEN)

    def nrm(k, shape, scale):
        return jax.random.normal(k, shape, f32) * scale

    return {
        'x_prompt': nrm(ks[0], (BATCH, SEQ, D_MODEL), 1.0),
        'x_sample': nrm(ks[1], (DEC_BATCH, DEC_SEQ, D_MODEL), 1.0),
        'state_attn_k': nrm(ks[2], (DEPTH, DEC_BATCH, n_buf, N_HEADS, HEAD_DIM), 1.0),
        'state_attn_v': nrm(ks[3], (DEPTH, DEC_BATCH, n_buf, N_HEADS, HEAD_DIM), 1.0),
        'state_conv': nrm(ks[4], (DEPTH, DEC_BATCH, CONV_WIDTH - 1, D_CONV), 1.0),
        'norm_mix_g': 1.0 + nrm(ks[5], (DEPTH, D_MODEL), 0.01),
        'w_in': nrm(ks[6], (DEPTH, D_MODEL, D_IN), D_MODEL ** -0.5),
        'w_conv': nrm(ks[7], (DEPTH, CONV_WIDTH, D_CONV), CONV_WIDTH ** -0.5),
        'w_out': nrm(ks[8], (DEPTH, D_ATTN + D_CONV, D_MODEL), (D_ATTN + D_CONV) ** -0.5),
        'norm_ffn_g': 1.0 + nrm(ks[9], (DEPTH, D_MODEL), 0.01),
        'w_gate': nrm(ks[10], (DEPTH, D_MODEL, D_FF), D_MODEL ** -0.5),
        'w_up': nrm(ks[11], (DEPTH, D_MODEL, D_FF), D_MODEL ** -0.5),
        'w_down': nrm(ks[12], (DEPTH, D_FF, D_MODEL), D_FF ** -0.5),
        'norm_final_g': 1.0 + nrm(ks[13], (D_MODEL,), 0.01),
    }

def reference(x_prompt, x_sample, state_attn_k, state_attn_v, state_conv, norm_mix_g, w_in,
              w_conv, w_out, norm_ffn_g, w_gate, w_up, w_down, norm_final_g):
    yp, ys = x_prompt, x_sample
    kp_l, vp_l, cp_l, ks_l, vs_l, cs_l = [], [], [], [], [], []
    for layer in range(DEPTH):
        yp, kp, vp, cp = _layer_prompt(yp, norm_mix_g[layer], w_in[layer], w_conv[layer],
                                       w_out[layer], norm_ffn_g[layer], w_gate[layer],
                                       w_up[layer], w_down[layer])
        ys, ks, vs, cs = _layer_sample(ys, state_attn_k[layer], state_attn_v[layer],
                                       state_conv[layer], norm_mix_g[layer], w_in[layer],
                                       w_conv[layer], w_out[layer], norm_ffn_g[layer],
                                       w_gate[layer], w_up[layer], w_down[layer])
        kp_l.append(kp); vp_l.append(vp); cp_l.append(cp)
        ks_l.append(ks); vs_l.append(vs); cs_l.append(cs)
    y_prompt = rms_norm(yp, norm_final_g)
    y_sample = rms_norm(ys, norm_final_g)
    new_k_prompt = jnp.stack(kp_l)
    new_v_prompt = jnp.stack(vp_l)
    new_conv_prompt = jnp.stack(cp_l)
    new_k_sample = jnp.stack(ks_l)
    new_v_sample = jnp.stack(vs_l)
    new_conv_sample = jnp.stack(cs_l)
    return (y_prompt, y_sample, new_k_prompt, new_v_prompt, new_conv_prompt,
            new_k_sample, new_v_sample, new_conv_sample)


_drawn_inputs = setup_inputs


def setup_inputs(seed=0):
    import zlib

    import numpy as np

    out = dict(_drawn_inputs(seed))
    spreads = {}
    factors = {'norm_mix_g': 3.827,
     'norm_ffn_g': 39.864,
     'norm_final_g': 30.028,
     'state_attn_k': 2.942,
     'state_attn_v': 3.572}
    for name, (base, spread) in spreads.items():
        noise = np.random.default_rng([zlib.crc32(name.encode()), seed]).standard_normal(out[name].shape)
        drawn = base * np.exp(spread * noise) if base else spread * noise
        out[name] = __import__('jax').numpy.asarray(drawn.astype(out[name].dtype))
    for name, factor in factors.items():
        out[name] = (out[name] * factor).astype(out[name].dtype)
    return out
```

```python
from contextlib import ExitStack

import numpy as np

import concourse.bass as bass
from concourse import mybir

F32 = mybir.dt.float32
F32R = mybir.dt.float32r
I32 = mybir.dt.int32
I16 = mybir.dt.int16
ALU = mybir.AluOpType
ACT = mybir.ActivationFunctionType
AX = mybir.AxisListType

P = 128
D = 1024
KT = D // P
PROMPT = 1024
NB, NT = 8, 4
SAMP = NB * NT
TOK = PROMPT + SAMP
NC = 3
CH = TOK // NC
HEADS, HD = 8, 64
DA = HEADS * HD
PAST = 2048
FF = 2816
GROUPS = FF // (2 * P)
EPS = 1e-6
LN2, LN3 = float(np.log(2.0)), float(np.log(3.0))
MASKED = -1e30
SLOPE = [2.0 ** -(h + 1) for h in range(HEADS)]

QK_UNITS, V_UNITS, CONV_UNITS, OUT_UNITS, FFN_UNITS = 8, 4, 12, 8, 6 * GROUPS
UNITS = QK_UNITS + V_UNITS + CONV_UNITS + OUT_UNITS + FFN_UNITS
CONV0 = QK_UNITS + V_UNITS
OUT0 = CONV0 + CONV_UNITS
FFN0 = OUT0 + OUT_UNITS
RING = 3
STAGE = 2

QK_JOBS = QK_UNITS * NC
VT = PROMPT // P + 1
V_JOBS = 2 * VT
CONV_JOBS = CONV_UNITS * NC
IN_JOBS = QK_JOBS + V_JOBS + CONV_JOBS


def f32(ap):
    return ap.bitcast(F32)


def build(nc, xT, w, gains, taps, conv_state, state_k, state_v, yT, kT, v_out, conv_tail):
    with ExitStack() as ctx:
        def sb(name, shape, dt=F32):
            return ctx.enter_context(nc.sbuf_tensor(name, shape, dt))

        def sem(name):
            return ctx.enter_context(nc.semaphore(name))

        act_hi = sb("act_hi", [P, KT, TOK], F32R)
        act_lo = sb("act_lo", [P, KT, TOK], F32R)
        pair_hi = sb("pair_hi", [P, 4, TOK], F32R)
        pair_lo = sb("pair_lo", [P, 4, TOK], F32R)
        w_stage = sb("w_stage", [P, STAGE, 1024])
        w_hi = sb("w_hi", [P, RING, 1024], F32R)
        w_lo = sb("w_lo", [P, RING, 1024], F32R)
        resid = sb("resid", [P, KT * TOK])
        res = resid[:, :].rearrange("p (k t) -> p k t", k=KT)
        pt_hi = sb("pt_hi", [P, KT, 256], F32R)
        pt_lo = sb("pt_lo", [P, KT, 256], F32R)
        out32 = sb("out32", [P, 4, CH])
        out_hl = sb("out_hl", [P, 2, 2 * CH], F32R)
        work = sb("work", [P, 4300])
        age_i = sb("age_i", [P, 1024], I16)
        ident = sb("ident", [P, P])
        ones = sb("ones", [P, P])
        g_sb = sb("g_sb", [P, 3, KT])
        taps_sb = sb("taps_sb", [P, 4, 3])
        cst_sb = sb("cst_sb", [P, 4, NB, 2])
        tail_sb = sb("tail_sb", [P, 4, 18])
        neg8slope = sb("neg8slope", [P, 1])
        gate_cell = sb("gate_cell", [P, 2])
        row_max, row_neg, row_sum, row_rec = (sb(n, [P, 2]) for n in ("row_max", "row_neg", "row_sum", "row_rec"))
        q_s = sb("q_s", [P, 4, SAMP])
        k_s = sb("k_s", [P, 4, SAMP])
        v_s = sb("v_s", [SAMP, DA])
        s_cls = sb("s_cls", [P, 6, NB, HEADS])
        s_near = sb("s_near", [P, NT, NB, HEADS])
        s_self = sb("s_self", [SAMP, NT, NB, HEADS])
        age_cls_i, age_near_i = sb("age_cls_i", [P, 6], I32), sb("age_near_i", [P, NT], I32)
        age_self_i = sb("age_self_i", [SAMP, NT, NB], I32)
        age_cls, age_near, age_self = sb("age_cls", [P, 6]), sb("age_near", [P, NT]), sb("age_self", [SAMP, NT * NB])
        cnt_cls, cnt_near, cnt_self = sb("cnt_cls", [P, 6]), sb("cnt_near", [P, NT]), sb("cnt_self", [SAMP, NT * NB])
        cnt_i, cnt_a, cnt_b = sb("cnt_i", [P, 32], I32), sb("cnt_a", [P, 32]), sb("cnt_b", [P, 32])
        top_cls = sb("top_cls", [P, NB * HEADS])
        top_part = sb("top_part", [NB * HEADS, 3, NT])
        top_col = sb("top_col", [NB * HEADS, NT])
        top_diag = sb("top_diag", [NT, NT, NB * HEADS])
        sum_rec = sb("sum_rec", [SAMP, NB])
        head_mask = sb("head_mask", [SAMP, HEADS, HD])
        sel_t = sb("sel_t", [SAMP, NT])

        rstd = work[:, 0:TOK]
        ssum = work[:, TOK:2 * TOK]
        sq = [work[:, 2112:2112 + TOK], work[:, 3168:3168 + TOK]]
        silu = work[:, 2112:2112 + 2 * TOK].rearrange("p (f t) -> p f t", f=2)
        q_rows = work[0:SAMP, 3168:3168 + DA]
        h_c = acc_c = work[:, 0:TOK]
        c_c = y_c = work[:, TOK:2 * TOK]
        b_c = work[:, 2 * TOK:3 * TOK]
        u_c = work[:, 3 * TOK:3 * TOK + 2 + PROMPT + 6 * NB]
        u_s = u_c[:, 2 + PROMPT:].rearrange("p (b t) -> p b t", b=NB)
        p_cls = work[:, 0:1536].rearrange("p (j b t h) -> p j b t h", j=6, b=NB, t=NT)
        p_near = work[:, 1536:1792].rearrange("p (b t h) -> p b t h", b=NB, t=NT)
        p_self = work[0:SAMP, 1792:2048].rearrange("p (b t h) -> p b t h", b=NB, t=NT)
        l_all = work[:, 2048:2304]
        o_b = [work[0:SAMP, 2816:3328], work[0:SAMP, 3328:3840]]
        o_s = work[:, 3840:3968]
        count8 = work[:, 0:1024]
        bias_h = [work[:, 1024:2048], work[:, 2048:3072]]
        age_f = work[:, 3072:4096]
        qc = resid[:, 0:512]
        qn = resid[:, 512:2560]
        k_far = resid[:, 2560:4096]
        k_mid = resid[:, 4096:5632]
        k_near = resid[:, 5632:6144]
        prod = resid[:, 6144:8192]
        v_tiles = [resid[:, 3584 * i:3584 * (i + 1)].rearrange("p (j n) -> p j n", j=7) for i in range(2)]
        prow = [resid[:, 0:1024], resid[:, 1024:2048]]
        o_low = resid[0:HD, 2048:2304]
        o32 = resid[:, 2304:2560]
        stack = [a[:, 4:8, :].rearrange("p k t -> p (k t)") for a in (act_hi, act_lo)]
        st_q = [s[:, 0:1024] for s in stack]
        st_khi = [s[:, 1024:2048] for s in stack]
        st_klo = [s[:, 2048:3072] for s in stack]
        st_v = [s[:, 3072:4096].rearrange("p (k e) -> p k e", k=KT) for s in stack]

        ps = ctx.enter_context(nc.psum_tensor("ps", [P, 8, 512], F32))

        qk_d = nc.dram_tensor("qk_d", [8, P, 2, TOK], F32).ap()
        v_d = nc.dram_tensor("v_d", [HEADS, P, KT, P], F32).ap()
        q_rows_d = nc.dram_tensor("q_rows_d", [SAMP, DA], F32).ap()

        consts_in = sem("consts_in")
        x_in = [sem(f"x_in{k}") for k in range(KT)]
        w_in = [sem(f"w_in{i}") for i in range(STAGE)]
        part_stored = [sem("part_stored0"), sem("part_stored1")]
        rows_stored = [sem("rows_stored0"), sem("rows_stored1")]
        q_rows_out, ld_qc, ld_qn = sem("q_rows_out"), sem("ld_qc"), sem("ld_qn")
        ld_far, ld_mid, ld_near = sem("ld_far"), sem("ld_mid"), sem("ld_near")
        v_ld = [sem("v_ld0"), sem("v_ld1")]
        st_in = [sem("st_in0"), sem("st_in1")]
        x2_in = [sem(f"x2_in{k}") for k in range(KT)]
        y_out = sem("y_out")
        made = sem("made")
        w_split = sem("w_split")
        pool_chain = sem("pool_chain")
        ss_done, ss_all = sem("ss_done"), sem("ss_all")
        job_done = sem("job_done")
        q_turned, self_scores = sem("q_turned"), sem("self_scores")
        new_pe, new_pv, new_turned = sem("new_pe"), sem("new_pv"), sem("new_turned")
        scored, turned, pv_done = sem("scored"), sem("turned"), sem("pv_done")
        sq_done, root, hi_done = sem("sq_done"), sem("root"), sem("hi_done")
        job_copied, q_rows_done = sem("job_copied"), sem("q_rows_done")
        new_exp = sem("new_exp")
        exped, pt_hi_done, low_done, mix_hi = sem("exped"), sem("pt_hi_done"), sem("low_done"), sem("mix_hi")
        h_sq, silu_done, hid_hi = sem("h_sq"), sem("silu_done"), sem("hid_hi")
        dve_chain = sem("dve_chain")
        mean_sq, y_done, lo_done = sem("mean_sq"), sem("y_done"), sem("lo_done")
        part_hi, part_lo, new_kept = sem("part_hi"), sem("part_lo"), sem("new_kept")
        conv_free = sem("conv_free")
        key_used, key_sum = sem("key_used"), sem("key_sum")
        top_ready, shifted, l_ready = sem("top_ready"), sem("shifted"), sem("l_ready")
        ob_done, new_mixed = sem("ob_done"), sem("new_mixed")
        biased, negated, normed = sem("biased"), sem("negated"), sem("normed")
        pt_lo_done, o_sum, mix_lo = sem("pt_lo_done"), sem("o_sum"), sem("mix_lo")
        h_done, h_ss = sem("h_done"), sem("h_ss")
        hidden, hid_lo, added = sem("hidden"), sem("hid_lo"), sem("added")

        block = ctx.enter_context(nc.Block())

        def cols(c):
            return slice(CH * c, CH * (c + 1))

        @block.sync
        def _(sp):
            def unit(u, slot=None):
                if slot is not None or u >= STAGE:
                    sp.wait_ge(w_split, 2 * (u - STAGE) + 2)
                s = u % STAGE if slot is None else slot
                sp.dma_start(w_stage[:, s, :], w[u]).then_inc(w_in[s], 16)

            unit(0)
            sp.dma_start(g_sb[:, :, :], gains).then_inc(consts_in, 16)
            sp.dma_start(taps_sb[:, :, :], taps).then_inc(consts_in, 16)
            sp.dma_start(cst_sb[:, :, :, :], conv_state).then_inc(consts_in, 16)
            for k in range(KT):
                sp.dma_start(res[:, k, :], xT[:, k, :]).then_inc(x_in[k], 16)
            for u in range(1, 4):
                unit(u)

            for n in range(QK_UNITS):
                for c in range(NC):
                    j = NC * n + c
                    sp.wait_ge(part_lo, j + 1)
                    sp.dma_start(qk_d[n, :, :, cols(c)],
                                 f32(out_hl[:, j % 2, :]).rearrange("p (s t) -> p s t", s=2)
                                 ).then_inc(part_stored[j % 2], 16)
                    if n >= 4:
                        sp.dma_start(kT[n - 4, :, cols(c)], out32[:, j % 2, :]).then_inc(rows_stored[j % 2], 16)
                unit(n + 4)

            sp.wait_ge(q_rows_done, 1)
            sp.dma_start(q_rows_d, q_rows).then_inc(q_rows_out, 16)

            for i in range(V_JOBS):
                j, vb, tt = QK_JOBS + i, i // VT, i % VT
                m = P if tt < VT - 1 else SAMP
                sp.wait_ge(part_lo, j + 1)
                if tt < VT - 1:
                    sp.dma_start(v_d[4 * vb:4 * vb + 4, :, tt, :].rearrange("h p e -> p h e"),
                                 f32(out_hl[:, j % 2, 0:512]).rearrange("p (h e) -> p h e", h=4)
                                 ).then_inc(part_stored[j % 2], 16)
                sp.dma_start(v_out[tt * P:tt * P + m, 256 * vb:256 * vb + 256],
                             out32[0:m, j % 2, 0:256]).then_inc(rows_stored[j % 2], 16)
                if i == 6:
                    unit(12)
                if tt == VT - 1:
                    unit(13 + vb)
            unit(15)

            sp.wait_ge(q_rows_out, 16)
            sp.wait_ge(lo_done, NC * KT)
            with sp.Fori(0, 2) as it:
                for pp in range(2):
                    for s in range(2):
                        b = 4 * it + 2 * pp + s
                        unit(6 * it + 16 + 3 * pp + s, (16 + 3 * pp + s) % STAGE)
                        far = state_k[b, 0:1536].rearrange("(i j r) n -> r i j n", i=32, j=3)
                        mid = state_k[b, 1536:1920].rearrange("(i j r) n -> r i j n", i=32, j=3)
                        sp.wait_ge(key_used, 3 * b + 1)
                        for t in range(NT):
                            sp.dma_start(k_far[32 * t:32 * t + 32].rearrange("p (j n) -> p j n", j=3),
                                         far[t]).then_inc(ld_far, 16)
                        sp.wait_ge(key_used, 3 * b + 2)
                        sp.dma_start(qc, q_rows_d.rearrange("(b t) n -> b t n", b=NB)[b].unsqueeze(1)
                                     .broadcast_to([NT, 32, DA])).then_inc(ld_qc, 16)
                        for t in range(NT):
                            sp.dma_start(k_mid[32 * t:32 * t + 32].rearrange("p (j n) -> p j n", j=3),
                                         mid[t]).then_inc(ld_mid, 16)
                        sp.wait_ge(key_used, 3 * b + 3)
                        sp.dma_start(qn, q_rows_d.rearrange("(b t) n -> b (t n)", b=NB)[b].unsqueeze(0)
                                     .broadcast_to([P, NT * DA])).then_inc(ld_qn, 16)
                        sp.dma_start(k_near, state_k[b, 1920:2048]).then_inc(ld_near, 16)
                    unit(6 * it + 18 + 3 * pp, (18 + 3 * pp) % STAGE)
            unit(28)

            sp.wait_ge(key_sum, 3 * NB)
            for b in range(NB):
                vt, ld = v_tiles[b % 2], v_ld[b % 2]
                far = state_v[b, 0:1536].rearrange("(i j r) n -> r i j n", i=32, j=3)
                mid = state_v[b, 1536:1920].rearrange("(i j r) n -> r i j n", i=32, j=3)
                if b >= 2:
                    sp.wait_ge(new_pv, b - 1)
                for t in range(NT):
                    sp.dma_start(vt[32 * t:32 * t + 32, 0:3, :], far[t]).then_inc(ld, 16)
                    sp.dma_start(vt[32 * t:32 * t + 32, 3:6, :], mid[t]).then_inc(ld, 16)
                sp.dma_start(vt[:, 6, :], state_v[b, 1920:2048]).then_inc(ld, 16)

            def load_head(hh, tile):
                r = slice(HD * hh, HD * hh + HD)
                s = st_in[hh]
                for half in range(2):
                    d = slice(HD * half, HD * half + HD)
                    sp.dma_start(f32(st_q[hh][d]), qk_d[tile, r, half, 0:PROMPT]).then_inc(s, 16)
                    sp.dma_start(f32(st_khi[hh][d]), qk_d[4 + tile, r, 0, 0:PROMPT]).then_inc(s, 16)
                    sp.dma_start(f32(st_klo[hh][d]), qk_d[4 + tile, r, 1, 0:PROMPT]).then_inc(s, 16)
                sp.dma_start(f32(st_v[hh]), v_d[2 * tile + hh]).then_inc(s, 16)

            for s in range(2):
                sp.wait_ge(part_stored[s], 16 * PARTS_STORED[s])
            sp.wait_ge(job_done, IN_JOBS)
            load_head(0, 0)
            load_head(1, 0)
            with sp.Fori(0, 3) as it:
                for hh in range(2):
                    sp.wait_ge(pv_done, 8 * it + 4 * hh + 4)
                    load_head(hh, it + 1)

            sp.wait_ge(mix_lo, 4 * HEADS)
            for k in range(KT):
                sp.dma_start(res[:, k, :], xT[:, k, :]).then_inc(x2_in[k], 16)
            for u in range(29, 37):
                unit(u)
            with sp.Fori(0, 10) as it:
                for s in range(6):
                    unit(6 * it + 37 + s, (37 + s) % STAGE)
            unit(97)

            for i in range(NC * KT):
                c, k = divmod(i, KT)
                sp.wait_ge(y_done, 2 * NC * KT + i + 1)
                sp.dma_start(yT[:, k, cols(c)], res[:, k, cols(c)]).then_inc(y_out, 16)
            sp.wait_ge(conv_free, 5)
            sp.dma_start(conv_tail, tail_sb[:, :, :]).then_inc(y_out, 16)
            sp.wait_ge(y_out, 16 * (NC * KT + 1))
            for s in range(2):
                sp.wait_ge(rows_stored[s], 16 * ROWS_STORED[s])

        @block.gpsimd
        def _(pool):
            chain = Chain(pool, pool_chain)
            chain(pool.memset(ident[:, :], 0.0))
            pool.memset(ones[:, :], 1.0).then_inc(made, 1)
            chain(pool.affine_select(out=ident[:, :], in_=ident[:, :], compare_op=ALU.not_equal, fill=1.0,
                                     base=0, pattern=[[-1, P]], channel_multiplier=1))

            def split(u, slot, stage, arrived, released):
                pool.wait_ge(w_in[stage], arrived)
                if released is not None:
                    pool.wait_ge(job_done, released)
                    pool.tensor_tensor(gate_cell[:, 0:1], ones[:, 0:1], ones[:, 0:1], ALU.mult)
                pool.tensor_copy(w_hi[:, slot, :], w_stage[:, stage, :]).then_inc(w_split, 1)
                pool.wait_ge(w_split, 2 * u + 1)
                pool.tensor_tensor(w_lo[:, slot, :], w_stage[:, stage, :], f32(w_hi[:, slot, :]),
                                   ALU.subtract).then_inc(w_split, 1)

            def straight(u):
                split(u, u % RING, u % STAGE, 16 * (u // STAGE + 1), jobs_through(u - RING) if u >= RING else None)

            straight(0)
            chain(pool.iota(age_i[:, :], pattern=[[-1, 1024]], base=896, channel_multiplier=1))
            for t in range(NT):
                q = slice(32 * t, 32 * t + 32)
                chain(pool.iota(age_cls_i[q, 0:3], pattern=[[-16, 3]], base=2048, channel_multiplier=-48))
                chain(pool.iota(age_cls_i[q, 3:6], pattern=[[-4, 3]], base=512, channel_multiplier=-12))
            chain(pool.iota(age_near_i[:, :], pattern=[[1, NT]], base=128, channel_multiplier=-1))
            chain(pool.iota(age_self_i[:, :, :], pattern=[[1, NT], [4, NB]], base=0, channel_multiplier=-1))
            chain(pool.affine_select(out=age_self_i[:, :, :], in_=age_self_i[:, :, :], compare_op=ALU.is_ge,
                                     fill=-1.0, base=0, pattern=[[0, NT], [-4, NB]], channel_multiplier=1))
            chain(pool.affine_select(out=age_self_i[:, :, :], in_=age_self_i[:, :, :], compare_op=ALU.is_ge,
                                     fill=-1.0, base=3, pattern=[[0, NT], [4, NB]], channel_multiplier=-1))
            chain(pool.memset(head_mask[:, :, :], 0.0))
            for t in range(NT):
                chain(pool.affine_select(out=head_mask[:, :, :], in_=head_mask[:, :, :],
                                         compare_op=ALU.not_equal, fill=1.0, base=-8 * t,
                                         pattern=[[-1, HEADS], [0, HD]], channel_multiplier=1))
            chain(pool.memset(sel_t[:, :], 1.0))
            chain(pool.affine_select(out=sel_t[:, :], in_=sel_t[:, :], compare_op=ALU.is_ge, fill=0.0,
                                     base=0, pattern=[[-8, NT]], channel_multiplier=1))
            pool.affine_select(out=sel_t[:, :], in_=sel_t[:, :], compare_op=ALU.is_ge, fill=0.0,
                               base=7, pattern=[[8, NT]], channel_multiplier=-1).then_inc(made, 1)

            for u in range(1, FFN0 + 16):
                straight(u)
            with pool.Fori(0, 4) as it:
                for s in range(12):
                    u = FFN0 + 16 + s
                    split(12 * it + u, u % RING, u % STAGE, 96 * it + 16 * (u // STAGE + 1),
                          72 * it + jobs_through(u - RING))
            straight(96)
            straight(97)

        @block.tensor
        def _(pe):
            def unit_ready(u):
                pe.wait_ge(w_split, 2 * u + 2)

            def three_pass(out, unit_slot, k, wcols, rhs_hi, rhs_lo, first, last):
                hi, lo = w_hi[:, unit_slot, wcols], w_lo[:, unit_slot, wcols]
                pe.matmul(out, hi, rhs_hi, start=first, stop=False)
                pe.matmul(out, hi, rhs_lo, start=False, stop=False)
                return pe.matmul(out, lo, rhs_hi, start=False, stop=last)

            def tile_job(bank, c, slot):
                for k in range(KT):
                    mm = three_pass(ps[:, bank, 0:CH], slot, k, slice(P * k, P * k + P),
                                    act_hi[:, k, cols(c)], act_lo[:, k, cols(c)], k == 0, k == KT - 1)
                mm.then_inc(job_done, 1)

            pe.wait_ge(made, 1)
            for k in range(KT):
                pe.wait_ge(sq_done, k + 1)
                for c in range(NC):
                    mm = pe.matmul(ps[:, c, 0:CH], ones[:, :], sq[k % 2][:, cols(c)], start=(k == 0), stop=(k == KT - 1))
                mm.then_inc(ss_done, 1)
            pe.wait_ge(mean_sq, NC)

            for n in range(QK_UNITS):
                unit_ready(n)
                for c in range(NC):
                    j = NC * n + c
                    if n == 0:
                        pe.wait_ge(lo_done, KT * (c + 1))
                    if j >= 6:
                        pe.wait_ge(job_copied, j - 5)
                    tile_job(3 * (n % 2) + c, c, n % RING)

            pe.wait_ge(new_kept, 8)
            pe.wait_ge(made, 2)
            for n in range(4):
                mm = pe.transpose(ps[0:SAMP, 6, P * n:P * n + P], q_s[:, n, :], ident[:, :])
            mm.then_inc(q_turned, 1)
            for odd in range(2):
                if odd:
                    pe.wait_ge(self_scores, 1)
                r = slice(HD * odd, HD * odd + HD)
                for n in range(4):
                    mm = pe.matmul(ps[0:SAMP, 7, 2 * n + odd:256:HEADS], k_s[r, n, :],
                                   q_s[r, n, :].rearrange("p (b t) -> p t b", b=NB), start=True, stop=True)
                mm.then_inc(self_scores, 1)

            for i in range(V_JOBS):
                j, vb, tt = QK_JOBS + i, i // VT, i % VT
                m = P if tt < VT - 1 else SAMP
                tk = slice(P * tt, P * tt + m)
                if tt == 0:
                    unit_ready(QK_UNITS + 2 * vb + 1)
                pe.wait_ge(job_copied, j - 5)
                for k in range(KT):
                    slot = (QK_UNITS + 2 * vb + k // 4) % RING
                    wc = slice(256 * (k % 4), 256 * (k % 4) + 256)
                    out = ps[0:m, i % 6, 0:256]
                    pe.matmul(out, act_hi[:, k, tk], w_hi[:, slot, wc], start=(k == 0), stop=False)
                    pe.matmul(out, act_hi[:, k, tk], w_lo[:, slot, wc], start=False, stop=False)
                    mm = pe.matmul(out, act_lo[:, k, tk], w_hi[:, slot, wc], start=False, stop=(k == KT - 1))
                mm.then_inc(job_done, 1)

            with pe.Fori(0, 2) as it:
                for pp in range(2):
                    for kind in range(3):
                        n = 3 * pp + kind
                        unit_ready(6 * it + CONV0 + n)
                        for c in range(NC):
                            j = 18 * it + QK_JOBS + V_JOBS + 3 * n + c
                            pe.wait_ge(job_copied, j - (2 if kind == 0 else 5))
                            tile_job(3 * (kind % 2) + c, c, n % RING)

            pe.wait_ge(top_ready, 1)
            pe.transpose(ps[0:64, 0, 0:P], top_cls[:, :], ident[:, :])
            for t in range(NT):
                pe.transpose(ps[0:64, 1, P * t:P * t + P], s_near[:, t].rearrange("p b h -> p (b h)"), ident[:, :])
            for t in range(NT):
                mm = pe.transpose(ps[0:64, 2, SAMP * t:SAMP * t + SAMP],
                                  s_self[:, t].rearrange("p b h -> p (b h)"), ident[0:SAMP, 0:SAMP])
            mm.then_inc(new_pe, 1)
            pe.wait_ge(top_ready, 2)
            pe.transpose(ps[0:NT, 3, 0:64], top_col[:, :], ident[0:64, 0:64]).then_inc(new_pe, 1)
            pe.wait_ge(top_ready, 3)
            pe.matmul(ps[:, 4, 0:256], ones[0:NT, :], top_diag[:, :, :].rearrange("p t x -> p (t x)"),
                      start=True, stop=True).then_inc(new_pe, 1)
            pe.wait_ge(l_ready, 1)
            for b in range(NB):
                mm = pe.matmul(ps[0:SAMP, 5, b:b + 1], l_all[:, 32 * b:32 * b + 32], ones[:, 0:1], start=True, stop=True)
            mm.then_inc(new_pe, 1)

            def to_channels(b):
                pe.wait_ge(ob_done, b + 1)
                for n in range(4):
                    mm = pe.matmul(ps[:, 0, 32 * n + 4 * b:32 * n + 4 * b + 4], o_b[b % 2][:, P * n:P * n + P],
                                   sel_t[:, :], start=True, stop=True)
                mm.then_inc(new_turned, 1)

            for b in range(NB):
                vt = v_tiles[b % 2]
                out = ps[0:SAMP, 6 + b % 2, :]
                pe.wait_ge(v_ld[b % 2], 144 * (b // 2 + 1))
                if b >= 2:
                    pe.wait_ge(ob_done, b - 1)
                for j in range(6):
                    pe.matmul(out, p_cls[:, j, b].rearrange("p t h -> p (t h)"), vt[:, j, :], start=(j == 0), stop=False)
                pe.matmul(out, p_near[:, b].rearrange("p t h -> p (t h)"), vt[:, 6, :], start=False, stop=False)
                pe.matmul(out, p_self[:, b].rearrange("p t h -> p (t h)"), v_s[:, :], start=False,
                          stop=True).then_inc(new_pv, 1)
                if b >= 1:
                    to_channels(b - 1)
            to_channels(NB - 1)
            pe.wait_ge(new_mixed, 1)

            def scores(it, s):
                hh, i = divmod(s, KT)
                if i == 0:
                    pe.wait_ge(st_in[hh], 112 * it + 112)
                if s >= 2:
                    pe.wait_ge(biased, 16 * it + s - 1)
                q = st_q[hh][:, P * i:P * i + P]
                for half, width in score_blocks(i):
                    kc = slice(512 * half, 512 * half + width)
                    out = ps[:, 2 * (s % 2) + half, 0:width]
                    pe.matmul(out, q, st_khi[hh][:, kc], start=True, stop=False)
                    mm = pe.matmul(out, q, st_klo[hh][:, kc], start=False, stop=True)
                mm.then_inc(scored, 1)

            def turn(it, s):
                pe.wait_ge(normed, 16 * it + s + 1)
                for f, (fs, bank, k0, nk) in enumerate(FILLS):
                    if fs != s:
                        continue
                    before = [g for g in range(f) if FILLS[g][1] == bank]
                    if before:
                        pe.wait_ge(pt_lo_done, 24 * it + before[-1] + 1)
                    for k in range(nk):
                        mm = pe.transpose(ps[:, bank, P * k:P * k + P],
                                          prow[s % 2][:, P * (k0 + k):P * (k0 + k) + P], ident[:, :])
                    mm.then_inc(turned, 1)

            def values(it, u):
                hh, i = divmod(2 * u + 1, KT)
                pe.wait_ge(pt_lo_done, 24 * it + fills_through(2 * u + 1))
                if u >= 2:
                    pe.wait_ge(o_sum, 8 * it + u - 1)
                for k in range(i + 1):
                    qs = slice(P, 256) if k == i else slice(0, 256)
                    out = ps[:, 6 + u % 2, qs]
                    pe.matmul(out, st_v[hh][:, k, :], pt_hi[:, k, qs], start=(k == 0), stop=False)
                    mm = pe.matmul(out, st_v[hh][:, k, :], pt_lo[:, k, qs], start=False, stop=(k == i))
                mm.then_inc(pv_done, 1)

            with pe.Fori(0, 4) as it:
                scores(it, 0)
                scores(it, 1)
                for s in range(18):
                    if s + 2 < 16:
                        scores(it, s + 2)
                    if s >= 2 and s % 2 == 1:
                        values(it, (s - 3) // 2)
                    if s < 16:
                        turn(it, s)
                pe.wait_ge(o_sum, 8 * it + 8)

            pe.wait_ge(mix_lo, 4 * HEADS)
            pe.wait_ge(new_mixed, 2)
            pe.wait_ge(conv_free, 5)
            for n in range(OUT_UNITS):
                unit_ready(OUT0 + n)
                for c in range(NC):
                    j = NC * n + c
                    if n >= 2:
                        pe.wait_ge(h_done, j - 5)
                    for k in range(KT):
                        hi, lo = (act_hi, act_lo) if k < 4 else (pair_hi, pair_lo)
                        mm = three_pass(ps[:, 3 * (n % 2) + c, 0:CH], (OUT0 + n) % RING, k, slice(P * k, P * k + P),
                                        hi[:, k % 4, cols(c)], lo[:, k % 4, cols(c)], k == 0, k == KT - 1)
                    mm.then_inc(job_done, 1)

            def sum_of_squares(which):
                for c in range(NC):
                    pe.wait_ge(h_ss, 24 * which + 22 + c)
                    pe.matmul(ps[:, c, 0:CH], ones[:, :], ssum[:, cols(c)], start=True, stop=True).then_inc(ss_all, 1)

            sum_of_squares(0)

            def gate_up(it, g, first=False):
                for n in range(4):
                    u = FFN0 + n if first else FFN0 + 6 * g - 2 + n
                    unit_ready(12 * it + u)
                    for c in range(NC):
                        if first and n == 0:
                            pe.wait_ge(lo_done, NC * KT + KT * (c + 1))
                        if n >= 2:
                            pe.wait_ge(silu_done, 12 * it + 6 * g + 3 * (n - 2) + c + 1)
                        elif not first:
                            pe.wait_ge(hidden, 12 * it + 6 * (g - 1) + 3 * n + c + 1)
                        tile_job(3 * (n % 2) + c, c, u % RING)

            def down(it, g, last=False):
                u0 = UNITS - 2 if last else FFN0 + 6 * (g + 1) + 2
                unit_ready(u0 + 1 if last else 12 * it + u0 + 1)
                pe.wait_ge(hid_lo, 12 * it + 6 * g + 6)
                for n in range(KT):
                    for c in range(NC):
                        i = NC * n + c
                        if i >= 2:
                            if last:
                                pe.wait_ge(h_done, NC * KT + i - 1)
                            else:
                                pe.wait_ge(added, 48 * it + 24 * g + i - 1)
                        for f in range(2):
                            mm = three_pass(ps[:, 6 + i % 2, 0:CH], (u0 + f) % RING, f, slice(P * n, P * n + P),
                                            pair_hi[:, 2 * (g % 2) + f, cols(c)], pair_lo[:, 2 * (g % 2) + f, cols(c)],
                                            f == 0, f == 1)
                        mm.then_inc(job_done, 1)
                if not last:
                    pe.wait_ge(added, 48 * it + 24 * g + 24)

            gate_up(0, 0, first=True)
            with pe.Fori(0, 5) as it:
                for g in (1, 2):
                    gate_up(it, g)
                    down(it, g - 1)
            down(5, 0, last=True)
            sum_of_squares(1)

        @block.scalar
        def _(act):
            def copy(out, in_):
                return act.activation(out, in_, ACT.Copy)

            def roots(which):
                for c in range(NC):
                    act.wait_ge(mean_sq, NC * which + c + 1)
                    act.activation(rstd[:, cols(c)], rstd[:, cols(c)], ACT.Sqrt).then_inc(root, 1)

            def normal_hi(which):
                for i in range(NC * KT):
                    c, k = divmod(i, KT)
                    act.wait_ge(y_done, NC * KT * which + i + 1)
                    copy(act_hi[:, k, cols(c)], out32[:, 2 + i % 2, :]).then_inc(hi_done, 1)

            for k in range(KT):
                act.wait_ge(x_in[k], 16)
                if k >= 2:
                    act.wait_ge(ss_done, k - 1)
                act.activation(sq[k % 2], res[:, k, :], ACT.Square).then_inc(sq_done, 1)
            roots(0)
            normal_hi(0)

            for j in range(QK_JOBS + V_JOBS):
                act.wait_ge(job_done, j + 1)
                if j >= 2:
                    act.wait_ge(part_lo, j - 1)
                if rows_before(j):
                    act.wait_ge(rows_stored[j % 2], 16 * rows_before(j))
                if j < QK_JOBS:
                    n, c = divmod(j, NC)
                    copy(out32[:, j % 2, :], ps[:, 3 * (n % 2) + c, 0:CH]).then_inc(job_copied, 1)
                else:
                    i = j - QK_JOBS
                    m = P if i % VT < VT - 1 else SAMP
                    copy(out32[0:m, j % 2, 0:256], ps[0:m, i % 6, 0:256]).then_inc(job_copied, 1)
                if j == QK_JOBS:
                    act.wait_ge(q_turned, 1)
                    copy(q_rows, ps[0:SAMP, 6, :]).then_inc(q_rows_done, 1)

            act.wait_ge(conv_free, 1)
            with act.Fori(0, 2) as it:
                for pp in range(2):
                    act.wait_ge(conv_free, 2 * it + pp + 1)
                    for kind in range(3):
                        for c in range(NC):
                            act.wait_ge(job_done, 18 * it + QK_JOBS + V_JOBS + 9 * pp + 3 * kind + c + 1)
                            copy((h_c, c_c, b_c)[kind][:, cols(c)],
                                 ps[:, 3 * (kind % 2) + c, 0:CH]).then_inc(job_copied, 1)

            act.wait_ge(shifted, 1)
            act.activation(p_near[:, :, :, :].rearrange("p b t h -> p t b h"), s_near[:, :, :, :],
                           ACT.Exp).then_inc(new_exp, 1)
            act.activation(p_self[:, :, :, :].rearrange("p b t h -> p t b h"), s_self[:, :, :, :],
                           ACT.Exp).then_inc(new_exp, 1)
            for t in range(NT):
                q = slice(32 * t, 32 * t + 32)
                act.activation(p_cls[q, :, :, t, :], s_cls[q, :, :, :], ACT.Exp).then_inc(new_exp, 1)

            with act.Fori(0, 4) as it:
                for s in range(20):
                    if s < 16:
                        act.wait_ge(negated, 16 * it + s + 1)
                        n = P * (s % KT + 1)
                        act.activation(prow[s % 2][:, 0:n], prow[s % 2][:, 0:n], ACT.Exp,
                                       bias=row_neg[:, s % 2:s % 2 + 1],
                                       accum_out=row_sum[:, s % 2:s % 2 + 1]).then_inc(exped, 1)
                    for f, (fs, bank, k0, nk) in enumerate(FILLS):
                        if fs != s - 1:
                            continue
                        act.wait_ge(turned, 24 * it + f + 1)
                        if fs >= 2:
                            act.wait_ge(pv_done, 8 * it + fs // 2)
                        copy(pt_hi[:, k0:k0 + nk, P * (fs % 2):P * (fs % 2) + P],
                             ps[:, bank, 0:P * nk].rearrange("p (k t) -> p k t", k=nk)).then_inc(pt_hi_done, 1)
                    if s >= 3 and s % 2 == 1 and (s - 3) // 2 < 8:
                        u = (s - 3) // 2
                        hh = u // 4
                        r = slice(HD * hh, HD * hh + HD)
                        act.wait_ge(pv_done, 8 * it + u + 1)
                        copy(o_low, ps[HD:P, 6 + u % 2, 0:256]).then_inc(low_done, 1)
                        act.wait_ge(o_sum, 8 * it + u + 1)
                        copy(act_hi[r, it, 256 * (u % 4):256 * (u % 4) + 256], o32[r]).then_inc(mix_hi, 1)

            def squares(which):
                for j in range(NC * KT):
                    n, c = divmod(j, NC)
                    act.wait_ge(h_done, NC * KT * which + j + 1)
                    if j >= 6:
                        act.wait_ge(h_ss, NC * KT * which + j - 5)
                    act.activation(sq[n % 2][:, cols(c)], res[:, n, cols(c)], ACT.Square).then_inc(h_sq, 1)

            squares(0)
            roots(1)
            normal_hi(1)

            def gates(it, g, first=False):
                job = OUT_JOB0 + 24 if first else 72 * it + FFN_JOB0 + 36 * g
                for i in range(6):
                    f, c = divmod(i, NC)
                    act.wait_ge(job_done, job + i + 1)
                    if not first:
                        act.wait_ge(hid_lo, 12 * it + 6 * (g - 1) + i + 1)
                    act.activation(silu[:, f, cols(c)], ps[:, 3 * f + c, 0:CH], ACT.Silu).then_inc(silu_done, 1)
                for i in range(6):
                    f, c = divmod(i, NC)
                    act.wait_ge(hidden, 12 * it + 6 * g + i + 1)
                    if not first:
                        act.wait_ge(job_done, job)
                    copy(pair_hi[:, 2 * (g % 2) + f, cols(c)], silu[:, f, cols(c)]).then_inc(hid_hi, 1)

            gates(0, 0, first=True)
            with act.Fori(0, 5) as it:
                for g in (1, 2):
                    gates(it, g)
            squares(1)
            roots(2)

        @block.vector
        def _(dve):
            chain = Chain(dve, dve_chain)

            def count_log(out, age, age_i, n_i, a, b, scale):
                chain(dve.tensor_copy(age, age_i))
                chain(dve.tensor_scalar(n_i, age_i, 3, None, ALU.bitwise_and))
                chain(dve.tensor_scalar(b, n_i, 0.0, None, ALU.is_equal))
                chain(dve.scalar_tensor_tensor(a, age, 512.0, b, ALU.is_le, ALU.mult))
                chain(dve.scalar_tensor_tensor(a, age, 128.0, a, ALU.is_le, ALU.add))
                chain(dve.tensor_scalar(n_i, age_i, 15, None, ALU.bitwise_and))
                chain(dve.tensor_scalar(b, n_i, 0.0, None, ALU.is_equal))
                chain(dve.scalar_tensor_tensor(b, age, 2048.0, b, ALU.is_le, ALU.mult))
                chain(dve.tensor_tensor(a, a, b, ALU.add))
                chain(dve.scalar_tensor_tensor(a, age, 0.0, a, ALU.is_ge, ALU.mult))
                chain(dve.tensor_scalar(b, a, 0.0, MASKED * scale, ALU.is_equal, ALU.mult))
                chain(dve.tensor_scalar(out, a, 2.0, LN2 * scale, ALU.is_equal, ALU.mult))
                chain(dve.tensor_tensor(out, out, b, ALU.add))
                chain(dve.tensor_scalar(b, a, 3.0, LN3 * scale, ALU.is_equal, ALU.mult))
                chain(dve.tensor_tensor(out, out, b, ALU.add))

            def norm(which):
                for c in range(NC):
                    if which == 0:
                        dve.wait_ge(ss_done, KT)
                    else:
                        dve.wait_ge(ss_all, NC * (which - 1) + c + 1)
                    dve.tensor_scalar(rstd[:, cols(c)], ps[:, c, 0:CH], 1.0 / D, EPS,
                                      ALU.mult, ALU.add).then_inc(mean_sq, 1)
                for c in range(NC):
                    dve.wait_ge(root, NC * which + c + 1)
                    chain(dve.reciprocal(rstd[:, cols(c)], rstd[:, cols(c)]))

                def low(i):
                    c, k = divmod(i, KT)
                    dve.wait_ge(hi_done, NC * KT * which + i + 1)
                    dve.tensor_tensor(act_lo[:, k, cols(c)], out32[:, 2 + i % 2, :], f32(act_hi[:, k, cols(c)]),
                                      ALU.subtract).then_inc(lo_done, 1)

                for i in range(NC * KT):
                    c, k = divmod(i, KT)
                    dst = res[:, k, cols(c)] if which == 2 else out32[:, 2 + i % 2, :]
                    if which < 2 and i >= 2:
                        dve.wait_ge(lo_done, NC * KT * which + i - 1)
                    dve.scalar_tensor_tensor(dst, res[:, k, cols(c)], g_sb[:, which, k:k + 1], rstd[:, cols(c)],
                                             ALU.mult, ALU.mult).then_inc(y_done, 1)
                    if which < 2 and i >= 1:
                        low(i - 1)
                if which < 2:
                    low(NC * KT - 1)

            dve.wait_ge(consts_in, 48)
            norm(0)
            dve.memset(neg8slope[:, :], -8.0 * SLOPE[0]).then_inc(key_used, 3)

            def low_part(j, hi, lo, src, wait):
                dve.wait_ge(part_hi, wait)
                dve.tensor_tensor(lo, src, f32(hi), ALU.subtract).then_inc(part_lo, 1)

            his = 0
            for j in range(QK_JOBS + V_JOBS):
                dve.wait_ge(job_copied, j + 1)
                src, hl = out32[:, j % 2, :], out_hl[:, j % 2, :]
                if j < QK_JOBS:
                    n, c = divmod(j, NC)
                    if c == NC - 1:
                        keep, scale = (q_s, HD ** -0.5) if n < 4 else (k_s, 1.0)
                        dve.tensor_scalar(keep[:, n % 4, :], src[:, CH - SAMP:CH], scale, None,
                                          ALU.mult).then_inc(new_kept, 1)
                    hi, lo = hl[:, 0:CH], hl[:, CH:2 * CH]
                else:
                    vb, tt = divmod(j - QK_JOBS, VT)
                    if tt == VT - 1:
                        dve.tensor_copy(v_s[:, 256 * vb:256 * vb + 256], src[0:SAMP, 0:256]).then_inc(part_lo, 1)
                        continue
                    src = src[:, 0:256].rearrange("p (h d) -> p h d", h=4)
                    parts = hl[:, 0:512].rearrange("p (h s d) -> p h s d", h=4, s=2)
                    hi, lo = parts[:, :, 0, :], parts[:, :, 1, :]
                if parts_before(j):
                    dve.wait_ge(part_stored[j % 2], 16 * parts_before(j))
                dve.tensor_copy(hi, src).then_inc(part_hi, 1)
                his += 1
                low_part(j, hi, lo, src, his)

            dve.wait_ge(made, 2)
            count_log(cnt_cls[:, :], age_cls[:, :], age_cls_i[:, :], cnt_i[:, 0:6], cnt_a[:, 0:6], cnt_b[:, 0:6], 1.0)
            count_log(cnt_near[:, :], age_near[:, :], age_near_i[:, :], cnt_i[:, 0:4], cnt_a[:, 0:4], cnt_b[:, 0:4], 1.0)
            count_log(cnt_self[:, :], age_self[:, :], age_self_i[:, :, :].rearrange("p t b -> p (t b)"),
                      cnt_i[0:SAMP, :], cnt_a[0:SAMP, :], cnt_b[0:SAMP, :], 1.0)
            dve.wait_ge(q_rows_out, 16)
            dve.memset(u_c[:, 0:2], 0.0).then_inc(conv_free, 1)

            def keys(b, which):
                if which < 2:
                    k_blk, ld = ((k_far, ld_far), (k_mid, ld_mid))[which]
                    dve.wait_ge(ld, 64 * b + 64)
                    dve.wait_ge(ld_qc, 16 * b + 16)
                    pr = prod[:, 0:1536].rearrange("p (j n) -> p j n", j=3)
                    kv = k_blk.rearrange("p (j n) -> p j n", j=3)
                    qv = qc.unsqueeze(1).broadcast_to([P, 3, DA])
                    dst, nj = s_cls[:, 3 * which:3 * which + 3, b, :], 3
                else:
                    dve.wait_ge(ld_near, 16 * b + 16)
                    dve.wait_ge(ld_qn, 16 * b + 16)
                    pr = prod.rearrange("p (j n) -> p j n", j=NT)
                    kv = k_near.unsqueeze(1).broadcast_to([P, NT, DA])
                    qv = qn.rearrange("p (j n) -> p j n", j=NT)
                    dst, nj = s_near[:, :, b, :], NT
                dve.wait_ge(key_used, 3 * b + which + 3)
                if which > 0:
                    dve.wait_ge(key_sum, 3 * b + which)
                dve.tensor_tensor(pr, kv, qv, ALU.mult).then_inc(key_used, 1)
                dve.wait_ge(key_used, 3 * b + which + 4)
                dve.tensor_reduce(dst, prod[:, 0:nj * DA].rearrange("p (j h d) -> p j h d", j=nj, h=HEADS),
                                  AX.X, ALU.add).then_inc(key_sum, 1)

            with dve.Fori(0, 2) as it:
                start = chain.loop(it, CONV_CHAIN, 2)
                for pp in range(2):
                    p = 2 * it + pp
                    b = 4 * it + 2 * pp
                    keys(b, 0)
                    keys(b, 1)
                    keys(b, 2)
                    dve.wait_ge(job_copied, 18 * it + QK_JOBS + V_JOBS + 9 * pp + 6)
                    chain(dve.tensor_tensor(u_c[:, 2:2 + PROMPT], c_c[:, 0:PROMPT], h_c[:, 0:PROMPT], ALU.mult))
                    chain(dve.tensor_tensor(u_s[:, :, 2:6], c_c[:, PROMPT:].rearrange("p (b t) -> p b t", b=NB),
                                            h_c[:, PROMPT:].rearrange("p (b t) -> p b t", b=NB), ALU.mult))
                    chain(dve.tensor_copy(u_s[:, :, 0:2], cst_sb[:, p, :, :]))
                    acc_s = acc_c[:, PROMPT:].rearrange("p (b t) -> p b t", b=NB)
                    for k in range(3):
                        w_k = taps_sb[:, p, k:k + 1]
                        for acc, u in ((acc_c[:, 0:PROMPT], u_c[:, k:k + PROMPT]), (acc_s, u_s[:, :, k:k + NT])):
                            if k == 0:
                                chain(dve.tensor_scalar(acc, u, w_k, None, ALU.mult))
                            else:
                                chain(dve.scalar_tensor_tensor(acc, u, w_k, acc, ALU.mult, ALU.add))
                    chain(dve.tensor_copy(tail_sb[:, p, 0:2], u_c[:, PROMPT:PROMPT + 2]))
                    chain(dve.tensor_copy(tail_sb[:, p, 2:18].rearrange("p (b t) -> p b t", b=NB), u_s[:, :, 4:6]))
                    for which in range(3):
                        keys(b + 1, which)
                    dve.wait_ge(job_copied, 18 * it + QK_JOBS + V_JOBS + 9 * pp + 9)
                    chain(dve.tensor_tensor(y_c, acc_c, b_c, ALU.mult))
                    chain(dve.tensor_copy(pair_hi[:, p, :], y_c))
                    dve.tensor_tensor(pair_lo[:, p, :], y_c, f32(pair_hi[:, p, :]), ALU.subtract).then_inc(conv_free, 1)
                chain.end(start)
            dve.wait_ge(conv_free, 5)

            chain(dve.memset(work[:, 0:1536], 0.0))
            dve.wait_ge(self_scores, 2)
            dve.wait_ge(key_sum, 3 * NB)
            chain(dve.tensor_copy(s_self[:, :, :, :].rearrange("p t b h -> p (t b h)"), ps[0:SAMP, 7, 0:256]))
            for s, age, cnt, n in ((s_cls, age_cls, cnt_cls, P), (s_near, age_near, cnt_near, P),
                                   (s_self, age_self, cnt_self, SAMP)):
                a3 = age[:, :].unsqueeze(2) if s is not s_self else age[:, :].rearrange("p (t b) -> p t b", t=NT)
                c3 = cnt[:, :].unsqueeze(2) if s is not s_self else cnt[:, :].rearrange("p (t b) -> p t b", t=NT)
                for h in range(HEADS):
                    view = s[:, :, :, h]
                    shape = list(view.shape)
                    chain(dve.scalar_tensor_tensor(view, a3.broadcast_to(shape), -SLOPE[h], view, ALU.mult, ALU.add))
                full = s[:, :, :, :]
                chain(dve.tensor_tensor(full, full, c3.unsqueeze(3).broadcast_to(list(full.shape)), ALU.add))
            dve.tensor_reduce(top_cls[:, :], s_cls[:, :, :, :].rearrange("p j b h -> p (b h) j"), AX.X,
                              ALU.max).then_inc(top_ready, 1)
            dve.wait_ge(new_pe, 1)
            for k, (bank, n) in enumerate(((0, 32), (1, P), (2, SAMP))):
                chain(dve.tensor_reduce(top_part[:, k, :], ps[0:64, bank, 0:NT * n].rearrange("p (t n) -> p t n", t=NT),
                                        AX.X, ALU.max))
            chain(dve.tensor_tensor(top_col[:, :], top_part[:, 0, :], top_part[:, 1, :], ALU.max))
            dve.tensor_tensor(top_col[:, :], top_col[:, :], top_part[:, 2, :], ALU.max).then_inc(top_ready, 1)
            dve.wait_ge(new_pe, 2)
            dve.tensor_tensor(top_diag[:, :, :], ps[0:NT, 3, 0:64].unsqueeze(1).broadcast_to([NT, NT, 64]),
                              ident[0:NT, 0:NT].unsqueeze(2).broadcast_to([NT, NT, 64]), ALU.mult).then_inc(top_ready, 1)
            dve.wait_ge(new_pe, 3)
            near = s_near[:, :, :, :].rearrange("p t b h -> p (t b h)")
            own = s_self[:, :, :, :].rearrange("p t b h -> p (t b h)")
            chain(dve.tensor_tensor(near, near, ps[:, 4, 0:256], ALU.subtract))
            chain(dve.tensor_tensor(own, own, ps[0:SAMP, 4, 0:256], ALU.subtract))
            for t in range(NT):
                q = slice(32 * t, 32 * t + 32)
                v = s_cls[q, :, :, :].rearrange("p j b h -> p j (b h)")
                ins = dve.tensor_tensor(v, v, ps[q, 4, 64 * t:64 * t + 64].unsqueeze(1).broadcast_to([32, 6, 64]),
                                        ALU.subtract)
                if t < NT - 1:
                    chain(ins)
            ins.then_inc(shifted, 1)
            dve.wait_ge(new_exp, 6)
            chain(dve.tensor_reduce(l_all, work[:, 0:1536].rearrange("p (j x) -> p x j", j=6), AX.X, ALU.add))
            chain(dve.tensor_tensor(l_all, l_all, work[:, 1536:1792], ALU.add))
            dve.tensor_tensor(l_all[0:SAMP], l_all[0:SAMP], work[0:SAMP, 1792:2048], ALU.add).then_inc(l_ready, 1)
            dve.wait_ge(new_pe, 4)
            chain(dve.reciprocal(sum_rec[:, :], ps[0:SAMP, 5, 0:NB]))
            for b in range(NB):
                dve.wait_ge(new_pv, b + 1)
                if b >= 2:
                    dve.wait_ge(new_turned, b - 1)
                dve.scalar_tensor_tensor(o_b[b % 2], ps[0:SAMP, 6 + b % 2, :], sum_rec[:, b:b + 1],
                                         head_mask[:, :, :].rearrange("p h d -> p (h d)"), ALU.mult,
                                         ALU.mult).then_inc(ob_done, 1)
            dve.wait_ge(new_turned, NB)
            dve.tensor_copy(o_s, ps[:, 0, 0:P]).then_inc(new_mixed, 1)
            dve.wait_ge(new_mixed, 1)
            o4 = o_s.rearrange("p (n t) -> p n t", n=4)
            chain(dve.tensor_copy(act_hi[:, 0:4, PROMPT:TOK], o4))
            dve.tensor_tensor(act_lo[:, 0:4, PROMPT:TOK], o4, f32(act_hi[:, 0:4, PROMPT:TOK]),
                              ALU.subtract).then_inc(new_mixed, 1)

            dve.wait_ge(new_mixed, 2)
            count_log(count8, age_f, age_i[:, :], bias_h[1].bitcast(I16)[:, 0:1024], bias_h[0], prow[0], 8.0)

            with dve.Fori(0, 4) as it:
                start = chain.loop(it, HEAD_CHAIN, 4)
                for s in range(20):
                    hh, i = divmod(s, KT)
                    if s < 16:
                        n = P * (i + 1)
                        if i == 0:
                            chain(dve.scalar_tensor_tensor(bias_h[hh], age_f, neg8slope[:, 0:1], count8,
                                                           ALU.mult, ALU.add))
                            chain(dve.tensor_scalar(neg8slope[:, :], neg8slope[:, :], 0.5, None, ALU.mult))
                        dve.wait_ge(scored, 16 * it + s + 1)
                        if s >= 2:
                            dve.wait_ge(turned, 24 * it + fills_through(s - 2))
                        dve.memset(gate_cell[:, 1:2], 0.0)
                        dve.tensor_tensor_reduce(
                            prow[s % 2][:, 0:n],
                            ps[:, 2 * (s % 2):2 * (s % 2) + 2, :].rearrange("p a b -> p (a b)")[:, 0:n],
                            bias_h[hh][:, 896 - P * i:1024], HD ** -0.5, -3e38, ALU.add, ALU.max,
                            row_max[:, s % 2:s % 2 + 1]).then_inc(biased, 1)
                        dve.wait_ge(biased, 16 * it + s + 1)
                        dve.tensor_scalar(row_neg[:, s % 2:s % 2 + 1], row_max[:, s % 2:s % 2 + 1], -1.0, None,
                                          ALU.mult).then_inc(negated, 1)
                    if 1 <= s < 17:
                        z, n = (s - 1) % 2, P * ((s - 1) % KT + 1)
                        dve.wait_ge(exped, 16 * it + s)
                        chain(dve.reciprocal(row_rec[:, z:z + 1], row_sum[:, z:z + 1]))
                        dve.tensor_scalar(prow[z][:, 0:n], prow[z][:, 0:n], row_rec[:, z:z + 1], None,
                                          ALU.mult).then_inc(normed, 1)
                    for f, (fs, bank, k0, nk) in enumerate(FILLS):
                        if fs != s - 2:
                            continue
                        dve.wait_ge(pt_hi_done, 24 * it + f + 1)
                        qs = slice(P * (fs % 2), P * (fs % 2) + P)
                        dve.tensor_tensor(pt_lo[:, k0:k0 + nk, qs],
                                          ps[:, bank, 0:P * nk].rearrange("p (k t) -> p k t", k=nk),
                                          f32(pt_hi[:, k0:k0 + nk, qs]), ALU.subtract).then_inc(pt_lo_done, 1)
                    if s >= 4 and s % 2 == 0 and (s - 4) // 2 < 8:
                        u = (s - 4) // 2
                        r = slice(HD * (u // 4), HD * (u // 4) + HD)
                        dve.wait_ge(low_done, 8 * it + u + 1)
                        dve.tensor_tensor(o32[r], ps[0:HD, 6 + u % 2, 0:256], o_low, ALU.add).then_inc(o_sum, 1)
                        dve.wait_ge(mix_hi, 8 * it + u + 1)
                        qs = slice(256 * (u % 4), 256 * (u % 4) + 256)
                        dve.tensor_tensor(act_lo[r, it, qs], o32[r], f32(act_hi[r, it, qs]),
                                          ALU.subtract).then_inc(mix_lo, 1)
                chain.end(start)

            def stream(which, job0):
                def add_squares(j):
                    n, c = divmod(j, NC)
                    dve.wait_ge(h_sq, NC * KT * which + j + 1)
                    if n == 0:
                        dve.tensor_copy(ssum[:, cols(c)], sq[n % 2][:, cols(c)]).then_inc(h_ss, 1)
                    else:
                        dve.wait_ge(h_ss, NC * KT * which + j - 2)
                        dve.tensor_tensor(ssum[:, cols(c)], ssum[:, cols(c)], sq[n % 2][:, cols(c)],
                                          ALU.add).then_inc(h_ss, 1)

                for j in range(NC * KT):
                    n, c = divmod(j, NC)
                    dve.wait_ge(job_done, job0 + j + 1)
                    if which == 0:
                        dve.wait_ge(x2_in[n], 16)
                        bank = 3 * (n % 2) + c
                    else:
                        bank = 6 + j % 2
                    dve.tensor_tensor(res[:, n, cols(c)], ps[:, bank, 0:CH], res[:, n, cols(c)],
                                      ALU.add).then_inc(h_done, 1)
                    if j >= 1:
                        add_squares(j - 1)
                add_squares(NC * KT - 1)

            stream(0, OUT_JOB0)
            norm(1)

            def hidden_of(it, g, first=False):
                job = OUT_JOB0 + 24 + 6 if first else 72 * it + FFN_JOB0 + 36 * g + 6

                def low(i):
                    f, c = divmod(i, NC)
                    dve.wait_ge(hid_hi, 12 * it + 6 * g + i + 1)
                    dve.tensor_tensor(pair_lo[:, 2 * (g % 2) + f, cols(c)], silu[:, f, cols(c)],
                                      f32(pair_hi[:, 2 * (g % 2) + f, cols(c)]), ALU.subtract).then_inc(hid_lo, 1)

                for i in range(6):
                    f, c = divmod(i, NC)
                    dve.wait_ge(job_done, job + i + 1)
                    dve.wait_ge(silu_done, 12 * it + 6 * g + i + 1)
                    dve.tensor_tensor(silu[:, f, cols(c)], ps[:, 3 * f + c, 0:CH], silu[:, f, cols(c)],
                                      ALU.mult).then_inc(hidden, 1)
                    if i >= 1:
                        low(i - 1)
                low(5)

            hidden_of(0, 0, first=True)
            with dve.Fori(0, 5) as it:
                for g in (1, 2):
                    hidden_of(it, g)
                    for i in range(NC * KT):
                        n, c = divmod(i, NC)
                        dve.wait_ge(job_done, 72 * it + FFN_JOB0 + 36 * g + 12 + i + 1)
                        dve.tensor_tensor(res[:, n, cols(c)], ps[:, 6 + i % 2, 0:CH], res[:, n, cols(c)],
                                          ALU.add).then_inc(added, 1)
            stream(1, LAST_JOB0)
            norm(2)


class Chain:

    def __init__(self, eng, sem):
        self.eng, self.sem, self.base, self.n = eng, sem, 0, 0

    def __call__(self, ins):
        ins.then_inc(self.sem, 1)
        self.n += 1
        self.eng.wait_ge(self.sem, self.base + self.n)

    def loop(self, it, per, turns):
        self.base, self.per, self.turns = it * per, per, turns
        return self.n

    def end(self, start):
        assert self.n - start == self.per, (self.n - start, self.per)
        self.base, self.n = 0, start + self.per * self.turns


CONV_CHAIN = 2 * 13
HEAD_CHAIN = 2 * 2 + 16
OUT_JOB0 = IN_JOBS
FFN_JOB0 = OUT_JOB0 + 24 + 12 - 36
LAST_JOB0 = OUT_JOB0 + 24 + 12 + 36 * (GROUPS - 1)


def jobs_through(u):
    if u < QK_UNITS:
        return NC * (u + 1)
    if u < CONV0:
        return QK_JOBS + VT * ((u - QK_UNITS) // 2 + 1)
    if u < OUT0:
        return QK_JOBS + V_JOBS + NC * (u - CONV0 + 1)
    if u < FFN0 + 4:
        return IN_JOBS + NC * (u - OUT0 + 1)
    g, s = divmod(u - FFN0 - 4, 6)
    base = OUT_JOB0 + 24 + 12 + 36 * g
    return base + (NC * (s + 1) if s < 4 else 36)


def parts_before(j):
    return sum(1 for i in range(j % 2, j, 2) if not (i >= QK_JOBS and (i - QK_JOBS) % VT == VT - 1))


def rows_before(j):
    return sum(1 for i in range(j % 2, j, 2) if i >= QK_JOBS // 2)


PARTS_STORED = [parts_before(QK_JOBS + V_JOBS), parts_before(QK_JOBS + V_JOBS + 1)]
ROWS_STORED = [rows_before(QK_JOBS + V_JOBS), rows_before(QK_JOBS + V_JOBS + 1)]


def fills():
    out = []
    for s in range(2 * KT):
        i = s % KT
        if i < 4:
            out.append((s, 4 + i % 2, 0, i + 1))
        else:
            out += [(s, 4, 0, 4), (s, 5, 4, i - 3)]
    return out


FILLS = fills()


def fills_through(s):
    return sum(1 for f in FILLS if f[0] <= s)


def score_blocks(i):
    n = P * (i + 1)
    return [(0, max(256, n))] if n <= 512 else [(0, 512), (1, max(256, n - 512))]


def weight_units(w_in, w_out, w_gate, w_up, w_down):
    def tile(w, c):
        return w[:, c:c + P].reshape(KT, P, P).transpose(1, 0, 2).reshape(P, 1024)

    def wide(w, c, half):
        return w[512 * half:512 * half + 512, c:c + 256].reshape(4, P, 256).transpose(1, 0, 2).reshape(P, 1024)

    def gates(g):
        return [tile(w_gate, 256 * g), tile(w_gate, 256 * g + P), tile(w_up, 256 * g), tile(w_up, 256 * g + P)]

    def downs(g):
        return [w_down[256 * g + P * f:256 * g + P * f + P, :] for f in range(2)]

    units = [tile(w_in, P * n) for n in range(8)]
    units += [wide(w_in, 2 * DA + 256 * vb, half) for vb in range(2) for half in range(2)]
    for p in range(4):
        units += [tile(w_in, 3 * DA + off + P * p) for off in (0, 2 * (D - DA), D - DA)]
    units += [tile(w_out, P * n) for n in range(KT)]
    units += gates(0)
    for g in range(1, GROUPS):
        units += gates(g) + downs(g - 1)
    units += downs(GROUPS - 1)
    return np.ascontiguousarray(np.stack(units))


def kernel(x_prompt, x_sample, state_attn_k, state_attn_v, state_conv, norm_mix_g, w_in, w_conv, w_out,
           norm_ffn_g, w_gate, w_up, w_down, norm_final_g):
    import concourse.bacc as bacc
    from concourse.bass_utils import run_bass_kernel_spmd

    a = np.ascontiguousarray
    x = np.concatenate([np.asarray(x_prompt)[0], np.asarray(x_sample).reshape(SAMP, D)])
    by_channel = lambda v: np.asarray(v).reshape(KT, P).T
    arrays = {
        "xT": a(x.T.reshape(KT, P, TOK).transpose(1, 0, 2)),
        "w": weight_units(*(np.asarray(m)[0] for m in (w_in, w_out, w_gate, w_up, w_down))),
        "gains": a(np.stack([by_channel(np.asarray(norm_mix_g)[0]), by_channel(np.asarray(norm_ffn_g)[0]),
                             by_channel(norm_final_g)], axis=1)),
        "taps": a(np.asarray(w_conv)[0].reshape(3, 4, P).transpose(2, 1, 0)),
        "conv_state": a(np.asarray(state_conv)[0].reshape(NB, 2, 4, P).transpose(3, 2, 0, 1)),
        "state_k": a(np.asarray(state_attn_k)[0].reshape(NB, PAST, DA)),
        "state_v": a(np.asarray(state_attn_v)[0].reshape(NB, PAST, DA)),
    }
    outs = {"yT": (P, KT, TOK), "kT": (4, P, TOK), "v": (TOK, DA), "conv_tail": (P, 4, 18)}
    nc = bacc.Bacc("TRN2", target_bir_lowering=False, num_devices=1, dynamic_dma_scratch_size=1024)
    args = [nc.dram_tensor(f"in_{n}", v.shape, F32, kind="ExternalInput").ap() for n, v in arrays.items()]
    args += [nc.dram_tensor(f"out_{n}", s, F32, kind="ExternalOutput").ap() for n, s in outs.items()]
    build(nc, *args)
    got = run_bass_kernel_spmd(nc, [{f"in_{n}": v for n, v in arrays.items()}], core_ids=[0]).results[0]
    y, k, v, tail = (np.asarray(got[f"out_{n}"]) for n in outs)

    y = y.transpose(2, 1, 0).reshape(TOK, D)
    k = k.transpose(2, 0, 1).reshape(TOK, HEADS, HD)
    v = v.reshape(TOK, HEADS, HD)
    tail = tail.transpose(2, 1, 0).reshape(18, D - DA)
    return (a(y[:PROMPT])[None], a(y[PROMPT:]).reshape(NB, NT, D),
            a(k[:PROMPT])[None, None], a(v[:PROMPT])[None, None], a(tail[:2])[None, None],
            a(k[PROMPT:]).reshape(1, NB, NT, HEADS, HD), a(v[PROMPT:]).reshape(1, NB, NT, HEADS, HD),
            a(tail[2:]).reshape(1, NB, 2, D - DA))
```

```python
from contextlib import ExitStack

import numpy as np

import concourse.bass as bass
from concourse import mybir

F32 = mybir.dt.float32
F32R = mybir.dt.float32r
I32 = mybir.dt.int32
I16 = mybir.dt.int16
ALU = mybir.AluOpType
ACT = mybir.ActivationFunctionType
AX = mybir.AxisListType

P = 128
D = 1024
KT = D // P
PROMPT = 1024
NB, NT = 8, 4
SAMP = NB * NT
TOK = PROMPT + SAMP
NC = 3
CH = TOK // NC
HEADS, HD = 8, 64
DA = HEADS * HD
PAST = 2048
FF = 2816
GROUPS = FF // (2 * P)
EPS = 1e-6
LN2, LN3 = float(np.log(2.0)), float(np.log(3.0))
MASKED = -1e30
SLOPE = [2.0 ** -(h + 1) for h in range(HEADS)]

QK_UNITS, V_UNITS, CONV_UNITS, OUT_UNITS, FFN_UNITS = 8, 4, 12, 8, 6 * GROUPS
UNITS = QK_UNITS + V_UNITS + CONV_UNITS + OUT_UNITS + FFN_UNITS
CONV0 = QK_UNITS + V_UNITS
OUT0 = CONV0 + CONV_UNITS
FFN0 = OUT0 + OUT_UNITS
RING = 3
STAGE = 2
PROWS = 4

QK_JOBS = QK_UNITS * NC
VT = PROMPT // P + 1
V_JOBS = 2 * VT
CONV_JOBS = CONV_UNITS * NC
IN_JOBS = QK_JOBS + V_JOBS + CONV_JOBS


def f32(ap):
    return ap.bitcast(F32)


def build(nc, xT, w, gains, taps, conv_state, state_k, state_v, yT, kT, v_out, conv_tail):
    with ExitStack() as ctx:
        def sb(name, shape, dt=F32):
            return ctx.enter_context(nc.sbuf_tensor(name, shape, dt))

        def sem(name):
            return ctx.enter_context(nc.semaphore(name))

        act_hi = sb("act_hi", [P, KT, TOK], F32R)
        act_lo = sb("act_lo", [P, KT, TOK], F32R)
        pair_hi = sb("pair_hi", [P, 4, TOK], F32R)
        pair_lo = sb("pair_lo", [P, 4, TOK], F32R)
        w_stage = sb("w_stage", [P, STAGE, 1024])
        w_hi = sb("w_hi", [P, RING, 1024], F32R)
        w_lo = sb("w_lo", [P, RING, 1024], F32R)
        resid = sb("resid", [P, KT * TOK])
        res = resid[:, :].rearrange("p (k t) -> p k t", k=KT)
        pt_hi = sb("pt_hi", [P, KT, 256], F32R)
        pt_lo = sb("pt_lo", [P, KT, 256], F32R)
        out32 = sb("out32", [P, 4, CH])
        out_hl = sb("out_hl", [P, 2, 2 * CH], F32R)
        work = sb("work", [P, 4300])
        age_i = sb("age_i", [P, 1024], I16)
        ident = sb("ident", [P, P])
        ones = sb("ones", [P, P])
        g_sb = sb("g_sb", [P, 3, KT])
        taps_sb = sb("taps_sb", [P, 4, 3])
        cst_sb = sb("cst_sb", [P, 4, NB, 2])
        tail_sb = sb("tail_sb", [P, 4, 18])
        neg8slope = sb("neg8slope", [P, 1])
        gate_cell = sb("gate_cell", [P, 2])
        row_neg, row_sum, row_rec = (sb(n, [P, 4]) for n in ("row_neg", "row_sum", "row_rec"))
        q_s = sb("q_s", [P, 4, SAMP])
        k_s = sb("k_s", [P, 4, SAMP])
        v_s = sb("v_s", [SAMP, DA])
        s_cls = sb("s_cls", [P, 6, NB, HEADS])
        s_near = sb("s_near", [P, NT, NB, HEADS])
        s_self = sb("s_self", [SAMP, NT, NB, HEADS])
        age_cls_i, age_near_i = sb("age_cls_i", [P, 6], I32), sb("age_near_i", [P, NT], I32)
        age_self_i = sb("age_self_i", [SAMP, NT, NB], I32)
        age_cls, age_near, age_self = sb("age_cls", [P, 6]), sb("age_near", [P, NT]), sb("age_self", [SAMP, NT * NB])
        cnt_cls, cnt_near, cnt_self = sb("cnt_cls", [P, 6]), sb("cnt_near", [P, NT]), sb("cnt_self", [SAMP, NT * NB])
        cnt_i, cnt_a, cnt_b = sb("cnt_i", [P, 32], I32), sb("cnt_a", [P, 32]), sb("cnt_b", [P, 32])
        top_cls = sb("top_cls", [P, NB * HEADS])
        top_part = sb("top_part", [NB * HEADS, 3, NT])
        top_col = sb("top_col", [NB * HEADS, NT])
        top_diag = sb("top_diag", [NT, NT, NB * HEADS])
        sum_rec = sb("sum_rec", [SAMP, NB])
        head_mask = sb("head_mask", [SAMP, HEADS, HD])
        sel_t = sb("sel_t", [SAMP, NT])

        rstd = work[:, 0:TOK]
        ssum = work[:, TOK:2 * TOK]
        sq = [work[:, 2112:2112 + TOK], work[:, 3168:3168 + TOK]]
        silu = work[:, 2112:2112 + 2 * TOK].rearrange("p (f t) -> p f t", f=2)
        q_rows = work[0:SAMP, 3168:3168 + DA]
        h_c = acc_c = work[:, 0:TOK]
        c_c = y_c = work[:, TOK:2 * TOK]
        b_c = work[:, 2 * TOK:3 * TOK]
        u_c = work[:, 3 * TOK:3 * TOK + 2 + PROMPT + 6 * NB]
        u_s = u_c[:, 2 + PROMPT:].rearrange("p (b t) -> p b t", b=NB)
        count8 = work[:, 0:1024]
        bias_h = [work[:, 1024:2048], work[:, 2048:3072]]
        age_f = work[:, 3072:4096]
        p_cls5 = resid[:, 7168:8448].rearrange("p (j b t h) -> p j b t h", j=5, b=NB, t=NT)
        spare = f32(out_hl[:, :, :]).rearrange("p a t -> p (a t)")
        p_rest, p_near, p_self = [spare[:, 256 * i:256 * i + 256].rearrange("p (b t h) -> p b t h", b=NB, t=NT)
                                  for i in range(3)]
        p_self = p_self[0:SAMP]
        l_all = spare[:, 768:1024]
        o_b = work[0:SAMP, 2560:3072]
        o_s = work[:, 4096:4096 + P]
        qc = resid[:, 0:512]
        qn = resid[:, 512:2560]
        k_far = resid[:, 2560:4096]
        k_mid = resid[:, 4096:5632]
        k_near = resid[:, 5632:6144]
        prod = resid[:, 6144:8192]
        v_tiles = [resid[:, 3584 * i:3584 * (i + 1)].rearrange("p (j n) -> p j n", j=7) for i in range(2)]
        prow = [resid[:, 1024 * i:1024 * (i + 1)] for i in range(PROWS)]
        pts_hi, pts_lo = ([t, w[:, 1:3, :].rearrange("p u x -> p (u x)").rearrange("p (k t) -> p k t", k=KT)]
                          for t, w in ((pt_hi, w_hi), (pt_lo, w_lo)))
        o_low = [out32[0:HD, i, 0:256] for i in range(2)]
        o32 = [out32[:, 2 + i, 0:256] for i in range(2)]
        stack = [a[:, 4:8, :].rearrange("p k t -> p (k t)") for a in (act_hi, act_lo)]
        st_q = [s[:, 0:1024] for s in stack]
        st_khi = [s[:, 1024:2048] for s in stack]
        st_klo = [s[:, 2048:3072] for s in stack]
        st_v = [s[:, 3072:4096].rearrange("p (k e) -> p k e", k=KT) for s in stack]

        ps = ctx.enter_context(nc.psum_tensor("ps", [P, 8, 512], F32))

        qk_d = nc.dram_tensor("qk_d", [8, P, 2, TOK], F32).ap()
        v_d = nc.dram_tensor("v_d", [HEADS, P, KT, P], F32).ap()
        q_rows_d = nc.dram_tensor("q_rows_d", [SAMP, DA], F32).ap()

        consts_in = sem("consts_in")
        x_in = [sem(f"x_in{k}") for k in range(KT)]
        w_in = [sem(f"w_in{i}") for i in range(STAGE)]
        part_stored = [sem("part_stored0"), sem("part_stored1")]
        rows_stored = [sem("rows_stored0"), sem("rows_stored1")]
        q_rows_out, ld_qc, ld_qn = sem("q_rows_out"), sem("ld_qc"), sem("ld_qn")
        ld_far, ld_mid, ld_near = sem("ld_far"), sem("ld_mid"), sem("ld_near")
        v_ld = [sem("v_ld0"), sem("v_ld1")]
        st_in = [sem("st_in0"), sem("st_in1")]
        x2_in = [sem(f"x2_in{k}") for k in range(KT)]
        y_out = sem("y_out")
        made = sem("made")
        w_split = sem("w_split")
        pool_chain = sem("pool_chain")
        pool_normed = sem("pool_normed")
        ss_done, ss_all = sem("ss_done"), sem("ss_all")
        job_done = sem("job_done")
        q_turned, self_scores = sem("q_turned"), sem("self_scores")
        new_pe, new_pv, new_turned = sem("new_pe"), sem("new_pv"), sem("new_turned")
        scored, turned, pv_done = sem("scored"), sem("turned"), sem("pv_done")
        sq_done, root, hi_done = sem("sq_done"), sem("root"), sem("hi_done")
        job_copied, q_rows_done = sem("job_copied"), sem("q_rows_done")
        new_exp = sem("new_exp")
        exped, pt_hi_done, low_done, mix_hi = sem("exped"), sem("pt_hi_done"), sem("low_done"), sem("mix_hi")
        h_sq, silu_done, hid_hi = sem("h_sq"), sem("silu_done"), sem("hid_hi")
        dve_chain = sem("dve_chain")
        mean_sq, y_done, lo_done = sem("mean_sq"), sem("y_done"), sem("lo_done")
        part_hi, part_lo, new_kept = sem("part_hi"), sem("part_lo"), sem("new_kept")
        conv_free = sem("conv_free")
        key_used, key_sum = sem("key_used"), sem("key_sum")
        top_ready, shifted, l_ready = sem("top_ready"), sem("shifted"), sem("l_ready")
        ob_done, new_mixed = sem("ob_done"), sem("new_mixed")
        biased, rec_done, normed = sem("biased"), sem("rec_done"), sem("normed")
        pt_lo_done, o_sum, mix_lo = sem("pt_lo_done"), sem("o_sum"), sem("mix_lo")
        h_done, h_ss = sem("h_done"), sem("h_ss")
        hidden, hid_lo, added = sem("hidden"), sem("hid_lo"), sem("added")

        block = ctx.enter_context(nc.Block())

        def cols(c):
            return slice(CH * c, CH * (c + 1))

        @block.sync
        def _(sp):
            def unit(u, slot=None):
                if slot is not None or u >= STAGE:
                    sp.wait_ge(w_split, 2 * (u - STAGE) + 2)
                s = u % STAGE if slot is None else slot
                sp.dma_start(w_stage[:, s, :], w[u]).then_inc(w_in[s], 16)

            unit(0)
            sp.dma_start(g_sb[:, :, :], gains).then_inc(consts_in, 16)
            sp.dma_start(taps_sb[:, :, :], taps).then_inc(consts_in, 16)
            sp.dma_start(cst_sb[:, :, :, :], conv_state).then_inc(consts_in, 16)
            for k in range(KT):
                sp.dma_start(res[:, k, :], xT[:, k, :]).then_inc(x_in[k], 16)
            for u in range(1, 4):
                unit(u)

            def load_keys(n):
                b, which = divmod(n, 3)
                if n >= 3:
                    sp.wait_ge(key_used, n + 1)
                else:
                    sp.wait_ge(key_used, 3)
                if which == 0:
                    far = state_k[b, 0:1536].rearrange("(i j r) n -> r i j n", i=32, j=3)
                    for t in range(NT):
                        sp.dma_start(k_far[32 * t:32 * t + 32].rearrange("p (j n) -> p j n", j=3),
                                     far[t]).then_inc(ld_far, 16)
                elif which == 1:
                    mid = state_k[b, 1536:1920].rearrange("(i j r) n -> r i j n", i=32, j=3)
                    sp.dma_start(qc, q_rows_d.rearrange("(b t) n -> b t n", b=NB)[b].unsqueeze(1)
                                 .broadcast_to([NT, 32, DA])).then_inc(ld_qc, 16)
                    for t in range(NT):
                        sp.dma_start(k_mid[32 * t:32 * t + 32].rearrange("p (j n) -> p j n", j=3),
                                     mid[t]).then_inc(ld_mid, 16)
                else:
                    sp.dma_start(qn, q_rows_d.rearrange("(b t) n -> b (t n)", b=NB)[b].unsqueeze(0)
                                 .broadcast_to([P, NT * DA])).then_inc(ld_qn, 16)
                    sp.dma_start(k_near, state_k[b, 1920:2048]).then_inc(ld_near, 16)

            for n in range(QK_UNITS):
                for c in range(NC):
                    j = NC * n + c
                    sp.wait_ge(part_lo, j + 1)
                    sp.dma_start(qk_d[n, :, :, cols(c)],
                                 f32(out_hl[:, j % 2, :]).rearrange("p (s t) -> p s t", s=2)
                                 ).then_inc(part_stored[j % 2], 16)
                    if n >= 4:
                        sp.dma_start(kT[n - 4, :, cols(c)], out32[:, j % 2, :]).then_inc(rows_stored[j % 2], 16)
                    if j == Q_ROWS_JOB:
                        sp.wait_ge(q_rows_done, 1)
                        sp.dma_start(q_rows_d, q_rows).then_inc(q_rows_out, 16)
                        sp.wait_ge(q_rows_out, 16)
                        for m in range(3):
                            load_keys(m)
                    if j in KEYS_BEHIND:
                        load_keys(KEYS_BEHIND.index(j) + 3)
                unit(n + 4)

            for i in range(V_JOBS):
                j, vb, tt = QK_JOBS + i, i // VT, i % VT
                m = P if tt < VT - 1 else SAMP
                sp.wait_ge(part_lo, j + 1)
                if tt < VT - 1:
                    sp.dma_start(v_d[4 * vb:4 * vb + 4, :, tt, :].rearrange("h p e -> p h e"),
                                 f32(out_hl[:, j % 2, 0:512]).rearrange("p (h e) -> p h e", h=4)
                                 ).then_inc(part_stored[j % 2], 16)
                sp.dma_start(v_out[tt * P:tt * P + m, 256 * vb:256 * vb + 256],
                             out32[0:m, j % 2, 0:256]).then_inc(rows_stored[j % 2], 16)
                if i == 6:
                    unit(12)
                if tt == VT - 1:
                    unit(13 + vb)
                if j in KEYS_BEHIND:
                    load_keys(KEYS_BEHIND.index(j) + 3)
            unit(15)

            for p in range(4):
                for n in range(4):
                    if p < 3 and KEYS_EARLY + 4 * p + n + 3 < 3 * NB:
                        load_keys(KEYS_EARLY + 4 * p + n + 3)
                    if n < 3 and 16 + 3 * p + n < OUT0 + 1 + STAGE:
                        unit(16 + 3 * p + n)

            sp.wait_ge(key_sum, 3 * NB)
            for b in range(NB):
                vt, ld = v_tiles[b % 2], v_ld[b % 2]
                far = state_v[b, 0:1536].rearrange("(i j r) n -> r i j n", i=32, j=3)
                mid = state_v[b, 1536:1920].rearrange("(i j r) n -> r i j n", i=32, j=3)
                if b >= 2:
                    sp.wait_ge(new_pv, b - 1)
                for t in range(NT):
                    sp.dma_start(vt[32 * t:32 * t + 32, 0:3, :], far[t]).then_inc(ld, 16)
                    sp.dma_start(vt[32 * t:32 * t + 32, 3:6, :], mid[t]).then_inc(ld, 16)
                sp.dma_start(vt[:, 6, :], state_v[b, 1920:2048]).then_inc(ld, 16)

            def load_head(hh, tile):
                r = slice(HD * hh, HD * hh + HD)
                s = st_in[hh]
                for half in range(2):
                    d = slice(HD * half, HD * half + HD)
                    sp.dma_start(f32(st_q[hh][d]), qk_d[tile, r, half, 0:PROMPT]).then_inc(s, 16)
                    sp.dma_start(f32(st_khi[hh][d]), qk_d[4 + tile, r, 0, 0:PROMPT]).then_inc(s, 16)
                    sp.dma_start(f32(st_klo[hh][d]), qk_d[4 + tile, r, 1, 0:PROMPT]).then_inc(s, 16)
                sp.dma_start(f32(st_v[hh]), v_d[2 * tile + hh]).then_inc(s, 16)

            for s in range(2):
                sp.wait_ge(part_stored[s], 16 * PARTS_STORED[s])
            sp.wait_ge(job_done, IN_JOBS)
            load_head(0, 0)
            load_head(1, 0)
            with sp.Fori(0, 3) as it:
                for hh in range(2):
                    sp.wait_ge(pv_done, 8 * it + 4 * hh + 4)
                    load_head(hh, it + 1)

            sp.wait_ge(mix_lo, 4 * HEADS)
            for k in range(KT):
                sp.dma_start(res[:, k, :], xT[:, k, :]).then_inc(x2_in[k], 16)
            for u in range(OUT0 + 1 + STAGE, 37):
                unit(u)
            with sp.Fori(0, 10) as it:
                for s in range(6):
                    unit(6 * it + 37 + s, (37 + s) % STAGE)
            unit(97)

            for i in range(NC * KT):
                c, k = divmod(i, KT)
                sp.wait_ge(y_done, 2 * NC * KT + i + 1)
                sp.dma_start(yT[:, k, cols(c)], res[:, k, cols(c)]).then_inc(y_out, 16)
            sp.wait_ge(conv_free, 5)
            sp.dma_start(conv_tail, tail_sb[:, :, :]).then_inc(y_out, 16)
            sp.wait_ge(y_out, 16 * (NC * KT + 1))
            for s in range(2):
                sp.wait_ge(rows_stored[s], 16 * ROWS_STORED[s])

        @block.gpsimd
        def _(pool):
            chain = Chain(pool, pool_chain)
            chain(pool.memset(ident[:, :], 0.0))
            pool.memset(ones[:, :], 1.0).then_inc(made, 1)
            chain(pool.affine_select(out=ident[:, :], in_=ident[:, :], compare_op=ALU.not_equal, fill=1.0,
                                     base=0, pattern=[[-1, P]], channel_multiplier=1))

            def split(u, slot, stage, arrived, released):
                pool.wait_ge(w_in[stage], arrived)
                if released is not None:
                    pool.wait_ge(job_done, released)
                    pool.tensor_tensor(gate_cell[:, 0:1], ones[:, 0:1], ones[:, 0:1], ALU.mult)
                pool.tensor_copy(w_hi[:, slot, :], w_stage[:, stage, :]).then_inc(w_split, 1)
                pool.wait_ge(w_split, 2 * u + 1)
                pool.tensor_tensor(w_lo[:, slot, :], w_stage[:, stage, :], f32(w_hi[:, slot, :]),
                                   ALU.subtract).then_inc(w_split, 1)

            def straight(u):
                split(u, u % RING, u % STAGE, 16 * (u // STAGE + 1), jobs_through(u - RING) if u >= RING else None)

            straight(0)
            chain(pool.iota(age_i[:, :], pattern=[[-1, 1024]], base=896, channel_multiplier=1))
            for t in range(NT):
                q = slice(32 * t, 32 * t + 32)
                chain(pool.iota(age_cls_i[q, 0:3], pattern=[[-16, 3]], base=2048, channel_multiplier=-48))
                chain(pool.iota(age_cls_i[q, 3:6], pattern=[[-4, 3]], base=512, channel_multiplier=-12))
            chain(pool.iota(age_near_i[:, :], pattern=[[1, NT]], base=128, channel_multiplier=-1))
            chain(pool.iota(age_self_i[:, :, :], pattern=[[1, NT], [4, NB]], base=0, channel_multiplier=-1))
            chain(pool.affine_select(out=age_self_i[:, :, :], in_=age_self_i[:, :, :], compare_op=ALU.is_ge,
                                     fill=-1.0, base=0, pattern=[[0, NT], [-4, NB]], channel_multiplier=1))
            chain(pool.affine_select(out=age_self_i[:, :, :], in_=age_self_i[:, :, :], compare_op=ALU.is_ge,
                                     fill=-1.0, base=3, pattern=[[0, NT], [4, NB]], channel_multiplier=-1))
            chain(pool.memset(head_mask[:, :, :], 0.0))
            for t in range(NT):
                chain(pool.affine_select(out=head_mask[:, :, :], in_=head_mask[:, :, :],
                                         compare_op=ALU.not_equal, fill=1.0, base=-8 * t,
                                         pattern=[[-1, HEADS], [0, HD]], channel_multiplier=1))
            chain(pool.memset(sel_t[:, :], 1.0))
            chain(pool.affine_select(out=sel_t[:, :], in_=sel_t[:, :], compare_op=ALU.is_ge, fill=0.0,
                                     base=0, pattern=[[-8, NT]], channel_multiplier=1))
            pool.affine_select(out=sel_t[:, :], in_=sel_t[:, :], compare_op=ALU.is_ge, fill=0.0,
                               base=7, pattern=[[8, NT]], channel_multiplier=-1).then_inc(made, 1)

            for u in range(1, OUT0 + 1):
                straight(u)

            def normalise(it, s):
                it, back, s = lagged(it, s)
                n = P * (s % KT + 1)
                if s % KT >= POOL_TILE:
                    pool.wait_ge(rec_done, 16 * it + s + 1 - 16 * back)
                    pool.tensor_tensor(prow[s % PROWS][:, 0:n], prow[s % PROWS][:, 0:n],
                                       row_rec[:, s % 4:s % 4 + 1].broadcast_to([P, n]),
                                       ALU.mult).then_inc(pool_normed, 1)

            def tick(it, s, first=False, last=False):
                if in_range(s - 1, first, last):
                    normalise(it, s - 1)

            for s in range(16):
                tick(0, s, first=True)
            with pool.Fori(1, 4) as it:
                for s in range(16):
                    tick(it, s)
            tick(4, 0, last=True)

            pool.wait_ge(pv_done, 4 * HEADS)
            for u in range(OUT0 + 1, FFN0 + 16):
                straight(u)
            with pool.Fori(0, 4) as it:
                for s in range(12):
                    u = FFN0 + 16 + s
                    split(12 * it + u, u % RING, u % STAGE, 96 * it + 16 * (u // STAGE + 1),
                          72 * it + jobs_through(u - RING))
            straight(96)
            straight(97)

        @block.tensor
        def _(pe):
            def unit_ready(u):
                pe.wait_ge(w_split, 2 * u + 2)

            def three_pass(out, unit_slot, k, wcols, rhs_hi, rhs_lo, first, last):
                hi, lo = w_hi[:, unit_slot, wcols], w_lo[:, unit_slot, wcols]
                pe.matmul(out, hi, rhs_hi, start=first, stop=False)
                pe.matmul(out, hi, rhs_lo, start=False, stop=False)
                return pe.matmul(out, lo, rhs_hi, start=False, stop=last)

            def tile_job(bank, c, slot):
                for k in range(KT):
                    mm = three_pass(ps[:, bank, 0:CH], slot, k, slice(P * k, P * k + P),
                                    act_hi[:, k, cols(c)], act_lo[:, k, cols(c)], k == 0, k == KT - 1)
                mm.then_inc(job_done, 1)

            pe.wait_ge(made, 1)
            for k in range(KT):
                pe.wait_ge(sq_done, k + 1)
                for c in range(NC):
                    mm = pe.matmul(ps[:, c, 0:CH], ones[:, :], sq[k % 2][:, cols(c)], start=(k == 0), stop=(k == KT - 1))
                mm.then_inc(ss_done, 1)
            pe.wait_ge(mean_sq, NC)

            for n in range(QK_UNITS):
                unit_ready(n)
                for c in range(NC):
                    j = NC * n + c
                    if n == 0:
                        pe.wait_ge(lo_done, KT * (c + 1))
                    if j >= 6:
                        pe.wait_ge(job_copied, j - 5)
                    tile_job(3 * (n % 2) + c, c, n % RING)
                    if j == Q_ROWS_JOB:
                        pe.wait_ge(new_kept, 4)
                        for m in range(4):
                            mm = pe.transpose(ps[0:SAMP, 6, P * m:P * m + P], q_s[:, m, :], ident[:, :])
                        mm.then_inc(q_turned, 1)

            pe.wait_ge(new_kept, 8)
            for odd in range(2):
                if odd:
                    pe.wait_ge(self_scores, 1)
                r = slice(HD * odd, HD * odd + HD)
                for n in range(4):
                    mm = pe.matmul(ps[0:SAMP, 7, 2 * n + odd:256:HEADS], k_s[r, n, :],
                                   q_s[r, n, :].rearrange("p (b t) -> p t b", b=NB), start=True, stop=True)
                mm.then_inc(self_scores, 1)

            for i in range(V_JOBS):
                j, vb, tt = QK_JOBS + i, i // VT, i % VT
                m = P if tt < VT - 1 else SAMP
                tk = slice(P * tt, P * tt + m)
                if tt == 0:
                    unit_ready(QK_UNITS + 2 * vb + 1)
                pe.wait_ge(job_copied, j - 5)
                for k in range(KT):
                    slot = (QK_UNITS + 2 * vb + k // 4) % RING
                    wc = slice(256 * (k % 4), 256 * (k % 4) + 256)
                    out = ps[0:m, i % 6, 0:256]
                    pe.matmul(out, act_hi[:, k, tk], w_hi[:, slot, wc], start=(k == 0), stop=False)
                    pe.matmul(out, act_hi[:, k, tk], w_lo[:, slot, wc], start=False, stop=False)
                    mm = pe.matmul(out, act_lo[:, k, tk], w_hi[:, slot, wc], start=False, stop=(k == KT - 1))
                mm.then_inc(job_done, 1)

            def new_maxima(step):
                pe.wait_ge(top_ready, step + 1)
                if step == 0:
                    pe.transpose(ps[0:64, 7, 0:P], top_cls[:, :], ident[:, :])
                    for t in range(NT):
                        mm = pe.transpose(ps[0:64, 7, P + SAMP * t:P + SAMP * t + SAMP],
                                          s_self[:, t].rearrange("p b h -> p (b h)"), ident[0:SAMP, 0:SAMP])
                    for t in range(NT):
                        mm = pe.transpose(ps[0:64, 6, P * t:P * t + P], s_near[:, t].rearrange("p b h -> p (b h)"),
                                          ident[:, :])
                elif step == 1:
                    mm = pe.transpose(ps[0:NT, 7, 256:320], top_col[:, :], ident[0:64, 0:64])
                else:
                    mm = pe.matmul(ps[:, 6, 0:256], ones[0:NT, :], top_diag[:, :, :].rearrange("p t x -> p (t x)"),
                                   start=True, stop=True)
                mm.then_inc(new_pe, 1)

            for p in range(4):
                for kind in range(3):
                    n = 3 * p + kind
                    unit_ready(CONV0 + n)
                    for c in range(NC):
                        j = QK_JOBS + V_JOBS + NC * n + c
                        pe.wait_ge(job_copied, j - (2 if n % 3 == 0 else 5))
                        tile_job(3 * (kind % 2) + c, c, n % RING)
                        if p == 3 and NC * kind + c in MAXIMA_BEHIND:
                            new_maxima(MAXIMA_BEHIND.index(NC * kind + c))

            pe.wait_ge(job_copied, IN_JOBS)

            def to_channels(b):
                pe.wait_ge(ob_done, b + 1)
                for n in range(4):
                    mm = pe.matmul(ps[:, 0, 32 * n + 4 * b:32 * n + 4 * b + 4], o_b[:, P * n:P * n + P],
                                   sel_t[:, :], start=True, stop=True)
                mm.then_inc(new_turned, 1)

            for b in range(NB):
                vt = v_tiles[b % 2]
                out = ps[0:SAMP, 2 + b % 2, :]
                pe.wait_ge(v_ld[b % 2], 144 * (b // 2 + 1))
                if b == 0:
                    pe.wait_ge(new_exp, 10)
                if b >= 2:
                    pe.wait_ge(ob_done, b - 1)
                for j in range(6):
                    p_j = p_cls5[:, j, b] if j < 5 else p_rest[:, b]
                    pe.matmul(out, p_j.rearrange("p t h -> p (t h)"), vt[:, j, :], start=(j == 0), stop=False)
                pe.matmul(out, p_near[:, b].rearrange("p t h -> p (t h)"), vt[:, 6, :], start=False, stop=False)
                pe.matmul(out, p_self[:, b].rearrange("p t h -> p (t h)"), v_s[:, :], start=False,
                          stop=True).then_inc(new_pv, 1)
                if b == 0:
                    pe.wait_ge(l_ready, 1)
                    for i in range(NB):
                        mm = pe.matmul(ps[0:SAMP, 1, i:i + 1], l_all[:, 32 * i:32 * i + 32], ones[:, 0:1],
                                       start=True, stop=True)
                    mm.then_inc(new_pe, 1)
                if b >= 1:
                    to_channels(b - 1)
            to_channels(NB - 1)
            pe.wait_ge(new_mixed, 1)

            def scores(it, s):
                it, back, s = lagged(it, s)
                hh, i = divmod(s, KT)
                if i == 0:
                    pe.wait_ge(st_in[hh], 112 * it + 112 * (1 - back))
                if not (is_first(it, back) and s < 2):
                    pe.wait_ge(biased, 16 * it + s - 1 - 16 * back)
                q = st_q[hh][:, P * i:P * i + P]
                for half, width in score_blocks(i):
                    kc = slice(512 * half, 512 * half + width)
                    out = ps[:, 2 * (s % 2) + half, 0:width]
                    pe.matmul(out, q, st_khi[hh][:, kc], start=True, stop=False)
                    mm = pe.matmul(out, q, st_klo[hh][:, kc], start=False, stop=True)
                mm.then_inc(scored, 1)

            def turn(it, s):
                it, back, s = lagged(it, s)
                done, per = (pool_normed, 2 * (KT - POOL_TILE)) if s % KT >= POOL_TILE else (normed, 2 * POOL_TILE)
                pe.wait_ge(done, per * it + norms_through(s) - per * back)
                for f, (fs, bank, k0, nk) in enumerate(FILLS):
                    if fs != s:
                        continue
                    if not (is_first(it, back) and f < 3):
                        pe.wait_ge(pt_lo_done, 24 * it + f - 2 - 24 * back)
                    for k in range(nk):
                        mm = pe.transpose(ps[:, bank, P * k:P * k + P],
                                          prow[s % PROWS][:, P * (k0 + k):P * (k0 + k) + P], ident[:, :])
                    mm.then_inc(turned, 1)

            def values(it, s):
                it, back, s = lagged(it, s)
                u = s // 2
                hh, i = divmod(s, KT)
                pe.wait_ge(pt_lo_done, 24 * it + fills_through(s) - 24 * back)
                if not (is_first(it, back) and u == 0):
                    pe.wait_ge(o_sum, 8 * it + u - 8 * back)
                for k in range(i + 1):
                    qs = slice(P, 256) if k == i else slice(0, 256)
                    out = ps[:, 7, qs]
                    pe.matmul(out, st_v[hh][:, k, :], pts_hi[u % 2][:, k, qs], start=(k == 0), stop=False)
                    mm = pe.matmul(out, st_v[hh][:, k, :], pts_lo[u % 2][:, k, qs], start=False, stop=(k == i))
                mm.then_inc(pv_done, 1)

            def tick(it, s, first=False, last=False):
                if not last:
                    scores(it, s)
                if in_range(s - TURN_LAG, first, last):
                    turn(it, s - TURN_LAG)
                if (s - VALUES_LAG) % 2 == 1 and in_range(s - VALUES_LAG, first, last):
                    values(it, s - VALUES_LAG)

            for s in range(16):
                tick(0, s, first=True)
            with pe.Fori(1, 4) as it:
                for s in range(16):
                    tick(it, s)
            for s in range(LAST_TICKS):
                tick(4, s, last=True)
            pe.wait_ge(o_sum, 32)

            pe.wait_ge(mix_lo, 4 * HEADS)
            pe.wait_ge(new_mixed, 2)
            pe.wait_ge(conv_free, 5)
            for n in range(OUT_UNITS):
                unit_ready(OUT0 + n)
                for c in range(NC):
                    j = NC * n + c
                    if n >= 2:
                        pe.wait_ge(h_done, j - 5)
                    for k in range(KT):
                        hi, lo = (act_hi, act_lo) if k < 4 else (pair_hi, pair_lo)
                        mm = three_pass(ps[:, 3 * (n % 2) + c, 0:CH], (OUT0 + n) % RING, k, slice(P * k, P * k + P),
                                        hi[:, k % 4, cols(c)], lo[:, k % 4, cols(c)], k == 0, k == KT - 1)
                    mm.then_inc(job_done, 1)

            def sum_of_squares(which):
                for c in range(NC):
                    pe.wait_ge(h_ss, 24 * which + 22 + c)
                    pe.matmul(ps[:, c, 0:CH], ones[:, :], ssum[:, cols(c)], start=True, stop=True).then_inc(ss_all, 1)

            sum_of_squares(0)

            def gate_up(it, g, first=False):
                for n in range(4):
                    u = FFN0 + n if first else FFN0 + 6 * g - 2 + n
                    unit_ready(12 * it + u)
                    for c in range(NC):
                        if first and n == 0:
                            pe.wait_ge(lo_done, NC * KT + KT * (c + 1))
                        if n >= 2:
                            pe.wait_ge(silu_done, 12 * it + 6 * g + 3 * (n - 2) + c + 1)
                        elif not first:
                            pe.wait_ge(hidden, 12 * it + 6 * (g - 1) + 3 * n + c + 1)
                        tile_job(3 * (n % 2) + c, c, u % RING)

            def down(it, g, last=False):
                u0 = UNITS - 2 if last else FFN0 + 6 * (g + 1) + 2
                unit_ready(u0 + 1 if last else 12 * it + u0 + 1)
                pe.wait_ge(hid_lo, 12 * it + 6 * g + 6)
                for n in range(KT):
                    for c in range(NC):
                        i = NC * n + c
                        if i >= 2:
                            if last:
                                pe.wait_ge(h_done, NC * KT + i - 1)
                            else:
                                pe.wait_ge(added, 48 * it + 24 * g + i - 1)
                        for f in range(2):
                            mm = three_pass(ps[:, 6 + i % 2, 0:CH], (u0 + f) % RING, f, slice(P * n, P * n + P),
                                            pair_hi[:, 2 * (g % 2) + f, cols(c)], pair_lo[:, 2 * (g % 2) + f, cols(c)],
                                            f == 0, f == 1)
                        mm.then_inc(job_done, 1)
                if not last:
                    pe.wait_ge(added, 48 * it + 24 * g + 24)

            gate_up(0, 0, first=True)
            with pe.Fori(0, 5) as it:
                for g in (1, 2):
                    gate_up(it, g)
                    down(it, g - 1)
            down(5, 0, last=True)
            sum_of_squares(1)

        @block.scalar
        def _(act):
            def copy(out, in_):
                return act.activation(out, in_, ACT.Copy)

            def roots(which):
                for c in range(NC):
                    act.wait_ge(mean_sq, NC * which + c + 1)
                    act.activation(rstd[:, cols(c)], rstd[:, cols(c)], ACT.Sqrt).then_inc(root, 1)

            def normal_hi(which):
                for i in range(NC * KT):
                    c, k = divmod(i, KT)
                    act.wait_ge(y_done, NC * KT * which + i + 1)
                    copy(act_hi[:, k, cols(c)], out32[:, 2 + i % 2, :]).then_inc(hi_done, 1)

            for k in range(KT):
                act.wait_ge(x_in[k], 16)
                if k >= 2:
                    act.wait_ge(ss_done, k - 1)
                act.activation(sq[k % 2], res[:, k, :], ACT.Square).then_inc(sq_done, 1)
            roots(0)
            normal_hi(0)

            for j in range(QK_JOBS + V_JOBS):
                act.wait_ge(job_done, j + 1)
                if j >= 2:
                    act.wait_ge(part_lo, j - 1)
                if rows_before(j):
                    act.wait_ge(rows_stored[j % 2], 16 * rows_before(j))
                if j < QK_JOBS:
                    n, c = divmod(j, NC)
                    copy(out32[:, j % 2, :], ps[:, 3 * (n % 2) + c, 0:CH]).then_inc(job_copied, 1)
                else:
                    i = j - QK_JOBS
                    m = P if i % VT < VT - 1 else SAMP
                    copy(out32[0:m, j % 2, 0:256], ps[0:m, i % 6, 0:256]).then_inc(job_copied, 1)
                if j == Q_ROWS_JOB:
                    act.wait_ge(q_turned, 1)
                    copy(q_rows, ps[0:SAMP, 6, :]).then_inc(q_rows_done, 1)

            act.wait_ge(conv_free, 1)
            for p in range(4):
                if p:
                    act.wait_ge(conv_free, p + 1)
                for kind in range(3):
                    for c in range(NC):
                        act.wait_ge(job_done, QK_JOBS + V_JOBS + 9 * p + 3 * kind + c + 1)
                        copy((h_c, c_c, b_c)[kind][:, cols(c)],
                             ps[:, 3 * (kind % 2) + c, 0:CH]).then_inc(job_copied, 1)

            act.wait_ge(shifted, 1)
            act.activation(p_near[:, :, :, :].rearrange("p b t h -> p t b h"), s_near[:, :, :, :],
                           ACT.Exp).then_inc(new_exp, 1)
            act.activation(p_self[:, :, :, :].rearrange("p b t h -> p t b h"), s_self[:, :, :, :],
                           ACT.Exp).then_inc(new_exp, 1)
            for t in range(NT):
                q = slice(32 * t, 32 * t + 32)
                act.activation(p_cls5[q, :, :, t, :], s_cls[q, 0:5, :, :], ACT.Exp).then_inc(new_exp, 1)
                act.activation(p_rest[q, :, t, :], s_cls[q, 5, :, :], ACT.Exp).then_inc(new_exp, 1)

            for c in range(2):
                act.wait_ge(rows_stored[c], 16 * ROWS_STORED[c])

            def exponentials(it, s):
                act.wait_ge(biased, 16 * it + s + 1)
                n = P * (s % KT + 1)
                act.activation(prow[s % PROWS][:, 0:n], prow[s % PROWS][:, 0:n], ACT.Exp, scale=-1.0,
                               bias=row_neg[:, s % 4:s % 4 + 1],
                               accum_out=row_sum[:, s % 4:s % 4 + 1]).then_inc(exped, 1)

            def high(it, s):
                it, back, s = lagged(it, s)
                u = s // 2
                for f, (fs, bank, k0, nk) in enumerate(FILLS):
                    if fs != s:
                        continue
                    act.wait_ge(turned, 24 * it + f + 1 - 24 * back)
                    if not (is_first(it, back) and u < 2):
                        act.wait_ge(pv_done, 8 * it + u - 1 - 8 * back)
                    copy(pts_hi[u % 2][:, k0:k0 + nk, P * (s % 2):P * (s % 2) + P],
                         ps[:, bank, 0:P * nk].rearrange("p (k t) -> p k t", k=nk)).then_inc(pt_hi_done, 1)

            def lower_half(it, s):
                it, back, s = lagged(it, s)
                u = s // 2
                act.wait_ge(pv_done, 8 * it + u + 1 - 8 * back)
                if not (is_first(it, back) and u < 2):
                    act.wait_ge(o_sum, 8 * it + u - 1 - 8 * back)
                copy(o_low[u % 2], ps[HD:P, 7, 0:256]).then_inc(low_done, 1)

            def outputs(it, s):
                it, back, s = lagged(it, s)
                u = s // 2
                r = slice(HD * (u // 4), HD * (u // 4) + HD)
                act.wait_ge(o_sum, 8 * it + u + 1 - 8 * back)
                copy(act_hi[r, it - back, 256 * (u % 4):256 * (u % 4) + 256], o32[u % 2][r]).then_inc(mix_hi, 1)

            def tick(it, s, first=False, last=False):
                if (s - VALUES_LAG) % 2 == 1 and in_range(s - VALUES_LAG, first, last):
                    lower_half(it, s - VALUES_LAG)
                if in_range(s - HIGH_LAG, first, last):
                    high(it, s - HIGH_LAG)
                if not last:
                    exponentials(it, s)
                if (s - MIX_LAG) % 2 == 1 and in_range(s - MIX_LAG, first, last):
                    outputs(it, s - MIX_LAG)

            for s in range(16):
                tick(0, s, first=True)
            with act.Fori(1, 4) as it:
                for s in range(16):
                    tick(it, s)
            for s in range(LAST_TICKS):
                tick(4, s, last=True)

            def squares(which):
                for j in range(NC * KT):
                    n, c = divmod(j, NC)
                    act.wait_ge(h_done, NC * KT * which + j + 1)
                    if j >= 6:
                        act.wait_ge(h_ss, NC * KT * which + j - 5)
                    act.activation(sq[n % 2][:, cols(c)], res[:, n, cols(c)], ACT.Square).then_inc(h_sq, 1)

            squares(0)
            roots(1)
            normal_hi(1)

            def gates(it, g, first=False):
                job = OUT_JOB0 + 24 if first else 72 * it + FFN_JOB0 + 36 * g
                for i in range(6):
                    f, c = divmod(i, NC)
                    act.wait_ge(job_done, job + i + 1)
                    if not first:
                        act.wait_ge(hid_lo, 12 * it + 6 * (g - 1) + i + 1)
                    act.activation(silu[:, f, cols(c)], ps[:, 3 * f + c, 0:CH], ACT.Silu).then_inc(silu_done, 1)
                for i in range(6):
                    f, c = divmod(i, NC)
                    act.wait_ge(hidden, 12 * it + 6 * g + i + 1)
                    if not first:
                        act.wait_ge(job_done, job)
                    copy(pair_hi[:, 2 * (g % 2) + f, cols(c)], silu[:, f, cols(c)]).then_inc(hid_hi, 1)

            gates(0, 0, first=True)
            with act.Fori(0, 5) as it:
                for g in (1, 2):
                    gates(it, g)
            squares(1)
            roots(2)

        @block.vector
        def _(dve):
            chain = Chain(dve, dve_chain)

            def count_steps(out, age, age_i, n_i, a, b, scale):
                yield chain(dve.tensor_copy(age, age_i))
                yield chain(dve.tensor_scalar(n_i, age_i, 3, None, ALU.bitwise_and))
                yield chain(dve.tensor_scalar(b, n_i, 0.0, None, ALU.is_equal))
                yield chain(dve.scalar_tensor_tensor(a, age, 512.0, b, ALU.is_le, ALU.mult))
                yield chain(dve.scalar_tensor_tensor(a, age, 128.0, a, ALU.is_le, ALU.add))
                yield chain(dve.tensor_scalar(n_i, age_i, 15, None, ALU.bitwise_and))
                yield chain(dve.tensor_scalar(b, n_i, 0.0, None, ALU.is_equal))
                yield chain(dve.scalar_tensor_tensor(b, age, 2048.0, b, ALU.is_le, ALU.mult))
                yield chain(dve.tensor_tensor(a, a, b, ALU.add))
                yield chain(dve.scalar_tensor_tensor(a, age, 0.0, a, ALU.is_ge, ALU.mult))
                yield chain(dve.tensor_scalar(b, a, 0.0, MASKED * scale, ALU.is_equal, ALU.mult))
                yield chain(dve.tensor_scalar(out, a, 2.0, LN2 * scale, ALU.is_equal, ALU.mult))
                yield chain(dve.tensor_tensor(out, out, b, ALU.add))
                yield chain(dve.tensor_scalar(b, a, 3.0, LN3 * scale, ALU.is_equal, ALU.mult))
                yield chain(dve.tensor_tensor(out, out, b, ALU.add))

            def count_log(*args):
                for _ in count_steps(*args):
                    pass

            def norm(which):
                for c in range(NC):
                    if which == 0:
                        dve.wait_ge(ss_done, KT)
                    else:
                        dve.wait_ge(ss_all, NC * (which - 1) + c + 1)
                    dve.tensor_scalar(rstd[:, cols(c)], ps[:, c, 0:CH], 1.0 / D, EPS,
                                      ALU.mult, ALU.add).then_inc(mean_sq, 1)
                for c in range(NC):
                    dve.wait_ge(root, NC * which + c + 1)
                    chain(dve.reciprocal(rstd[:, cols(c)], rstd[:, cols(c)]))

                def low(i):
                    c, k = divmod(i, KT)
                    dve.wait_ge(hi_done, NC * KT * which + i + 1)
                    dve.tensor_tensor(act_lo[:, k, cols(c)], out32[:, 2 + i % 2, :], f32(act_hi[:, k, cols(c)]),
                                      ALU.subtract).then_inc(lo_done, 1)

                for i in range(NC * KT):
                    c, k = divmod(i, KT)
                    dst = res[:, k, cols(c)] if which == 2 else out32[:, 2 + i % 2, :]
                    if which < 2 and i >= 2:
                        dve.wait_ge(lo_done, NC * KT * which + i - 1)
                    dve.scalar_tensor_tensor(dst, res[:, k, cols(c)], g_sb[:, which, k:k + 1], rstd[:, cols(c)],
                                             ALU.mult, ALU.mult).then_inc(y_done, 1)
                    if which < 2 and i >= 1:
                        low(i - 1)
                if which < 2:
                    low(NC * KT - 1)

            dve.wait_ge(consts_in, 48)
            norm(0)
            dve.memset(neg8slope[:, :], -8.0 * SLOPE[0]).then_inc(key_used, 3)

            def low_part(j, hi, lo, src, wait):
                dve.wait_ge(part_hi, wait)
                dve.tensor_tensor(lo, src, f32(hi), ALU.subtract).then_inc(part_lo, 1)

            def keys(n):
                b, which = divmod(n, 3)
                if which < 2:
                    k_blk, ld = ((k_far, ld_far), (k_mid, ld_mid))[which]
                    dve.wait_ge(ld, 64 * b + 64)
                    dve.wait_ge(ld_qc, 16 * b + 16)
                    pr = prod[:, 0:1536].rearrange("p (j n) -> p j n", j=3)
                    kv = k_blk.rearrange("p (j n) -> p j n", j=3)
                    qv = qc.unsqueeze(1).broadcast_to([P, 3, DA])
                    dst, nj = s_cls[:, 3 * which:3 * which + 3, b, :], 3
                else:
                    dve.wait_ge(ld_near, 16 * b + 16)
                    dve.wait_ge(ld_qn, 16 * b + 16)
                    pr = prod.rearrange("p (j n) -> p j n", j=NT)
                    kv = k_near.unsqueeze(1).broadcast_to([P, NT, DA])
                    qv = qn.rearrange("p (j n) -> p j n", j=NT)
                    dst, nj = s_near[:, :, b, :], NT
                if n:
                    dve.wait_ge(key_sum, n)
                dve.tensor_tensor(pr, kv, qv, ALU.mult).then_inc(key_used, 1)
                dve.wait_ge(key_used, n + 4)
                dve.tensor_reduce(dst, prod[:, 0:nj * DA].rearrange("p (j h d) -> p j h d", j=nj, h=HEADS),
                                  AX.X, ALU.add).then_inc(key_sum, 1)

            his = 0
            for j in range(QK_JOBS + V_JOBS):
                dve.wait_ge(job_copied, j + 1)
                src, hl = out32[:, j % 2, :], out_hl[:, j % 2, :]
                if j < QK_JOBS:
                    n, c = divmod(j, NC)
                    if c == NC - 1:
                        keep, scale = (q_s, HD ** -0.5) if n < 4 else (k_s, 1.0)
                        dve.tensor_scalar(keep[:, n % 4, :], src[:, CH - SAMP:CH], scale, None,
                                          ALU.mult).then_inc(new_kept, 1)
                    hi, lo = hl[:, 0:CH], hl[:, CH:2 * CH]
                else:
                    vb, tt = divmod(j - QK_JOBS, VT)
                    src = src[:, 0:256].rearrange("p (h d) -> p h d", h=4)
                    parts = hl[:, 0:512].rearrange("p (h s d) -> p h s d", h=4, s=2)
                    hi, lo = parts[:, :, 0, :], parts[:, :, 1, :]
                if j >= QK_JOBS and tt == VT - 1:
                    dve.tensor_copy(v_s[:, 256 * vb:256 * vb + 256],
                                    out32[0:SAMP, j % 2, 0:256]).then_inc(part_lo, 1)
                else:
                    if parts_before(j):
                        dve.wait_ge(part_stored[j % 2], 16 * parts_before(j))
                    dve.tensor_copy(hi, src).then_inc(part_hi, 1)
                    his += 1
                    low_part(j, hi, lo, src, his)
                if j + 1 in KEYS_BEHIND:
                    keys(KEYS_BEHIND.index(j + 1))

            dve.wait_ge(made, 2)
            count_log(cnt_cls[:, :], age_cls[:, :], age_cls_i[:, :], cnt_i[:, 0:6], cnt_a[:, 0:6], cnt_b[:, 0:6], 1.0)
            count_log(cnt_near[:, :], age_near[:, :], age_near_i[:, :], cnt_i[:, 0:4], cnt_a[:, 0:4], cnt_b[:, 0:4], 1.0)
            count_log(cnt_self[:, :], age_self[:, :], age_self_i[:, :, :].rearrange("p t b -> p (t b)"),
                      cnt_i[0:SAMP, :], cnt_a[0:SAMP, :], cnt_b[0:SAMP, :], 1.0)
            dve.wait_ge(q_rows_out, 16)
            dve.memset(u_c[:, 0:2], 0.0).then_inc(conv_free, 1)

            def new_tokens_shift():
                dve.wait_ge(self_scores, 2)
                dve.wait_ge(key_sum, 3 * NB)
                for c in range(2):
                    dve.wait_ge(part_stored[c], 16 * PARTS_STORED[c])
                chain(dve.memset(p_cls5, 0.0))
                chain(dve.memset(p_rest, 0.0))
                chain(dve.tensor_copy(s_self[:, :, :, :].rearrange("p t b h -> p (t b h)"), ps[0:SAMP, 7, 0:256]))
                for s, age, cnt, n in ((s_cls, age_cls, cnt_cls, P), (s_near, age_near, cnt_near, P),
                                       (s_self, age_self, cnt_self, SAMP)):
                    a3 = age[:, :].unsqueeze(2) if s is not s_self else age[:, :].rearrange("p (t b) -> p t b", t=NT)
                    c3 = cnt[:, :].unsqueeze(2) if s is not s_self else cnt[:, :].rearrange("p (t b) -> p t b", t=NT)
                    for h in range(HEADS):
                        view = s[:, :, :, h]
                        shape = list(view.shape)
                        chain(dve.scalar_tensor_tensor(view, a3.broadcast_to(shape), -SLOPE[h], view, ALU.mult, ALU.add))
                    full = s[:, :, :, :]
                    chain(dve.tensor_tensor(full, full, c3.unsqueeze(3).broadcast_to(list(full.shape)), ALU.add))
                dve.tensor_reduce(top_cls[:, :], s_cls[:, :, :, :].rearrange("p j b h -> p (b h) j"), AX.X,
                                  ALU.max).then_inc(top_ready, 1)
                dve.wait_ge(new_pe, 1)
                for k, (bank, c0, n) in enumerate(((7, 0, 32), (6, 0, P), (7, P, SAMP))):
                    chain(dve.tensor_reduce(top_part[:, k, :], ps[0:64, bank, c0:c0 + NT * n].rearrange("p (t n) -> p t n", t=NT),
                                            AX.X, ALU.max))
                chain(dve.tensor_tensor(top_col[:, :], top_part[:, 0, :], top_part[:, 1, :], ALU.max))
                dve.tensor_tensor(top_col[:, :], top_col[:, :], top_part[:, 2, :], ALU.max).then_inc(top_ready, 1)
                dve.wait_ge(new_pe, 2)
                dve.tensor_tensor(top_diag[:, :, :], ps[0:NT, 7, 256:320].unsqueeze(1).broadcast_to([NT, NT, 64]),
                                  ident[0:NT, 0:NT].unsqueeze(2).broadcast_to([NT, NT, 64]), ALU.mult).then_inc(top_ready, 1)
                dve.wait_ge(new_pe, 3)
                near = s_near[:, :, :, :].rearrange("p t b h -> p (t b h)")
                own = s_self[:, :, :, :].rearrange("p t b h -> p (t b h)")
                chain(dve.tensor_tensor(near, near, ps[:, 6, 0:256], ALU.subtract))
                chain(dve.tensor_tensor(own, own, ps[0:SAMP, 6, 0:256], ALU.subtract))
                for t in range(NT):
                    q = slice(32 * t, 32 * t + 32)
                    v = s_cls[q, :, :, :].rearrange("p j b h -> p j (b h)")
                    ins = dve.tensor_tensor(v, v, ps[q, 6, 64 * t:64 * t + 64].unsqueeze(1).broadcast_to([32, 6, 64]),
                                            ALU.subtract)
                    if t < NT - 1:
                        chain(ins)
                ins.then_inc(shifted, 1)
            for p in range(4):
                if p < 3:
                    keys(KEYS_EARLY + 4 * p)
                    keys(KEYS_EARLY + 4 * p + 1)
                else:
                    new_tokens_shift()
                dve.wait_ge(job_copied, QK_JOBS + V_JOBS + 9 * p + 6)
                chain(dve.tensor_tensor(u_c[:, 2:2 + PROMPT], c_c[:, 0:PROMPT], h_c[:, 0:PROMPT], ALU.mult))
                chain(dve.tensor_tensor(u_s[:, :, 2:6], c_c[:, PROMPT:].rearrange("p (b t) -> p b t", b=NB),
                                        h_c[:, PROMPT:].rearrange("p (b t) -> p b t", b=NB), ALU.mult))
                chain(dve.tensor_copy(u_s[:, :, 0:2], cst_sb[:, p, :, :]))
                acc_s = acc_c[:, PROMPT:].rearrange("p (b t) -> p b t", b=NB)
                for k in range(3):
                    w_k = taps_sb[:, p, k:k + 1]
                    for acc, u in ((acc_c[:, 0:PROMPT], u_c[:, k:k + PROMPT]), (acc_s, u_s[:, :, k:k + NT])):
                        if k == 0:
                            chain(dve.tensor_scalar(acc, u, w_k, None, ALU.mult))
                        else:
                            chain(dve.scalar_tensor_tensor(acc, u, w_k, acc, ALU.mult, ALU.add))
                chain(dve.tensor_copy(tail_sb[:, p, 0:2], u_c[:, PROMPT:PROMPT + 2]))
                chain(dve.tensor_copy(tail_sb[:, p, 2:18].rearrange("p (b t) -> p b t", b=NB), u_s[:, :, 4:6]))
                if p < 3:
                    keys(KEYS_EARLY + 4 * p + 2)
                    keys(KEYS_EARLY + 4 * p + 3)
                dve.wait_ge(job_copied, QK_JOBS + V_JOBS + 9 * p + 9)
                chain(dve.tensor_tensor(y_c, acc_c, b_c, ALU.mult))
                chain(dve.tensor_copy(pair_hi[:, p, :], y_c))
                dve.tensor_tensor(pair_lo[:, p, :], y_c, f32(pair_hi[:, p, :]), ALU.subtract).then_inc(conv_free, 1)
            dve.wait_ge(conv_free, 5)

            dve.wait_ge(new_exp, 10)
            chain(dve.tensor_reduce(l_all, resid[:, 7168:8448].rearrange("p (j x) -> p x j", j=5), AX.X, ALU.add))
            chain(dve.tensor_tensor(l_all, l_all, spare[:, 0:256], ALU.add))
            chain(dve.tensor_tensor(l_all, l_all, spare[:, 256:512], ALU.add))
            dve.tensor_tensor(l_all[0:SAMP], l_all[0:SAMP], spare[0:SAMP, 512:768], ALU.add).then_inc(l_ready, 1)
            for c in range(2):
                dve.wait_ge(rows_stored[c], 16 * ROWS_STORED[c])
            tables = count_steps(count8, age_f, age_i[:, :], bias_h[1].bitcast(I16)[:, 0:1024], bias_h[0],
                                 out32[:, :, :].rearrange("p a t -> p (a t)")[:, 0:1024], 8.0)
            dve.wait_ge(new_pe, 4)
            chain(dve.reciprocal(sum_rec[:, :], ps[0:SAMP, 1, 0:NB]))
            for b in range(NB):
                dve.wait_ge(new_pv, b + 1)
                if b >= 1:
                    dve.wait_ge(new_turned, b)
                dve.scalar_tensor_tensor(o_b, ps[0:SAMP, 2 + b % 2, :], sum_rec[:, b:b + 1],
                                         head_mask[:, :, :].rearrange("p h d -> p (h d)"), ALU.mult,
                                         ALU.mult).then_inc(ob_done, 1)
                for _ in range(2):
                    next(tables, None)
            dve.wait_ge(new_turned, NB)
            dve.tensor_copy(o_s, ps[:, 0, 0:P]).then_inc(new_mixed, 1)
            dve.wait_ge(new_mixed, 1)
            o4 = o_s.rearrange("p (n t) -> p n t", n=4)
            chain(dve.tensor_copy(act_hi[:, 0:4, PROMPT:TOK], o4))
            dve.tensor_tensor(act_lo[:, 0:4, PROMPT:TOK], o4, f32(act_hi[:, 0:4, PROMPT:TOK]),
                              ALU.subtract).then_inc(new_mixed, 1)

            dve.wait_ge(new_mixed, 2)

            def head_bias(hh):
                chain(dve.scalar_tensor_tensor(bias_h[hh], age_f, neg8slope[:, 0:1], count8, ALU.mult, ALU.add))
                chain(dve.tensor_scalar(neg8slope[:, :], neg8slope[:, :], 0.5, None, ALU.mult))

            def reciprocals(it, s):
                it, back, s = lagged(it, s)
                dve.wait_ge(exped, 16 * it + s + 1 - 16 * back)
                dve.reciprocal(row_rec[:, s % 4:s % 4 + 1], row_sum[:, s % 4:s % 4 + 1]).then_inc(rec_done, 1)

            def biased_scores(it, s):
                hh, i = divmod(s, KT)
                n = P * (i + 1)
                dve.tensor_tensor_reduce(
                    prow[s % PROWS][:, 0:n],
                    ps[:, 2 * (s % 2):2 * (s % 2) + 2, :].rearrange("p a b -> p (a b)")[:, 0:n],
                    bias_h[hh][:, 896 - P * i:1024], -HD ** -0.5, 3e38, ALU.add, ALU.min,
                    row_neg[:, s % 4:s % 4 + 1]).then_inc(biased, 1)

            def normalise(it, s):
                it, back, s = lagged(it, s)
                n = P * (s % KT + 1)
                if s % KT >= POOL_TILE:
                    return
                dve.wait_ge(rec_done, 16 * it + s + 1 - 16 * back)
                dve.tensor_scalar(prow[s % PROWS][:, 0:n], prow[s % PROWS][:, 0:n], row_rec[:, s % 4:s % 4 + 1], None,
                                  ALU.mult).then_inc(normed, 1)

            def low_probs(it, s):
                it, back, s = lagged(it, s)
                u = s // 2
                for f, (fs, bank, k0, nk) in enumerate(FILLS):
                    if fs != s:
                        continue
                    dve.wait_ge(pt_hi_done, 24 * it + f + 1 - 24 * back)
                    qs = slice(P * (s % 2), P * (s % 2) + P)
                    dve.tensor_tensor(pts_lo[u % 2][:, k0:k0 + nk, qs],
                                      ps[:, bank, 0:P * nk].rearrange("p (k t) -> p k t", k=nk),
                                      f32(pts_hi[u % 2][:, k0:k0 + nk, qs]), ALU.subtract).then_inc(pt_lo_done, 1)

            def outputs(it, s):
                it, back, s = lagged(it, s)
                u = s // 2
                r = slice(HD * (u // 4), HD * (u // 4) + HD)
                if not (is_first(it, back) and u < 2):
                    dve.wait_ge(mix_lo, 8 * it + u - 1 - 8 * back)
                dve.wait_ge(low_done, 8 * it + u + 1 - 8 * back)
                dve.tensor_tensor(o32[u % 2][r], ps[0:HD, 7, 0:256], o_low[u % 2], ALU.add).then_inc(o_sum, 1)

            def mixed(it, s):
                it, back, s = lagged(it, s)
                u = s // 2
                r = slice(HD * (u // 4), HD * (u // 4) + HD)
                qs = slice(256 * (u % 4), 256 * (u % 4) + 256)
                dve.wait_ge(mix_hi, 8 * it + u + 1 - 8 * back)
                dve.tensor_tensor(act_lo[r, it - back, qs], o32[u % 2][r], f32(act_hi[r, it - back, qs]),
                                  ALU.subtract).then_inc(mix_lo, 1)

            def tick(it, s, first=False, last=False):
                if not last:
                    if s % KT == 0:
                        head_bias(s // KT)
                    dve.wait_ge(scored, 16 * it + s + 1)
                    if not (first and s < PROWS):
                        back = 1 if s < PROWS else 0
                        dve.wait_ge(turned, 24 * it + fills_through((s - PROWS) % 16) - 24 * back)
                if in_range(s - 1, first, last):
                    reciprocals(it, s - 1)
                if not last:
                    biased_scores(it, s)
                if in_range(s - 1, first, last):
                    normalise(it, s - 1)
                if in_range(s - HIGH_LAG, first, last):
                    low_probs(it, s - HIGH_LAG)
                if (s - MIX_LAG) % 2 == 1 and in_range(s - MIX_LAG, first, last):
                    mixed(it, s - MIX_LAG)
                if (s - VALUES_LAG) % 2 == 1 and in_range(s - VALUES_LAG, first, last):
                    outputs(it, s - VALUES_LAG)

            for s in range(16):
                tick(0, s, first=True)
            with dve.Fori(1, 4) as it:
                start = chain.loop(it - 1, HEAD_CHAIN, 3)
                for s in range(16):
                    tick(it, s)
                chain.end(start)
            for s in range(LAST_TICKS):
                tick(4, s, last=True)

            def stream(which, job0):
                def add_squares(j):
                    n, c = divmod(j, NC)
                    dve.wait_ge(h_sq, NC * KT * which + j + 1)
                    if n == 0:
                        dve.tensor_copy(ssum[:, cols(c)], sq[n % 2][:, cols(c)]).then_inc(h_ss, 1)
                    else:
                        dve.wait_ge(h_ss, NC * KT * which + j - 2)
                        dve.tensor_tensor(ssum[:, cols(c)], ssum[:, cols(c)], sq[n % 2][:, cols(c)],
                                          ALU.add).then_inc(h_ss, 1)

                for j in range(NC * KT):
                    n, c = divmod(j, NC)
                    dve.wait_ge(job_done, job0 + j + 1)
                    if which == 0:
                        dve.wait_ge(x2_in[n], 16)
                        bank = 3 * (n % 2) + c
                    else:
                        bank = 6 + j % 2
                    dve.tensor_tensor(res[:, n, cols(c)], ps[:, bank, 0:CH], res[:, n, cols(c)],
                                      ALU.add).then_inc(h_done, 1)
                    if j >= 1:
                        add_squares(j - 1)
                add_squares(NC * KT - 1)

            stream(0, OUT_JOB0)
            norm(1)

            def hidden_of(it, g, first=False):
                job = OUT_JOB0 + 24 + 6 if first else 72 * it + FFN_JOB0 + 36 * g + 6

                def low(i):
                    f, c = divmod(i, NC)
                    dve.wait_ge(hid_hi, 12 * it + 6 * g + i + 1)
                    dve.tensor_tensor(pair_lo[:, 2 * (g % 2) + f, cols(c)], silu[:, f, cols(c)],
                                      f32(pair_hi[:, 2 * (g % 2) + f, cols(c)]), ALU.subtract).then_inc(hid_lo, 1)

                for i in range(6):
                    f, c = divmod(i, NC)
                    dve.wait_ge(job_done, job + i + 1)
                    dve.wait_ge(silu_done, 12 * it + 6 * g + i + 1)
                    dve.tensor_tensor(silu[:, f, cols(c)], ps[:, 3 * f + c, 0:CH], silu[:, f, cols(c)],
                                      ALU.mult).then_inc(hidden, 1)
                    if i >= 1:
                        low(i - 1)
                low(5)

            hidden_of(0, 0, first=True)
            with dve.Fori(0, 5) as it:
                for g in (1, 2):
                    hidden_of(it, g)
                    for i in range(NC * KT):
                        n, c = divmod(i, NC)
                        dve.wait_ge(job_done, 72 * it + FFN_JOB0 + 36 * g + 12 + i + 1)
                        dve.tensor_tensor(res[:, n, cols(c)], ps[:, 6 + i % 2, 0:CH], res[:, n, cols(c)],
                                          ALU.add).then_inc(added, 1)
            stream(1, LAST_JOB0)
            norm(2)


class Chain:

    def __init__(self, eng, sem):
        self.eng, self.sem, self.base, self.n = eng, sem, 0, 0

    def __call__(self, ins):
        ins.then_inc(self.sem, 1)
        self.n += 1
        self.eng.wait_ge(self.sem, self.base + self.n)

    def loop(self, it, per, turns):
        self.base, self.per, self.turns = it * per, per, turns
        return self.n

    def end(self, start):
        assert self.n - start == self.per, (self.n - start, self.per)
        self.base, self.n = 0, start + self.per * self.turns


Q_ROWS_JOB = 13
KEYS_EARLY = 12
KEYS_BEHIND = [18 + 2 * n for n in range(KEYS_EARLY)]
MAXIMA_BEHIND = [4, 5, 6]
HEAD_CHAIN = 2 * 2
TURN_LAG, HIGH_LAG, VALUES_LAG, MIX_LAG = 3, 2, 4, 5
LAST_TICKS = MIX_LAG + 1
POOL_TILE = 3
OUT_JOB0 = IN_JOBS
FFN_JOB0 = OUT_JOB0 + 24 + 12 - 36
LAST_JOB0 = OUT_JOB0 + 24 + 12 + 36 * (GROUPS - 1)


def jobs_through(u):
    if u < QK_UNITS:
        return NC * (u + 1)
    if u < CONV0:
        return QK_JOBS + VT * ((u - QK_UNITS) // 2 + 1)
    if u < OUT0:
        return QK_JOBS + V_JOBS + NC * (u - CONV0 + 1)
    if u < FFN0 + 4:
        return IN_JOBS + NC * (u - OUT0 + 1)
    g, s = divmod(u - FFN0 - 4, 6)
    base = OUT_JOB0 + 24 + 12 + 36 * g
    return base + (NC * (s + 1) if s < 4 else 36)


def parts_before(j):
    return sum(1 for i in range(j % 2, j, 2) if not (i >= QK_JOBS and (i - QK_JOBS) % VT == VT - 1))


def rows_before(j):
    return sum(1 for i in range(j % 2, j, 2) if i >= QK_JOBS // 2)


PARTS_STORED = [parts_before(QK_JOBS + V_JOBS), parts_before(QK_JOBS + V_JOBS + 1)]
ROWS_STORED = [rows_before(QK_JOBS + V_JOBS), rows_before(QK_JOBS + V_JOBS + 1)]


def fills():
    out = []
    for s in range(2 * KT):
        i = s % KT
        if i < 4:
            out.append((s, 0, i + 1))
        else:
            out += [(s, 0, 4), (s, 4, i - 3)]
    return [(s, 4 + f % 3, k0, n) for f, (s, k0, n) in enumerate(out)]


FILLS = fills()


def lagged(it, s):
    return it, (1 if s < 0 else 0), s % 16


def is_first(it, back):
    return isinstance(it, int) and it - back == 0


def in_range(s, first, last):
    return s >= 0 if first else s < 0 if last else True


def norms_through(s):
    return sum(1 for i in range(s + 1) if (i % KT >= POOL_TILE) == (s % KT >= POOL_TILE))


def fills_through(s):
    return sum(1 for f in FILLS if f[0] <= s)


def score_blocks(i):
    n = P * (i + 1)
    return [(0, max(256, n))] if n <= 512 else [(0, 512), (1, max(256, n - 512))]


def weight_units(w_in, w_out, w_gate, w_up, w_down):
    def tile(w, c):
        return w[:, c:c + P].reshape(KT, P, P).transpose(1, 0, 2).reshape(P, 1024)

    def wide(w, c, half):
        return w[512 * half:512 * half + 512, c:c + 256].reshape(4, P, 256).transpose(1, 0, 2).reshape(P, 1024)

    def gates(g):
        return [tile(w_gate, 256 * g), tile(w_gate, 256 * g + P), tile(w_up, 256 * g), tile(w_up, 256 * g + P)]

    def downs(g):
        return [w_down[256 * g + P * f:256 * g + P * f + P, :] for f in range(2)]

    units = [tile(w_in, P * n) for n in range(8)]
    units += [wide(w_in, 2 * DA + 256 * vb, half) for vb in range(2) for half in range(2)]
    for p in range(4):
        units += [tile(w_in, 3 * DA + off + P * p) for off in (0, 2 * (D - DA), D - DA)]
    units += [tile(w_out, P * n) for n in range(KT)]
    units += gates(0)
    for g in range(1, GROUPS):
        units += gates(g) + downs(g - 1)
    units += downs(GROUPS - 1)
    return np.ascontiguousarray(np.stack(units))


def kernel(x_prompt, x_sample, state_attn_k, state_attn_v, state_conv, norm_mix_g, w_in, w_conv, w_out,
           norm_ffn_g, w_gate, w_up, w_down, norm_final_g):
    import concourse.bacc as bacc
    from concourse.bass_utils import run_bass_kernel_spmd

    a = np.ascontiguousarray
    x = np.concatenate([np.asarray(x_prompt)[0], np.asarray(x_sample).reshape(SAMP, D)])
    by_channel = lambda v: np.asarray(v).reshape(KT, P).T
    arrays = {
        "xT": a(x.T.reshape(KT, P, TOK).transpose(1, 0, 2)),
        "w": weight_units(*(np.asarray(m)[0] for m in (w_in, w_out, w_gate, w_up, w_down))),
        "gains": a(np.stack([by_channel(np.asarray(norm_mix_g)[0]), by_channel(np.asarray(norm_ffn_g)[0]),
                             by_channel(norm_final_g)], axis=1)),
        "taps": a(np.asarray(w_conv)[0].reshape(3, 4, P).transpose(2, 1, 0)),
        "conv_state": a(np.asarray(state_conv)[0].reshape(NB, 2, 4, P).transpose(3, 2, 0, 1)),
        "state_k": a(np.asarray(state_attn_k)[0].reshape(NB, PAST, DA)),
        "state_v": a(np.asarray(state_attn_v)[0].reshape(NB, PAST, DA)),
    }
    outs = {"yT": (P, KT, TOK), "kT": (4, P, TOK), "v": (TOK, DA), "conv_tail": (P, 4, 18)}
    nc = bacc.Bacc("TRN2", target_bir_lowering=False, num_devices=1, dynamic_dma_scratch_size=1024)
    args = [nc.dram_tensor(f"in_{n}", v.shape, F32, kind="ExternalInput").ap() for n, v in arrays.items()]
    args += [nc.dram_tensor(f"out_{n}", s, F32, kind="ExternalOutput").ap() for n, s in outs.items()]
    build(nc, *args)
    got = run_bass_kernel_spmd(nc, [{f"in_{n}": v for n, v in arrays.items()}], core_ids=[0]).results[0]
    y, k, v, tail = (np.asarray(got[f"out_{n}"]) for n in outs)

    y = y.transpose(2, 1, 0).reshape(TOK, D)
    k = k.transpose(2, 0, 1).reshape(TOK, HEADS, HD)
    v = v.reshape(TOK, HEADS, HD)
    tail = tail.transpose(2, 1, 0).reshape(18, D - DA)
    return (a(y[:PROMPT])[None], a(y[PROMPT:]).reshape(NB, NT, D),
            a(k[:PROMPT])[None, None], a(v[:PROMPT])[None, None], a(tail[:2])[None, None],
            a(k[PROMPT:]).reshape(1, NB, NT, HEADS, HD), a(v[PROMPT:]).reshape(1, NB, NT, HEADS, HD),
            a(tail[2:]).reshape(1, NB, 2, D - DA))
```

```python
from contextlib import ExitStack

import numpy as np

import concourse.bass as bass
from concourse import mybir

F32 = mybir.dt.float32
F32R = mybir.dt.float32r
I32 = mybir.dt.int32
I16 = mybir.dt.int16
ALU = mybir.AluOpType
ACT = mybir.ActivationFunctionType
AX = mybir.AxisListType

P = 128
D = 1024
KT = D // P
PROMPT = 1024
NB, NT = 8, 4
SAMP = NB * NT
TOK = PROMPT + SAMP
NC = 3
CH = TOK // NC
HEADS, HD = 8, 64
DA = HEADS * HD
PAST = 2048
FF = 2816
GROUPS = FF // (2 * P)
EPS = 1e-6
LN2, LN3 = float(np.log(2.0)), float(np.log(3.0))
MASKED = -1e30
SLOPE = [2.0 ** -(h + 1) for h in range(HEADS)]

QK_UNITS, V_UNITS, CONV_UNITS, OUT_UNITS, FFN_UNITS = 8, 4, 12, 8, 6 * GROUPS
UNITS = QK_UNITS + V_UNITS + CONV_UNITS + OUT_UNITS + FFN_UNITS
CONV0 = QK_UNITS + V_UNITS
OUT0 = CONV0 + CONV_UNITS
FFN0 = OUT0 + OUT_UNITS
RING = 3
STAGE = 2
PROWS = 4

QK_JOBS = QK_UNITS * NC
VT = PROMPT // P + 1
V_JOBS = 2 * VT
CONV_JOBS = CONV_UNITS * NC
IN_JOBS = QK_JOBS + V_JOBS + CONV_JOBS


def f32(ap):
    return ap.bitcast(F32)


def build(nc, xT, w, gains, taps, conv_state, state_k, state_v, yT, kT, v_out, conv_tail):
    with ExitStack() as ctx:
        def sb(name, shape, dt=F32):
            return ctx.enter_context(nc.sbuf_tensor(name, shape, dt))

        def sem(name):
            return ctx.enter_context(nc.semaphore(name))

        act_hi = sb("act_hi", [P, KT, TOK], F32R)
        act_lo = sb("act_lo", [P, KT, TOK], F32R)
        pair_hi = sb("pair_hi", [P, 4, TOK], F32R)
        pair_lo = sb("pair_lo", [P, 4, TOK], F32R)
        w_stage = sb("w_stage", [P, STAGE, 1024])
        w_hi = sb("w_hi", [P, RING, 1024], F32R)
        w_lo = sb("w_lo", [P, RING, 1024], F32R)
        resid = sb("resid", [P, KT * TOK])
        res = resid[:, :].rearrange("p (k t) -> p k t", k=KT)
        pt_hi = sb("pt_hi", [P, KT, 256], F32R)
        pt_lo = sb("pt_lo", [P, KT, 256], F32R)
        out32 = sb("out32", [P, 4, CH])
        out_hl = sb("out_hl", [P, 2, 2 * CH], F32R)
        work = sb("work", [P, 4300])
        age_i = sb("age_i", [P, 1024], I16)
        ident = sb("ident", [P, P])
        ones = sb("ones", [P, P])
        g_sb = sb("g_sb", [P, 3, KT])
        taps_sb = sb("taps_sb", [P, 4, 3])
        cst_sb = sb("cst_sb", [P, 4, NB, 2])
        tail_sb = sb("tail_sb", [P, 4, 18])
        neg8slope = sb("neg8slope", [P, 1])
        gate_cell = sb("gate_cell", [P, 2])
        row_neg, row_sum, row_rec = (sb(n, [P, 4]) for n in ("row_neg", "row_sum", "row_rec"))
        q_s = sb("q_s", [P, 4, SAMP])
        k_s = sb("k_s", [P, 4, SAMP])
        v_s = sb("v_s", [SAMP, DA])
        s_cls = sb("s_cls", [P, 6, NB, HEADS])
        s_near = sb("s_near", [P, NT, NB, HEADS])
        s_self = sb("s_self", [SAMP, NT, NB, HEADS])
        age_cls_i, age_near_i = sb("age_cls_i", [P, 6], I32), sb("age_near_i", [P, NT], I32)
        age_self_i = sb("age_self_i", [SAMP, NT, NB], I32)
        age_cls, age_near, age_self = sb("age_cls", [P, 6]), sb("age_near", [P, NT]), sb("age_self", [SAMP, NT * NB])
        cnt_cls, cnt_near, cnt_self = sb("cnt_cls", [P, 6]), sb("cnt_near", [P, NT]), sb("cnt_self", [SAMP, NT * NB])
        cnt_i, cnt_a, cnt_b = sb("cnt_i", [P, 32], I32), sb("cnt_a", [P, 32]), sb("cnt_b", [P, 32])
        top_cls = sb("top_cls", [P, NB * HEADS])
        top_part = sb("top_part", [NB * HEADS, 3, NT])
        top_col = sb("top_col", [NB * HEADS, NT])
        top_diag = sb("top_diag", [NT, NT, NB * HEADS])
        sum_rec = sb("sum_rec", [SAMP, NB])
        head_mask = sb("head_mask", [SAMP, HEADS, HD])
        sel_t = sb("sel_t", [SAMP, NT])

        rstd = work[:, 0:TOK]
        ssum = work[:, TOK:2 * TOK]
        sq = [work[:, 2112:2112 + TOK], work[:, 3168:3168 + TOK]]
        sq6 = [sq[i // NC][:, CH * (i % NC):CH * (i % NC) + CH] for i in range(6)]
        last_hi, last_lo = (t[:, 0:4, :].rearrange("p k t -> p (k t)") for t in (pt_hi, pt_lo))
        silu = work[:, 2112:2112 + 2 * TOK].rearrange("p (f t) -> p f t", f=2)
        q_rows = work[0:SAMP, 3168:3168 + DA]
        h_c = acc_c = work[:, 0:TOK]
        c_c = y_c = work[:, TOK:2 * TOK]
        b_c = work[:, 2 * TOK:3 * TOK]
        u_c = work[:, 3 * TOK:3 * TOK + 2 + PROMPT + 6 * NB]
        u_s = u_c[:, 2 + PROMPT:].rearrange("p (b t) -> p b t", b=NB)
        count8 = work[:, 0:1024]
        bias_h = [work[:, 1024:2048], work[:, 2048:3072]]
        age_f = work[:, 3072:4096]
        p_cls5 = resid[:, 7168:8448].rearrange("p (j b t h) -> p j b t h", j=5, b=NB, t=NT)
        spare = f32(out_hl[:, :, :]).rearrange("p a t -> p (a t)")
        p_rest, p_near, p_self = [spare[:, 256 * i:256 * i + 256].rearrange("p (b t h) -> p b t h", b=NB, t=NT)
                                  for i in range(3)]
        p_self = p_self[0:SAMP]
        l_all = spare[:, 768:1024]
        o_b = work[0:SAMP, 2560:3072]
        o_s = work[:, 4096:4096 + P]
        qc = resid[:, 0:512]
        qn = resid[:, 512:2560]
        k_far = resid[:, 2560:4096]
        k_mid = resid[:, 4096:5632]
        k_near = resid[:, 5632:6144]
        prod = resid[:, 6144:8192]
        v_tiles = [resid[:, 3584 * i:3584 * (i + 1)].rearrange("p (j n) -> p j n", j=7) for i in range(2)]
        prow = [resid[:, 1024 * i:1024 * (i + 1)] for i in range(PROWS)]
        pts_hi, pts_lo = ([t, w[:, 1:3, :].rearrange("p u x -> p (u x)").rearrange("p (k t) -> p k t", k=KT)]
                          for t, w in ((pt_hi, w_hi), (pt_lo, w_lo)))
        o_low = [out32[0:HD, i, 0:256] for i in range(2)]
        o32 = [out32[:, 2 + i, 0:256] for i in range(2)]
        stack = [a[:, 4:8, :].rearrange("p k t -> p (k t)") for a in (act_hi, act_lo)]
        st_q = [s[:, 0:1024] for s in stack]
        st_khi = [s[:, 1024:2048] for s in stack]
        st_klo = [s[:, 2048:3072] for s in stack]
        st_v = [s[:, 3072:4096].rearrange("p (k e) -> p k e", k=KT) for s in stack]

        ps = ctx.enter_context(nc.psum_tensor("ps", [P, 8, 512], F32))

        qk_d = nc.dram_tensor("qk_d", [8, P, 2, TOK], F32).ap()
        v_d = nc.dram_tensor("v_d", [HEADS, P, KT, P], F32).ap()
        q_rows_d = nc.dram_tensor("q_rows_d", [SAMP, DA], F32).ap()

        consts_in = sem("consts_in")
        x_in = [sem(f"x_in{k}") for k in range(KT)]
        w_in = [sem(f"w_in{i}") for i in range(STAGE)]
        part_stored = [sem("part_stored0"), sem("part_stored1")]
        rows_stored = [sem("rows_stored0"), sem("rows_stored1")]
        q_rows_out, ld_qc, ld_qn = sem("q_rows_out"), sem("ld_qc"), sem("ld_qn")
        ld_far, ld_mid, ld_near = sem("ld_far"), sem("ld_mid"), sem("ld_near")
        v_ld = [sem("v_ld0"), sem("v_ld1")]
        st_in = [sem("st_in0"), sem("st_in1")]
        x2_in = [sem(f"x2_in{k}") for k in range(KT)]
        y_out = sem("y_out")
        made = sem("made")
        w_split = sem("w_split")
        pool_chain = sem("pool_chain")
        pool_lo = sem("pool_lo")
        pool_normed, last_ss = sem("pool_normed"), sem("last_ss")
        ss_done, ss_all = sem("ss_done"), sem("ss_all")
        job_done = sem("job_done")
        q_turned, self_scores = sem("q_turned"), sem("self_scores")
        new_pe, new_pv, new_turned = sem("new_pe"), sem("new_pv"), sem("new_turned")
        scored, turned, pv_done = sem("scored"), sem("turned"), sem("pv_done")
        sq_done, root, hi_done = sem("sq_done"), sem("root"), sem("hi_done")
        job_copied, q_rows_done = sem("job_copied"), sem("q_rows_done")
        new_exp = sem("new_exp")
        exped, pt_hi_done, low_done, mix_hi = sem("exped"), sem("pt_hi_done"), sem("low_done"), sem("mix_hi")
        h_sq, silu_done, hid_hi = sem("h_sq"), sem("silu_done"), sem("hid_hi")
        dve_chain = sem("dve_chain")
        mean_sq, y_done, lo_done = sem("mean_sq"), sem("y_done"), sem("lo_done")
        part_hi, part_lo, new_kept = sem("part_hi"), sem("part_lo"), sem("new_kept")
        conv_free = sem("conv_free")
        key_used, key_sum = sem("key_used"), sem("key_sum")
        top_ready, shifted, l_ready = sem("top_ready"), sem("shifted"), sem("l_ready")
        ob_done, new_mixed = sem("ob_done"), sem("new_mixed")
        biased, rec_done, normed = sem("biased"), sem("rec_done"), sem("normed")
        pt_lo_done, o_sum, mix_lo = sem("pt_lo_done"), sem("o_sum"), sem("mix_lo")
        h_done, h_ss = sem("h_done"), sem("h_ss")
        hidden, hid_lo, added = sem("hidden"), sem("hid_lo"), sem("added")

        block = ctx.enter_context(nc.Block())

        def norm_slot(which, i):
            return sq6[i % 6] if which == 0 else out32[:, 2 + i % 2, :]

        def cols(c):
            return slice(CH * c, CH * (c + 1))

        @block.sync
        def _(sp):
            def unit(u, slot=None):
                if slot is not None or u >= STAGE:
                    sp.wait_ge(w_split, 2 * (u - STAGE) + 2)
                s = u % STAGE if slot is None else slot
                sp.dma_start(w_stage[:, s, :], w[u]).then_inc(w_in[s], 16)

            unit(0)
            sp.dma_start(g_sb[:, :, :], gains).then_inc(consts_in, 16)
            sp.dma_start(taps_sb[:, :, :], taps).then_inc(consts_in, 16)
            sp.dma_start(cst_sb[:, :, :, :], conv_state).then_inc(consts_in, 16)
            for k in range(KT):
                sp.dma_start(res[:, k, :], xT[:, k, :]).then_inc(x_in[k], 16)
            for u in range(1, 4):
                unit(u)

            def load_queries(n):
                b, which = divmod(n, 3)
                if which == 1:
                    sp.dma_start(qc, q_rows_d.rearrange("(b t) n -> b t n", b=NB)[b].unsqueeze(1)
                                 .broadcast_to([NT, 32, DA])).then_inc(ld_qc, 16)
                elif which == 2:
                    sp.dma_start(qn, q_rows_d.rearrange("(b t) n -> b (t n)", b=NB)[b].unsqueeze(0)
                                 .broadcast_to([P, NT * DA])).then_inc(ld_qn, 16)

            def load_keys(n):
                b, which = divmod(n, 3)
                if n >= 3:
                    sp.wait_ge(key_used, n + 1)
                else:
                    sp.wait_ge(key_used, 3)
                if which == 0:
                    far = state_k[b, 0:1536].rearrange("(i j r) n -> r i j n", i=32, j=3)
                    for t in range(NT):
                        sp.dma_start(k_far[32 * t:32 * t + 32].rearrange("p (j n) -> p j n", j=3),
                                     far[t]).then_inc(ld_far, 16)
                elif which == 1:
                    mid = state_k[b, 1536:1920].rearrange("(i j r) n -> r i j n", i=32, j=3)
                    for t in range(NT):
                        sp.dma_start(k_mid[32 * t:32 * t + 32].rearrange("p (j n) -> p j n", j=3),
                                     mid[t]).then_inc(ld_mid, 16)
                else:
                    sp.dma_start(k_near, state_k[b, 1920:2048]).then_inc(ld_near, 16)

            for u in range(QK_UNITS):
                for j in range(NC * u, NC * u + NC):
                    n, c = QK_ORDER[j]
                    sp.wait_ge(part_lo, j + 1)
                    sp.dma_start(qk_d[n, :, :, cols(c)],
                                 f32(out_hl[:, j % 2, :]).rearrange("p (s t) -> p s t", s=2)
                                 ).then_inc(part_stored[j % 2], 16)
                    if n >= 4:
                        sp.dma_start(kT[n - 4, :, cols(c)], out32[:, j % 2, :]).then_inc(rows_stored[j % 2], 16)
                    if j == Q_ROWS_JOB:
                        sp.wait_ge(q_rows_done, 1)
                        sp.dma_start(q_rows_d, q_rows).then_inc(q_rows_out, 16)
                        sp.wait_ge(q_rows_out, 16)
                        for m in range(3):
                            load_queries(m)
                    if j in FIRST_KEYS_BEHIND:
                        load_keys(FIRST_KEYS_BEHIND.index(j))
                    if j in KEYS_BEHIND:
                        load_keys(KEYS_BEHIND.index(j) + 3)
                        load_queries(KEYS_BEHIND.index(j) + 3)
                unit(u + 4)

            for i in range(V_JOBS):
                j, vb, tt = QK_JOBS + i, i // VT, i % VT
                m = P if tt < VT - 1 else SAMP
                sp.wait_ge(part_lo, j + 1)
                if tt < VT - 1:
                    sp.dma_start(v_d[4 * vb:4 * vb + 4, :, tt, :].rearrange("h p e -> p h e"),
                                 f32(out_hl[:, j % 2, 0:512]).rearrange("p (h e) -> p h e", h=4)
                                 ).then_inc(part_stored[j % 2], 16)
                sp.dma_start(v_out[tt * P:tt * P + m, 256 * vb:256 * vb + 256],
                             out32[0:m, j % 2, 0:256]).then_inc(rows_stored[j % 2], 16)
                if i == 6:
                    unit(12)
                if tt == VT - 1:
                    unit(13 + vb)
                if j in KEYS_BEHIND:
                    load_keys(KEYS_BEHIND.index(j) + 3)
                    load_queries(KEYS_BEHIND.index(j) + 3)
            unit(15)

            for p in range(4):
                for n in range(4):
                    if p < 3 and KEYS_EARLY + 4 * p + n + 3 < 3 * NB:
                        load_keys(KEYS_EARLY + 4 * p + n + 3)
                        load_queries(KEYS_EARLY + 4 * p + n + 3)
                    if n < 3 and 16 + 3 * p + n < OUT0 + 1 + STAGE:
                        unit(16 + 3 * p + n)

            sp.wait_ge(key_sum, 3 * NB)
            for b in range(NB):
                vt, ld = v_tiles[b % 2], v_ld[b % 2]
                far = state_v[b, 0:1536].rearrange("(i j r) n -> r i j n", i=32, j=3)
                mid = state_v[b, 1536:1920].rearrange("(i j r) n -> r i j n", i=32, j=3)
                if b >= 2:
                    sp.wait_ge(new_pv, b - 1)
                for t in range(NT):
                    sp.dma_start(vt[32 * t:32 * t + 32, 0:3, :], far[t]).then_inc(ld, 16)
                    sp.dma_start(vt[32 * t:32 * t + 32, 3:6, :], mid[t]).then_inc(ld, 16)
                sp.dma_start(vt[:, 6, :], state_v[b, 1920:2048]).then_inc(ld, 16)

            def load_head(hh, tile):
                r = slice(HD * hh, HD * hh + HD)
                s = st_in[hh]
                for half in range(2):
                    d = slice(HD * half, HD * half + HD)
                    sp.dma_start(f32(st_q[hh][d]), qk_d[tile, r, half, 0:PROMPT]).then_inc(s, 16)
                    sp.dma_start(f32(st_khi[hh][d]), qk_d[4 + tile, r, 0, 0:PROMPT]).then_inc(s, 16)
                    sp.dma_start(f32(st_klo[hh][d]), qk_d[4 + tile, r, 1, 0:PROMPT]).then_inc(s, 16)
                sp.dma_start(f32(st_v[hh]), v_d[2 * tile + hh]).then_inc(s, 16)

            for s in range(2):
                sp.wait_ge(part_stored[s], 16 * PARTS_STORED[s])
            sp.wait_ge(job_done, IN_JOBS)
            load_head(0, 0)
            load_head(1, 0)
            with sp.Fori(0, 3) as it:
                for hh in range(2):
                    sp.wait_ge(pv_done, 8 * it + 4 * hh + 4)
                    load_head(hh, it + 1)

            sp.wait_ge(mix_lo, 4 * HEADS)
            for k in range(KT):
                sp.dma_start(res[:, k, :], xT[:, k, :]).then_inc(x2_in[k], 16)
            for u in range(OUT0 + 1 + STAGE, 37):
                unit(u)
            with sp.Fori(0, 10) as it:
                for s in range(6):
                    unit(6 * it + 37 + s, (37 + s) % STAGE)
            unit(97)

            for i in range(NC * KT):
                c, k = divmod(i, KT)
                sp.wait_ge(y_done, 2 * NC * KT + i + 1)
                sp.dma_start(yT[:, k, cols(c)], res[:, k, cols(c)]).then_inc(y_out, 16)
            sp.wait_ge(conv_free, 5)
            sp.dma_start(conv_tail, tail_sb[:, :, :]).then_inc(y_out, 16)
            sp.wait_ge(y_out, 16 * (NC * KT + 1))
            for s in range(2):
                sp.wait_ge(rows_stored[s], 16 * ROWS_STORED[s])

        @block.gpsimd
        def _(pool):
            chain = Chain(pool, pool_chain)
            chain(pool.memset(ident[:, :], 0.0))
            pool.memset(ones[:, :], 1.0).then_inc(made, 1)
            chain(pool.affine_select(out=ident[:, :], in_=ident[:, :], compare_op=ALU.not_equal, fill=1.0,
                                     base=0, pattern=[[-1, P]], channel_multiplier=1))

            def split(u, slot, stage, arrived, released, hi=None, lo=None):
                pool.wait_ge(w_in[stage], arrived)
                if released is not None:
                    pool.wait_ge(job_done, released)
                    pool.tensor_tensor(gate_cell[:, 0:1], ones[:, 0:1], ones[:, 0:1], ALU.mult)
                hi, lo = (w_hi[:, slot, :], w_lo[:, slot, :]) if hi is None else (hi, lo)
                pool.tensor_copy(hi, w_stage[:, stage, :]).then_inc(w_split, 1)
                pool.wait_ge(w_split, 2 * u + 1)
                pool.tensor_tensor(lo, w_stage[:, stage, :], f32(hi), ALU.subtract).then_inc(w_split, 1)

            def straight(u):
                if u in (CONV0 - 1, UNITS - 1):
                    split(u, None, u % STAGE, 16 * (u // STAGE + 1), None, last_hi, last_lo)
                    return
                split(u, u % RING, u % STAGE, 16 * (u // STAGE + 1), jobs_through(u - RING) if u >= RING else None)

            straight(0)
            chain(pool.iota(age_i[:, :], pattern=[[-1, 1024]], base=896, channel_multiplier=1))
            for t in range(NT):
                q = slice(32 * t, 32 * t + 32)
                chain(pool.iota(age_cls_i[q, 0:3], pattern=[[-16, 3]], base=2048, channel_multiplier=-48))
                chain(pool.iota(age_cls_i[q, 3:6], pattern=[[-4, 3]], base=512, channel_multiplier=-12))
            chain(pool.iota(age_near_i[:, :], pattern=[[1, NT]], base=128, channel_multiplier=-1))
            chain(pool.iota(age_self_i[:, :, :], pattern=[[1, NT], [4, NB]], base=0, channel_multiplier=-1))
            chain(pool.affine_select(out=age_self_i[:, :, :], in_=age_self_i[:, :, :], compare_op=ALU.is_ge,
                                     fill=-1.0, base=0, pattern=[[0, NT], [-4, NB]], channel_multiplier=1))
            chain(pool.affine_select(out=age_self_i[:, :, :], in_=age_self_i[:, :, :], compare_op=ALU.is_ge,
                                     fill=-1.0, base=3, pattern=[[0, NT], [4, NB]], channel_multiplier=-1))
            chain(pool.memset(head_mask[:, :, :], 0.0))
            for t in range(NT):
                chain(pool.affine_select(out=head_mask[:, :, :], in_=head_mask[:, :, :],
                                         compare_op=ALU.not_equal, fill=1.0, base=-8 * t,
                                         pattern=[[-1, HEADS], [0, HD]], channel_multiplier=1))
            chain(pool.memset(sel_t[:, :], 1.0))
            chain(pool.affine_select(out=sel_t[:, :], in_=sel_t[:, :], compare_op=ALU.is_ge, fill=0.0,
                                     base=0, pattern=[[-8, NT]], channel_multiplier=1))
            pool.affine_select(out=sel_t[:, :], in_=sel_t[:, :], compare_op=ALU.is_ge, fill=0.0,
                               base=7, pattern=[[8, NT]], channel_multiplier=-1).then_inc(made, 1)

            straight(1)
            straight(2)
            for i in range(1, NC * KT, 2):
                c, k = divmod(i, KT)
                pool.wait_ge(hi_done, i + 1)
                pool.tensor_tensor(act_lo[:, k, cols(c)], norm_slot(0, i), f32(act_hi[:, k, cols(c)]),
                                   ALU.subtract).then_inc(pool_lo, 1)
            for u in range(3, OUT0 + 1):
                straight(u)

            def normalise(it, s):
                it, back, s = lagged(it, s)
                n = P * (s % KT + 1)
                if s % KT >= POOL_TILE:
                    pool.wait_ge(rec_done, 16 * it + s + 1 - 16 * back)
                    pool.tensor_tensor(prow[s % PROWS][:, 0:n], prow[s % PROWS][:, 0:n],
                                       row_rec[:, s % 4:s % 4 + 1].broadcast_to([P, n]),
                                       ALU.mult).then_inc(pool_normed, 1)

            def tick(it, s, first=False, last=False):
                if in_range(s - 1, first, last):
                    normalise(it, s - 1)

            for s in range(16):
                tick(0, s, first=True)
            with pool.Fori(1, 4) as it:
                for s in range(16):
                    tick(it, s)
            tick(4, 0, last=True)

            pool.wait_ge(pv_done, 4 * HEADS)
            for u in range(OUT0 + 1, FFN0 + 16):
                straight(u)
            with pool.Fori(0, 4) as it:
                for s in range(12):
                    u = FFN0 + 16 + s
                    split(12 * it + u, u % RING, u % STAGE, 96 * it + 16 * (u // STAGE + 1),
                          72 * it + jobs_through(u - RING))
            straight(UNITS - 2)
            straight(UNITS - 1)

            for j, (n, c) in enumerate(LAST_ORDER):
                pool.wait_ge(h_sq, NC * KT + j + 1)
                if n == 0:
                    pool.tensor_copy(ssum[:, cols(c)], sq6[j % 6]).then_inc(last_ss, 1)
                else:
                    pool.wait_ge(last_ss, j)
                    pool.tensor_tensor(ssum[:, cols(c)], ssum[:, cols(c)], sq6[j % 6], ALU.add).then_inc(last_ss, 1)

        @block.tensor
        def _(pe):
            def unit_ready(u):
                pe.wait_ge(w_split, 2 * u + 2)

            def three_pass(out, unit_slot, k, wcols, rhs_hi, rhs_lo, first, last):
                hi, lo = w_hi[:, unit_slot, wcols], w_lo[:, unit_slot, wcols]
                pe.matmul(out, hi, rhs_hi, start=first, stop=False)
                pe.matmul(out, hi, rhs_lo, start=False, stop=False)
                return pe.matmul(out, lo, rhs_hi, start=False, stop=last)

            def tile_job(bank, c, slot):
                for k in range(KT):
                    mm = three_pass(ps[:, bank, 0:CH], slot, k, slice(P * k, P * k + P),
                                    act_hi[:, k, cols(c)], act_lo[:, k, cols(c)], k == 0, k == KT - 1)
                mm.then_inc(job_done, 1)

            pe.wait_ge(made, 1)
            for k in range(KT):
                pe.wait_ge(sq_done, k + 1)
                for c in range(NC):
                    mm = pe.matmul(ps[:, c, 0:CH], ones[:, :], sq[k % 2][:, cols(c)], start=(k == 0), stop=(k == KT - 1))
                mm.then_inc(ss_done, 1)
            pe.wait_ge(mean_sq, NC)

            for j, (n, c) in enumerate(QK_ORDER):
                unit_ready(n)
                if n == 0:
                    pe.wait_ge(lo_done, KT // 2 * (c + 1))
                    pe.wait_ge(pool_lo, KT // 2 * (c + 1))
                if j >= 6:
                    pe.wait_ge(job_copied, j - 5)
                tile_job(j % 6, c, n % RING)
                if j == Q_ROWS_JOB:
                    pe.wait_ge(new_kept, 4)
                    for m in range(4):
                        mm = pe.transpose(ps[0:SAMP, 6, P * m:P * m + P], q_s[:, m, :], ident[:, :])
                    mm.then_inc(q_turned, 1)

            pe.wait_ge(new_kept, 8)
            for odd in range(2):
                if odd:
                    pe.wait_ge(self_scores, 1)
                r = slice(HD * odd, HD * odd + HD)
                for n in range(4):
                    mm = pe.matmul(ps[0:SAMP, 7, 2 * n + odd:256:HEADS], k_s[r, n, :],
                                   q_s[r, n, :].rearrange("p (b t) -> p t b", b=NB), start=True, stop=True)
                mm.then_inc(self_scores, 1)

            for i in range(V_JOBS):
                j, vb, tt = QK_JOBS + i, i // VT, i % VT
                m = P if tt < VT - 1 else SAMP
                tk = slice(P * tt, P * tt + m)
                if tt == 0:
                    unit_ready(QK_UNITS + 2 * vb + 1)
                pe.wait_ge(job_copied, j - 5)
                for k in range(KT):
                    u = QK_UNITS + 2 * vb + k // 4
                    hi, lo = (last_hi, last_lo) if u == CONV0 - 1 else (w_hi[:, u % RING], w_lo[:, u % RING])
                    wc = slice(256 * (k % 4), 256 * (k % 4) + 256)
                    out = ps[0:m, i % 6, 0:256]
                    pe.matmul(out, act_hi[:, k, tk], hi[:, wc], start=(k == 0), stop=False)
                    pe.matmul(out, act_hi[:, k, tk], lo[:, wc], start=False, stop=False)
                    mm = pe.matmul(out, act_lo[:, k, tk], hi[:, wc], start=False, stop=(k == KT - 1))
                mm.then_inc(job_done, 1)

            def new_maxima(step):
                pe.wait_ge(top_ready, step + 1)
                if step == 0:
                    pe.transpose(ps[0:64, 7, 0:P], top_cls[:, :], ident[:, :])
                    for t in range(NT):
                        mm = pe.transpose(ps[0:64, 7, P + SAMP * t:P + SAMP * t + SAMP],
                                          s_self[:, t].rearrange("p b h -> p (b h)"), ident[0:SAMP, 0:SAMP])
                    for t in range(NT):
                        mm = pe.transpose(ps[0:64, 6, P * t:P * t + P], s_near[:, t].rearrange("p b h -> p (b h)"),
                                          ident[:, :])
                elif step == 1:
                    mm = pe.transpose(ps[0:NT, 7, 256:320], top_col[:, :], ident[0:64, 0:64])
                else:
                    mm = pe.matmul(ps[:, 6, 0:256], ones[0:NT, :], top_diag[:, :, :].rearrange("p t x -> p (t x)"),
                                   start=True, stop=True)
                mm.then_inc(new_pe, 1)

            for p in range(4):
                for kind in range(3):
                    n = 3 * p + kind
                    unit_ready(CONV0 + n)
                    for c in range(NC):
                        j = QK_JOBS + V_JOBS + NC * n + c
                        pe.wait_ge(job_copied, j - (2 if n % 3 == 0 else 5))
                        tile_job(3 * (kind % 2) + c, c, n % RING)
                        if p == 3 and NC * kind + c in MAXIMA_BEHIND:
                            new_maxima(MAXIMA_BEHIND.index(NC * kind + c))

            pe.wait_ge(job_copied, IN_JOBS)

            def to_channels(b):
                pe.wait_ge(ob_done, b + 1)
                for n in range(4):
                    mm = pe.matmul(ps[:, 0, 32 * n + 4 * b:32 * n + 4 * b + 4], o_b[:, P * n:P * n + P],
                                   sel_t[:, :], start=True, stop=True)
                mm.then_inc(new_turned, 1)

            for b in range(NB):
                vt = v_tiles[b % 2]
                out = ps[0:SAMP, 2 + b % 2, :]
                pe.wait_ge(v_ld[b % 2], 144 * (b // 2 + 1))
                if b == 0:
                    pe.wait_ge(new_exp, 10)
                if b >= 2:
                    pe.wait_ge(ob_done, b - 1)
                for j in range(6):
                    p_j = p_cls5[:, j, b] if j < 5 else p_rest[:, b]
                    pe.matmul(out, p_j.rearrange("p t h -> p (t h)"), vt[:, j, :], start=(j == 0), stop=False)
                pe.matmul(out, p_near[:, b].rearrange("p t h -> p (t h)"), vt[:, 6, :], start=False, stop=False)
                pe.matmul(out, p_self[:, b].rearrange("p t h -> p (t h)"), v_s[:, :], start=False,
                          stop=True).then_inc(new_pv, 1)
                if b == 0:
                    pe.wait_ge(l_ready, 1)
                    for i in range(NB):
                        mm = pe.matmul(ps[0:SAMP, 1, i:i + 1], l_all[:, 32 * i:32 * i + 32], ones[:, 0:1],
                                       start=True, stop=True)
                    mm.then_inc(new_pe, 1)
                if b >= 1:
                    to_channels(b - 1)
            to_channels(NB - 1)
            pe.wait_ge(new_mixed, 1)

            def scores(it, s):
                it, back, s = lagged(it, s)
                hh, i = divmod(s, KT)
                if i == 0:
                    pe.wait_ge(st_in[hh], 112 * it + 112 * (1 - back))
                if not (is_first(it, back) and s < 2):
                    pe.wait_ge(biased, 16 * it + s - 1 - 16 * back)
                q = st_q[hh][:, P * i:P * i + P]
                for half, width in score_blocks(i):
                    kc = slice(512 * half, 512 * half + width)
                    out = ps[:, 2 * (s % 2) + half, 0:width]
                    pe.matmul(out, q, st_khi[hh][:, kc], start=True, stop=False)
                    mm = pe.matmul(out, q, st_klo[hh][:, kc], start=False, stop=True)
                mm.then_inc(scored, 1)

            def turn(it, s):
                it, back, s = lagged(it, s)
                done, per = (pool_normed, 2 * (KT - POOL_TILE)) if s % KT >= POOL_TILE else (normed, 2 * POOL_TILE)
                pe.wait_ge(done, per * it + norstd_through(s) - per * back)
                for f, (fs, bank, k0, nk) in enumerate(FILLS):
                    if fs != s:
                        continue
                    if not (is_first(it, back) and f < 3):
                        pe.wait_ge(pt_lo_done, 24 * it + f - 2 - 24 * back)
                    for k in range(nk):
                        mm = pe.transpose(ps[:, bank, P * k:P * k + P],
                                          prow[s % PROWS][:, P * (k0 + k):P * (k0 + k) + P], ident[:, :])
                    mm.then_inc(turned, 1)

            def values(it, s):
                it, back, s = lagged(it, s)
                u = s // 2
                hh, i = divmod(s, KT)
                pe.wait_ge(pt_lo_done, 24 * it + fills_through(s) - 24 * back)
                if not (is_first(it, back) and u == 0):
                    pe.wait_ge(o_sum, 8 * it + u - 8 * back)
                for k in range(i + 1):
                    qs = slice(P, 256) if k == i else slice(0, 256)
                    out = ps[:, 7, qs]
                    pe.matmul(out, st_v[hh][:, k, :], pts_hi[u % 2][:, k, qs], start=(k == 0), stop=False)
                    mm = pe.matmul(out, st_v[hh][:, k, :], pts_lo[u % 2][:, k, qs], start=False, stop=(k == i))
                mm.then_inc(pv_done, 1)

            def tick(it, s, first=False, last=False):
                if (s - VALUES_LAG) % 2 == 1 and in_range(s - VALUES_LAG, first, last):
                    values(it, s - VALUES_LAG)
                if in_range(s - TURN_LAG, first, last):
                    turn(it, s - TURN_LAG)
                if not last:
                    scores(it, s)

            for s in range(16):
                tick(0, s, first=True)
            with pe.Fori(1, 4) as it:
                for s in range(16):
                    tick(it, s)
            for s in range(LAST_TICKS):
                tick(4, s, last=True)
            pe.wait_ge(o_sum, 32)

            pe.wait_ge(mix_lo, 4 * HEADS)
            pe.wait_ge(new_mixed, 2)
            pe.wait_ge(conv_free, 5)
            def sum_of_squares(which, c):
                pe.wait_ge((h_ss, last_ss)[which], chunk_end(which, c))
                if which == 0 and c == 2:
                    pe.wait_ge(mean_sq, NC + 1)
                bank = 6 + c % 2 if which == 0 else c
                pe.matmul(ps[:, bank, 0:CH], ones[:, :], ssum[:, cols(c)], start=True, stop=True).then_inc(ss_all, 1)

            for j, (n, c) in enumerate(OUT_ORDER):
                unit_ready(OUT0 + n)
                if j >= 6:
                    pe.wait_ge(h_done, j - 5)
                for k in range(KT):
                    hi, lo = (act_hi, act_lo) if k < 4 else (pair_hi, pair_lo)
                    mm = three_pass(ps[:, j % 6, 0:CH], (OUT0 + n) % RING, k, slice(P * k, P * k + P),
                                    hi[:, k % 4, cols(c)], lo[:, k % 4, cols(c)], k == 0, k == KT - 1)
                mm.then_inc(job_done, 1)
                if j in SUMS_BEHIND:
                    sum_of_squares(0, SUMS_BEHIND.index(j))

            def gate_up(it, g, first=False):
                if first:
                    for i, (n, c) in enumerate(FIRST_GATES):
                        if n == 0:
                            pe.wait_ge(lo_done, LOWS + KT * (c + 1))
                        unit_ready(FFN0 + n)
                        tile_job(3 * n + c, c, (FFN0 + n) % RING)
                        if i == 0:
                            sum_of_squares(0, 2)
                for n in range(2 if first else 0, 4):
                    u = FFN0 + n if first else FFN0 + 6 * g - 2 + n
                    unit_ready(12 * it + u)
                    for c in range(NC):
                        if n >= 2:
                            i = FIRST_GATES.index((n - 2, c)) if first else 3 * (n - 2) + c
                            pe.wait_ge(silu_done, 12 * it + 6 * g + i + 1)
                        else:
                            pe.wait_ge(hidden, 12 * it + 6 * (g - 1) + 3 * n + c + 1)
                        tile_job(3 * (n % 2) + c, c, u % RING)

            def down(it, g, last=False):
                u0 = UNITS - 2 if last else FFN0 + 6 * (g + 1) + 2
                unit_ready(u0 + 1 if last else 12 * it + u0 + 1)
                pe.wait_ge(hid_lo, 12 * it + 6 * g + 6)
                if last:
                    pe.wait_ge(added, NC * KT * (GROUPS - 1))
                else:
                    pe.wait_ge(hidden, 12 * it + 6 * (g + 1) + 1)
                for i in range(NC * KT):
                    n, c = LAST_ORDER[i] if last else divmod(i, NC)
                    if i >= 2:
                        if last:
                            pe.wait_ge(h_done, NC * KT + i - 1)
                        else:
                            pe.wait_ge(added, 48 * it + 24 * g + i - 1)
                    for f in range(2):
                        hi, lo = (last_hi, last_lo) if last and f else (w_hi[:, (u0 + f) % RING], w_lo[:, (u0 + f) % RING])
                        hi, lo = hi[:, P * n:P * n + P], lo[:, P * n:P * n + P]
                        out = ps[:, 6 + i % 2, 0:CH]
                        x_hi, x_lo = (t[:, 2 * (g % 2) + f, cols(c)] for t in (pair_hi, pair_lo))
                        pe.matmul(out, hi, x_hi, start=(f == 0), stop=False)
                        pe.matmul(out, hi, x_lo, start=False, stop=False)
                        mm = pe.matmul(out, lo, x_hi, start=False, stop=(f == 1))
                    mm.then_inc(job_done, 1)
                    if last and i in LAST_SUMS_BEHIND:
                        sum_of_squares(1, LAST_SUMS_BEHIND.index(i))
                if last:
                    sum_of_squares(1, 2)

            gate_up(0, 0, first=True)
            with pe.Fori(0, 5) as it:
                for g in (1, 2):
                    gate_up(it, g)
                    down(it, g - 1)
            down(5, 0, last=True)

        @block.scalar
        def _(act):
            def copy(out, in_):
                return act.activation(out, in_, ACT.Copy)

            def take_root(which, c):
                act.wait_ge(mean_sq, NC * which + c + 1)
                act.activation(rstd[:, cols(c)], rstd[:, cols(c)], ACT.Sqrt).then_inc(root, 1)

            def normal_hi(which, c):
                for k in range(KT):
                    i = KT * c + k
                    act.wait_ge(y_done, NC * KT * which + i + 1)
                    copy(act_hi[:, k, cols(c)], norm_slot(which, i)).then_inc(hi_done, 1)

            for k in range(KT):
                act.wait_ge(x_in[k], 16)
                if k >= 2:
                    act.wait_ge(ss_done, k - 1)
                act.activation(sq[k % 2], res[:, k, :], ACT.Square).then_inc(sq_done, 1)
            for c in range(NC):
                take_root(0, c)
            for c in range(NC):
                normal_hi(0, c)

            for j in range(QK_JOBS + V_JOBS):
                act.wait_ge(job_done, j + 1)
                if j >= 2:
                    act.wait_ge(part_lo, j - 1)
                if rows_before(j):
                    act.wait_ge(rows_stored[j % 2], 16 * rows_before(j))
                if j < QK_JOBS:
                    copy(out32[:, j % 2, :], ps[:, j % 6, 0:CH]).then_inc(job_copied, 1)
                else:
                    i = j - QK_JOBS
                    m = P if i % VT < VT - 1 else SAMP
                    copy(out32[0:m, j % 2, 0:256], ps[0:m, i % 6, 0:256]).then_inc(job_copied, 1)
                if j == Q_ROWS_JOB:
                    act.wait_ge(q_turned, 1)
                    copy(q_rows, ps[0:SAMP, 6, :]).then_inc(q_rows_done, 1)

            act.wait_ge(conv_free, 1)
            for p in range(4):
                if p:
                    act.wait_ge(conv_free, p + 1)
                for kind in range(3):
                    for c in range(NC):
                        act.wait_ge(job_done, QK_JOBS + V_JOBS + 9 * p + 3 * kind + c + 1)
                        copy((h_c, c_c, b_c)[kind][:, cols(c)],
                             ps[:, 3 * (kind % 2) + c, 0:CH]).then_inc(job_copied, 1)

            act.wait_ge(shifted, 1)
            act.activation(p_near[:, :, :, :].rearrange("p b t h -> p t b h"), s_near[:, :, :, :],
                           ACT.Exp).then_inc(new_exp, 1)
            act.activation(p_self[:, :, :, :].rearrange("p b t h -> p t b h"), s_self[:, :, :, :],
                           ACT.Exp).then_inc(new_exp, 1)
            for t in range(NT):
                q = slice(32 * t, 32 * t + 32)
                act.activation(p_cls5[q, :, :, t, :], s_cls[q, 0:5, :, :], ACT.Exp).then_inc(new_exp, 1)
                act.activation(p_rest[q, :, t, :], s_cls[q, 5, :, :], ACT.Exp).then_inc(new_exp, 1)

            for c in range(2):
                act.wait_ge(rows_stored[c], 16 * ROWS_STORED[c])

            def exponentials(it, s):
                act.wait_ge(biased, 16 * it + s + 1)
                n = P * (s % KT + 1)
                act.activation(prow[s % PROWS][:, 0:n], prow[s % PROWS][:, 0:n], ACT.Exp, scale=-1.0,
                               bias=row_neg[:, s % 4:s % 4 + 1],
                               accum_out=row_sum[:, s % 4:s % 4 + 1]).then_inc(exped, 1)

            def high(it, s):
                it, back, s = lagged(it, s)
                u = s // 2
                for f, (fs, bank, k0, nk) in enumerate(FILLS):
                    if fs != s:
                        continue
                    act.wait_ge(turned, 24 * it + f + 1 - 24 * back)
                    if not (is_first(it, back) and u < 2):
                        act.wait_ge(pv_done, 8 * it + u - 1 - 8 * back)
                    copy(pts_hi[u % 2][:, k0:k0 + nk, P * (s % 2):P * (s % 2) + P],
                         ps[:, bank, 0:P * nk].rearrange("p (k t) -> p k t", k=nk)).then_inc(pt_hi_done, 1)

            def lower_half(it, s):
                it, back, s = lagged(it, s)
                u = s // 2
                act.wait_ge(pv_done, 8 * it + u + 1 - 8 * back)
                if not (is_first(it, back) and u < 2):
                    act.wait_ge(o_sum, 8 * it + u - 1 - 8 * back)
                copy(o_low[u % 2], ps[HD:P, 7, 0:256]).then_inc(low_done, 1)

            def outputs(it, s):
                it, back, s = lagged(it, s)
                u = s // 2
                r = slice(HD * (u // 4), HD * (u // 4) + HD)
                act.wait_ge(o_sum, 8 * it + u + 1 - 8 * back)
                copy(act_hi[r, it - back, 256 * (u % 4):256 * (u % 4) + 256], o32[u % 2][r]).then_inc(mix_hi, 1)

            def tick(it, s, first=False, last=False):
                if not last:
                    exponentials(it, s)
                if (s - HALF_LAG) % 2 == 1 and in_range(s - HALF_LAG, first, last):
                    lower_half(it, s - HALF_LAG)
                if in_range(s - HIGH_LAG, first, last):
                    high(it, s - HIGH_LAG)
                if (s - MIX_LAG) % 2 == 1 and in_range(s - MIX_LAG, first, last):
                    outputs(it, s - MIX_LAG)

            for s in range(16):
                tick(0, s, first=True)
            with act.Fori(1, 4) as it:
                for s in range(16):
                    tick(it, s)
            for s in range(LAST_TICKS):
                tick(4, s, last=True)

            def square(which, j):
                n, c = H_ORDERS[which][j]
                act.wait_ge(h_done, NC * KT * which + j + 1)
                if j >= 6:
                    act.wait_ge((h_ss, last_ss)[which], j - 5)
                act.activation(sq6[j % 6], res[:, n, cols(c)], ACT.Square).then_inc(h_sq, 1)

            for j in range(NC * KT):
                square(0, j)
                if j in SUMS_BEHIND:
                    take_root(1, SUMS_BEHIND.index(j))
                    normal_hi(1, SUMS_BEHIND.index(j))
            take_root(1, 2)
            normal_hi(1, 2)

            def gates(it, g, first=False):
                job = OUT_JOB0 + 24 if first else 72 * it + FFN_JOB0 + 36 * g
                for i in range(6):
                    f, c = FIRST_GATES[i] if first else divmod(i, NC)
                    act.wait_ge(job_done, job + i + 1)
                    if not first:
                        act.wait_ge(hid_lo, 12 * it + 6 * (g - 1) + i + 1)
                    act.activation(silu[:, f, cols(c)], ps[:, 3 * f + c, 0:CH], ACT.Silu).then_inc(silu_done, 1)
                for i in range(6):
                    f, c = divmod(i, NC)
                    act.wait_ge(hidden, 12 * it + 6 * g + i + 1)
                    if not first:
                        act.wait_ge(job_done, job)
                    copy(pair_hi[:, 2 * (g % 2) + f, cols(c)], silu[:, f, cols(c)]).then_inc(hid_hi, 1)

            gates(0, 0, first=True)
            with act.Fori(0, 5) as it:
                for g in (1, 2):
                    gates(it, g)
            for j in range(NC * KT):
                square(1, j)
                if j - 1 in LAST_SUMS_BEHIND:
                    take_root(2, LAST_SUMS_BEHIND.index(j - 1))
            take_root(2, 2)

        @block.vector
        def _(dve):
            chain = Chain(dve, dve_chain)

            def count_steps(out, age, age_i, n_i, a, b, scale):
                yield chain(dve.tensor_copy(age, age_i))
                yield chain(dve.tensor_scalar(n_i, age_i, 3, None, ALU.bitwise_and))
                yield chain(dve.tensor_scalar(b, n_i, 0.0, None, ALU.is_equal))
                yield chain(dve.scalar_tensor_tensor(a, age, 512.0, b, ALU.is_le, ALU.mult))
                yield chain(dve.scalar_tensor_tensor(a, age, 128.0, a, ALU.is_le, ALU.add))
                yield chain(dve.tensor_scalar(n_i, age_i, 15, None, ALU.bitwise_and))
                yield chain(dve.tensor_scalar(b, n_i, 0.0, None, ALU.is_equal))
                yield chain(dve.scalar_tensor_tensor(b, age, 2048.0, b, ALU.is_le, ALU.mult))
                yield chain(dve.tensor_tensor(a, a, b, ALU.add))
                yield chain(dve.scalar_tensor_tensor(a, age, 0.0, a, ALU.is_ge, ALU.mult))
                yield chain(dve.tensor_scalar(b, a, 0.0, MASKED * scale, ALU.is_equal, ALU.mult))
                yield chain(dve.tensor_scalar(out, a, 2.0, LN2 * scale, ALU.is_equal, ALU.mult))
                yield chain(dve.tensor_tensor(out, out, b, ALU.add))
                yield chain(dve.tensor_scalar(b, a, 3.0, LN3 * scale, ALU.is_equal, ALU.mult))
                yield chain(dve.tensor_tensor(out, out, b, ALU.add))

            def count_log(*args):
                for _ in count_steps(*args):
                    pass

            def mean_square(which, c):
                if which == 0:
                    dve.wait_ge(ss_done, KT)
                else:
                    dve.wait_ge(ss_all, NC * (which - 1) + c + 1)
                bank = 6 + c % 2 if which == 1 else c
                dve.tensor_scalar(rstd[:, cols(c)], ps[:, bank, 0:CH], 1.0 / D, EPS, ALU.mult, ALU.add).then_inc(mean_sq, 1)

            def normal(which, c, k, dst):
                if k == 0:
                    dve.wait_ge(root, NC * which + c + 1)
                    chain(dve.reciprocal(rstd[:, cols(c)], rstd[:, cols(c)]))
                dve.scalar_tensor_tensor(dst, res[:, k, cols(c)], g_sb[:, which, k:k + 1], rstd[:, cols(c)],
                                         ALU.mult, ALU.mult).then_inc(y_done, 1)

            def norm(which, c):
                def low(i):
                    k = i % KT
                    if which == 0 and k % 2:
                        return
                    dve.wait_ge(hi_done, NC * KT * which + i + 1)
                    dve.tensor_tensor(act_lo[:, k, cols(c)], norm_slot(which, i), f32(act_hi[:, k, cols(c)]),
                                      ALU.subtract).then_inc(lo_done, 1)

                for k in range(KT):
                    i = KT * c + k
                    if which == 0 and i >= 6:
                        dve.wait_ge((lo_done, pool_lo)[k % 2], i // 2 - 2)
                    elif which and i >= 2:
                        dve.wait_ge(lo_done, LOWS + i - 1)
                    normal(which, c, k, norm_slot(which, i))
                    if k >= 1:
                        low(i - 1)
                low(KT * c + KT - 1)

            dve.wait_ge(consts_in, 48)
            for c in range(NC):
                mean_square(0, c)
            for c in range(NC):
                norm(0, c)
            dve.memset(neg8slope[:, :], -8.0 * SLOPE[0]).then_inc(key_used, 3)

            def low_part(j, hi, lo, src, wait):
                dve.wait_ge(part_hi, wait)
                dve.tensor_tensor(lo, src, f32(hi), ALU.subtract).then_inc(part_lo, 1)

            def keys(n):
                b, which = divmod(n, 3)
                if which < 2:
                    k_blk, ld = ((k_far, ld_far), (k_mid, ld_mid))[which]
                    dve.wait_ge(ld, 64 * b + 64)
                    dve.wait_ge(ld_qc, 16 * b + 16)
                    pr = prod[:, 0:1536].rearrange("p (j n) -> p j n", j=3)
                    kv = k_blk.rearrange("p (j n) -> p j n", j=3)
                    qv = qc.unsqueeze(1).broadcast_to([P, 3, DA])
                    dst, nj = s_cls[:, 3 * which:3 * which + 3, b, :], 3
                else:
                    dve.wait_ge(ld_near, 16 * b + 16)
                    dve.wait_ge(ld_qn, 16 * b + 16)
                    pr = prod.rearrange("p (j n) -> p j n", j=NT)
                    kv = k_near.unsqueeze(1).broadcast_to([P, NT, DA])
                    qv = qn.rearrange("p (j n) -> p j n", j=NT)
                    dst, nj = s_near[:, :, b, :], NT
                if n:
                    dve.wait_ge(key_sum, n)
                dve.tensor_tensor(pr, kv, qv, ALU.mult).then_inc(key_used, 1)
                dve.wait_ge(key_used, n + 4)
                dve.tensor_reduce(dst, prod[:, 0:nj * DA].rearrange("p (j h d) -> p j h d", j=nj, h=HEADS),
                                  AX.X, ALU.add).then_inc(key_sum, 1)

            his = 0
            for j in range(QK_JOBS + V_JOBS):
                dve.wait_ge(job_copied, j + 1)
                src, hl = out32[:, j % 2, :], out_hl[:, j % 2, :]
                if j < QK_JOBS:
                    n, c = QK_ORDER[j]
                    if c == NC - 1:
                        keep, scale = (q_s, HD ** -0.5) if n < 4 else (k_s, 1.0)
                        dve.tensor_scalar(keep[:, n % 4, :], src[:, CH - SAMP:CH], scale, None,
                                          ALU.mult).then_inc(new_kept, 1)
                    hi, lo = hl[:, 0:CH], hl[:, CH:2 * CH]
                else:
                    vb, tt = divmod(j - QK_JOBS, VT)
                    src = src[:, 0:256].rearrange("p (h d) -> p h d", h=4)
                    parts = hl[:, 0:512].rearrange("p (h s d) -> p h s d", h=4, s=2)
                    hi, lo = parts[:, :, 0, :], parts[:, :, 1, :]
                if j >= QK_JOBS and tt == VT - 1:
                    dve.tensor_copy(v_s[:, 256 * vb:256 * vb + 256],
                                    out32[0:SAMP, j % 2, 0:256]).then_inc(part_lo, 1)
                else:
                    if parts_before(j):
                        dve.wait_ge(part_stored[j % 2], 16 * parts_before(j))
                    dve.tensor_copy(hi, src).then_inc(part_hi, 1)
                    his += 1
                    low_part(j, hi, lo, src, his)
                if j + 1 in KEYS_BEHIND:
                    keys(KEYS_BEHIND.index(j + 1))

            dve.wait_ge(made, 2)
            count_log(cnt_cls[:, :], age_cls[:, :], age_cls_i[:, :], cnt_i[:, 0:6], cnt_a[:, 0:6], cnt_b[:, 0:6], 1.0)
            count_log(cnt_near[:, :], age_near[:, :], age_near_i[:, :], cnt_i[:, 0:4], cnt_a[:, 0:4], cnt_b[:, 0:4], 1.0)
            count_log(cnt_self[:, :], age_self[:, :], age_self_i[:, :, :].rearrange("p t b -> p (t b)"),
                      cnt_i[0:SAMP, :], cnt_a[0:SAMP, :], cnt_b[0:SAMP, :], 1.0)
            dve.wait_ge(q_rows_out, 16)
            dve.memset(u_c[:, 0:2], 0.0).then_inc(conv_free, 1)

            def new_tokens_shift():
                dve.wait_ge(self_scores, 2)
                dve.wait_ge(key_sum, 3 * NB)
                for c in range(2):
                    dve.wait_ge(part_stored[c], 16 * PARTS_STORED[c])
                chain(dve.memset(p_cls5, 0.0))
                chain(dve.memset(p_rest, 0.0))
                chain(dve.tensor_copy(s_self[:, :, :, :].rearrange("p t b h -> p (t b h)"), ps[0:SAMP, 7, 0:256]))
                for s, age, cnt, n in ((s_cls, age_cls, cnt_cls, P), (s_near, age_near, cnt_near, P),
                                       (s_self, age_self, cnt_self, SAMP)):
                    a3 = age[:, :].unsqueeze(2) if s is not s_self else age[:, :].rearrange("p (t b) -> p t b", t=NT)
                    c3 = cnt[:, :].unsqueeze(2) if s is not s_self else cnt[:, :].rearrange("p (t b) -> p t b", t=NT)
                    for h in range(HEADS):
                        view = s[:, :, :, h]
                        shape = list(view.shape)
                        chain(dve.scalar_tensor_tensor(view, a3.broadcast_to(shape), -SLOPE[h], view, ALU.mult, ALU.add))
                    full = s[:, :, :, :]
                    chain(dve.tensor_tensor(full, full, c3.unsqueeze(3).broadcast_to(list(full.shape)), ALU.add))
                dve.tensor_reduce(top_cls[:, :], s_cls[:, :, :, :].rearrange("p j b h -> p (b h) j"), AX.X,
                                  ALU.max).then_inc(top_ready, 1)
                dve.wait_ge(new_pe, 1)
                for k, (bank, c0, n) in enumerate(((7, 0, 32), (6, 0, P), (7, P, SAMP))):
                    chain(dve.tensor_reduce(top_part[:, k, :], ps[0:64, bank, c0:c0 + NT * n].rearrange("p (t n) -> p t n", t=NT),
                                            AX.X, ALU.max))
                chain(dve.tensor_tensor(top_col[:, :], top_part[:, 0, :], top_part[:, 1, :], ALU.max))
                dve.tensor_tensor(top_col[:, :], top_col[:, :], top_part[:, 2, :], ALU.max).then_inc(top_ready, 1)
                dve.wait_ge(new_pe, 2)
                dve.tensor_tensor(top_diag[:, :, :], ps[0:NT, 7, 256:320].unsqueeze(1).broadcast_to([NT, NT, 64]),
                                  ident[0:NT, 0:NT].unsqueeze(2).broadcast_to([NT, NT, 64]), ALU.mult).then_inc(top_ready, 1)
                dve.wait_ge(new_pe, 3)
                near = s_near[:, :, :, :].rearrange("p t b h -> p (t b h)")
                own = s_self[:, :, :, :].rearrange("p t b h -> p (t b h)")
                chain(dve.tensor_tensor(near, near, ps[:, 6, 0:256], ALU.subtract))
                chain(dve.tensor_tensor(own, own, ps[0:SAMP, 6, 0:256], ALU.subtract))
                for t in range(NT):
                    q = slice(32 * t, 32 * t + 32)
                    v = s_cls[q, :, :, :].rearrange("p j b h -> p j (b h)")
                    ins = dve.tensor_tensor(v, v, ps[q, 6, 64 * t:64 * t + 64].unsqueeze(1).broadcast_to([32, 6, 64]),
                                            ALU.subtract)
                    if t < NT - 1:
                        chain(ins)
                ins.then_inc(shifted, 1)
            for p in range(4):
                if p < 3:
                    keys(KEYS_EARLY + 4 * p)
                    keys(KEYS_EARLY + 4 * p + 1)
                else:
                    new_tokens_shift()
                dve.wait_ge(job_copied, QK_JOBS + V_JOBS + 9 * p + 6)
                chain(dve.tensor_tensor(u_c[:, 2:2 + PROMPT], c_c[:, 0:PROMPT], h_c[:, 0:PROMPT], ALU.mult))
                chain(dve.tensor_tensor(u_s[:, :, 2:6], c_c[:, PROMPT:].rearrange("p (b t) -> p b t", b=NB),
                                        h_c[:, PROMPT:].rearrange("p (b t) -> p b t", b=NB), ALU.mult))
                chain(dve.tensor_copy(u_s[:, :, 0:2], cst_sb[:, p, :, :]))
                acc_s = acc_c[:, PROMPT:].rearrange("p (b t) -> p b t", b=NB)
                for k in range(3):
                    w_k = taps_sb[:, p, k:k + 1]
                    for acc, u in ((acc_c[:, 0:PROMPT], u_c[:, k:k + PROMPT]), (acc_s, u_s[:, :, k:k + NT])):
                        if k == 0:
                            chain(dve.tensor_scalar(acc, u, w_k, None, ALU.mult))
                        else:
                            chain(dve.scalar_tensor_tensor(acc, u, w_k, acc, ALU.mult, ALU.add))
                chain(dve.tensor_copy(tail_sb[:, p, 0:2], u_c[:, PROMPT:PROMPT + 2]))
                chain(dve.tensor_copy(tail_sb[:, p, 2:18].rearrange("p (b t) -> p b t", b=NB), u_s[:, :, 4:6]))
                if p < 3:
                    keys(KEYS_EARLY + 4 * p + 2)
                    keys(KEYS_EARLY + 4 * p + 3)
                dve.wait_ge(job_copied, QK_JOBS + V_JOBS + 9 * p + 9)
                chain(dve.tensor_tensor(y_c, acc_c, b_c, ALU.mult))
                chain(dve.tensor_copy(pair_hi[:, p, :], y_c))
                dve.tensor_tensor(pair_lo[:, p, :], y_c, f32(pair_hi[:, p, :]), ALU.subtract).then_inc(conv_free, 1)
            dve.wait_ge(conv_free, 5)

            dve.wait_ge(new_exp, 10)
            chain(dve.tensor_reduce(l_all, resid[:, 7168:8448].rearrange("p (j x) -> p x j", j=5), AX.X, ALU.add))
            chain(dve.tensor_tensor(l_all, l_all, spare[:, 0:256], ALU.add))
            chain(dve.tensor_tensor(l_all, l_all, spare[:, 256:512], ALU.add))
            dve.tensor_tensor(l_all[0:SAMP], l_all[0:SAMP], spare[0:SAMP, 512:768], ALU.add).then_inc(l_ready, 1)
            for c in range(2):
                dve.wait_ge(rows_stored[c], 16 * ROWS_STORED[c])
            tables = count_steps(count8, age_f, age_i[:, :], bias_h[1].bitcast(I16)[:, 0:1024], bias_h[0],
                                 out32[:, :, :].rearrange("p a t -> p (a t)")[:, 0:1024], 8.0)
            dve.wait_ge(new_pe, 4)
            chain(dve.reciprocal(sum_rec[:, :], ps[0:SAMP, 1, 0:NB]))
            for b in range(NB):
                dve.wait_ge(new_pv, b + 1)
                if b >= 1:
                    dve.wait_ge(new_turned, b)
                dve.scalar_tensor_tensor(o_b, ps[0:SAMP, 2 + b % 2, :], sum_rec[:, b:b + 1],
                                         head_mask[:, :, :].rearrange("p h d -> p (h d)"), ALU.mult,
                                         ALU.mult).then_inc(ob_done, 1)
                for _ in range(2):
                    next(tables, None)
            dve.wait_ge(new_turned, NB)
            dve.tensor_copy(o_s, ps[:, 0, 0:P]).then_inc(new_mixed, 1)
            dve.wait_ge(new_mixed, 1)
            o4 = o_s.rearrange("p (n t) -> p n t", n=4)
            chain(dve.tensor_copy(act_hi[:, 0:4, PROMPT:TOK], o4))
            dve.tensor_tensor(act_lo[:, 0:4, PROMPT:TOK], o4, f32(act_hi[:, 0:4, PROMPT:TOK]),
                              ALU.subtract).then_inc(new_mixed, 1)

            dve.wait_ge(new_mixed, 2)

            def head_bias(hh):
                chain(dve.scalar_tensor_tensor(bias_h[hh], age_f, neg8slope[:, 0:1], count8, ALU.mult, ALU.add))
                chain(dve.tensor_scalar(neg8slope[:, :], neg8slope[:, :], 0.5, None, ALU.mult))

            def reciprocals(it, s):
                it, back, s = lagged(it, s)
                dve.wait_ge(exped, 16 * it + s + 1 - 16 * back)
                dve.reciprocal(row_rec[:, s % 4:s % 4 + 1], row_sum[:, s % 4:s % 4 + 1]).then_inc(rec_done, 1)

            def biased_scores(it, s):
                hh, i = divmod(s, KT)
                n = P * (i + 1)
                dve.tensor_tensor_reduce(
                    prow[s % PROWS][:, 0:n],
                    ps[:, 2 * (s % 2):2 * (s % 2) + 2, :].rearrange("p a b -> p (a b)")[:, 0:n],
                    bias_h[hh][:, 896 - P * i:1024], -HD ** -0.5, 3e38, ALU.add, ALU.min,
                    row_neg[:, s % 4:s % 4 + 1]).then_inc(biased, 1)

            def normalise(it, s):
                it, back, s = lagged(it, s)
                n = P * (s % KT + 1)
                if s % KT >= POOL_TILE:
                    return
                dve.wait_ge(rec_done, 16 * it + s + 1 - 16 * back)
                dve.tensor_scalar(prow[s % PROWS][:, 0:n], prow[s % PROWS][:, 0:n], row_rec[:, s % 4:s % 4 + 1], None,
                                  ALU.mult).then_inc(normed, 1)

            def low_probs(it, s):
                it, back, s = lagged(it, s)
                u = s // 2
                for f, (fs, bank, k0, nk) in enumerate(FILLS):
                    if fs != s:
                        continue
                    dve.wait_ge(pt_hi_done, 24 * it + f + 1 - 24 * back)
                    qs = slice(P * (s % 2), P * (s % 2) + P)
                    dve.tensor_tensor(pts_lo[u % 2][:, k0:k0 + nk, qs],
                                      ps[:, bank, 0:P * nk].rearrange("p (k t) -> p k t", k=nk),
                                      f32(pts_hi[u % 2][:, k0:k0 + nk, qs]), ALU.subtract).then_inc(pt_lo_done, 1)

            def outputs(it, s):
                it, back, s = lagged(it, s)
                u = s // 2
                r = slice(HD * (u // 4), HD * (u // 4) + HD)
                if not (is_first(it, back) and u < 2):
                    dve.wait_ge(mix_lo, 8 * it + u - 1 - 8 * back)
                dve.wait_ge(low_done, 8 * it + u + 1 - 8 * back)
                dve.tensor_tensor(o32[u % 2][r], ps[0:HD, 7, 0:256], o_low[u % 2], ALU.add).then_inc(o_sum, 1)

            def mixed(it, s):
                it, back, s = lagged(it, s)
                u = s // 2
                r = slice(HD * (u // 4), HD * (u // 4) + HD)
                qs = slice(256 * (u % 4), 256 * (u % 4) + 256)
                dve.wait_ge(mix_hi, 8 * it + u + 1 - 8 * back)
                dve.tensor_tensor(act_lo[r, it - back, qs], o32[u % 2][r], f32(act_hi[r, it - back, qs]),
                                  ALU.subtract).then_inc(mix_lo, 1)

            def tick(it, s, first=False, last=False):
                if not last:
                    if s % KT == BIAS_TICK:
                        head_bias((s // KT + 1) % 2)
                    dve.wait_ge(scored, 16 * it + s + 1)
                    if not (first and s < PROWS):
                        back = 1 if s < PROWS else 0
                        dve.wait_ge(turned, 24 * it + fills_through((s - PROWS) % 16) - 24 * back)
                if in_range(s - 1, first, last):
                    reciprocals(it, s - 1)
                if not last:
                    biased_scores(it, s)
                if (s - SUM_LAG) % 2 == 1 and in_range(s - SUM_LAG, first, last):
                    outputs(it, s - SUM_LAG)
                if in_range(s - 1, first, last):
                    normalise(it, s - 1)
                if in_range(s - LOW_LAG, first, last):
                    low_probs(it, s - LOW_LAG)
                if (s - MIX_LOW_LAG) % 2 == 1 and in_range(s - MIX_LOW_LAG, first, last):
                    mixed(it, s - MIX_LOW_LAG)

            head_bias(0)
            for s in range(16):
                tick(0, s, first=True)
            with dve.Fori(1, 4) as it:
                start = chain.loop(it - 1, HEAD_CHAIN, 3)
                for s in range(16):
                    tick(it, s)
                chain.end(start)
            for s in range(LAST_TICKS):
                tick(4, s, last=True)

            def add_product(which, j):
                n, c = H_ORDERS[which][j]
                dve.wait_ge(job_done, (OUT_JOB0, LAST_JOB0)[which] + j + 1)
                if which == 0:
                    dve.wait_ge(x2_in[n], 16)
                bank = j % 6 if which == 0 else 6 + j % 2
                dve.tensor_tensor(res[:, n, cols(c)], ps[:, bank, 0:CH], res[:, n, cols(c)],
                                  ALU.add).then_inc(h_done, 1)

            def add_squares(j):
                n, c = OUT_ORDER[j]
                dve.wait_ge(h_sq, j + 1)
                if n == 0:
                    dve.tensor_copy(ssum[:, cols(c)], sq6[j % 6]).then_inc(h_ss, 1)
                else:
                    dve.wait_ge(h_ss, OUT_ORDER.index((n - 1, c)) + 1)
                    dve.tensor_tensor(ssum[:, cols(c)], ssum[:, cols(c)], sq6[j % 6], ALU.add).then_inc(h_ss, 1)

            for j in range(NC * KT):
                add_product(0, j)
                if j >= 1:
                    add_squares(j - 1)
                if j in SUMS_BEHIND:
                    mean_square(1, SUMS_BEHIND.index(j))
                    norm(1, SUMS_BEHIND.index(j))
            add_squares(NC * KT - 1)
            mean_square(1, 2)
            norm(1, 2)

            def hidden_of(it, g, first=False):
                job = OUT_JOB0 + 24 + 6 if first else 72 * it + FFN_JOB0 + 36 * g + 6

                def low(i):
                    f, c = divmod(i, NC)
                    dve.wait_ge(hid_hi, 12 * it + 6 * g + i + 1)
                    dve.tensor_tensor(pair_lo[:, 2 * (g % 2) + f, cols(c)], silu[:, f, cols(c)],
                                      f32(pair_hi[:, 2 * (g % 2) + f, cols(c)]), ALU.subtract).then_inc(hid_lo, 1)

                for i in range(6):
                    f, c = divmod(i, NC)
                    dve.wait_ge(job_done, job + i + 1)
                    dve.wait_ge(silu_done, 12 * it + 6 * g + (FIRST_GATES.index((f, c)) if first else i) + 1)
                    dve.tensor_tensor(silu[:, f, cols(c)], ps[:, 3 * f + c, 0:CH], silu[:, f, cols(c)],
                                      ALU.mult).then_inc(hidden, 1)
                    if i >= 1:
                        low(i - 1)
                low(5)

            hidden_of(0, 0, first=True)
            with dve.Fori(0, 5) as it:
                for g in (1, 2):
                    hidden_of(it, g)
                    for i in range(NC * KT):
                        n, c = divmod(i, NC)
                        dve.wait_ge(job_done, 72 * it + FFN_JOB0 + 36 * g + 12 + i + 1)
                        dve.tensor_tensor(res[:, n, cols(c)], ps[:, 6 + i % 2, 0:CH], res[:, n, cols(c)],
                                          ALU.add).then_inc(added, 1)
            tiles = []
            for j in range(NC * KT):
                add_product(1, j)
                if tiles:
                    normal(2, *tiles.pop(0))
                if j - 1 in LAST_SUMS_BEHIND:
                    c = LAST_SUMS_BEHIND.index(j - 1)
                    mean_square(2, c)
                    tiles += [(c, k, res[:, k, cols(c)]) for k in range(KT)]
            for tile in tiles:
                normal(2, *tile)
            mean_square(2, 2)
            for k in range(KT):
                normal(2, 2, k, res[:, k, cols(2)])


class Chain:

    def __init__(self, eng, sem):
        self.eng, self.sem, self.base, self.n = eng, sem, 0, 0

    def __call__(self, ins):
        ins.then_inc(self.sem, 1)
        self.n += 1
        self.eng.wait_ge(self.sem, self.base + self.n)

    def loop(self, it, per, turns):
        self.base, self.per, self.turns = it * per, per, turns
        return self.n

    def end(self, start):
        assert self.n - start == self.per, (self.n - start, self.per)
        self.base, self.n = 0, start + self.per * self.turns


QK_ORDER = [(n, c) for c in range(NC) for n in (0, 1)] + [(n, c) for n in range(2, QK_UNITS) for c in range(NC)]
OUT_ORDER = [(n, c) for n in range(OUT_UNITS - 3) for c in range(NC)] + [
    (n, c) for c in range(NC) for n in range(OUT_UNITS - 3, OUT_UNITS)]
LAST_ORDER = [(n, c) for c in range(NC) for n in range(KT)]
FIRST_GATES = [(f, c) for c in range(NC) for f in range(2)]
H_ORDERS = [OUT_ORDER, LAST_ORDER]
Q_ROWS_JOB = 13
KEYS_EARLY = 12
FIRST_KEYS_BEHIND = [7, 8, 9]
KEYS_BEHIND = [18 + 2 * n for n in range(KEYS_EARLY)]
MAXIMA_BEHIND = [4, 5, 6]
HEAD_CHAIN = 2 * 2
TURN_LAG, VALUES_LAG = 3, 5
HIGH_LAG, HALF_LAG, MIX_LAG = 1, 3, 4
LOW_LAG, SUM_LAG, MIX_LOW_LAG = 2, 4, 6
LAST_TICKS = MIX_LOW_LAG + 1
BIAS_TICK = 1
POOL_TILE = 2
OUT_JOB0 = IN_JOBS
FFN_JOB0 = OUT_JOB0 + 24 + 12 - 36
LAST_JOB0 = OUT_JOB0 + 24 + 12 + 36 * (GROUPS - 1)


LOWS = NC * KT // 2
SUMS_BEHIND = [18, 22]
LAST_SUMS_BEHIND = [11, 19]


def chunk_end(which, c):
    return max(j for j, (n, cc) in enumerate(H_ORDERS[which]) if cc == c) + 1


def jobs_through(u):
    if u < QK_UNITS:
        return QK_ORDER.index((u, NC - 1)) + 1
    if u < CONV0:
        return QK_JOBS + VT * ((u - QK_UNITS) // 2 + 1)
    if u < OUT0:
        return QK_JOBS + V_JOBS + NC * (u - CONV0 + 1)
    if u < FFN0:
        return IN_JOBS + OUT_ORDER.index((u - OUT0, NC - 1)) + 1
    if u < FFN0 + 2:
        return IN_JOBS + len(OUT_ORDER) + FIRST_GATES.index((u - FFN0, NC - 1)) + 1
    if u < FFN0 + 4:
        return IN_JOBS + NC * (u - OUT0 + 1)
    g, s = divmod(u - FFN0 - 4, 6)
    base = OUT_JOB0 + 24 + 12 + 36 * g
    return base + (NC * (s + 1) if s < 4 else 36)


def parts_before(j):
    return sum(1 for i in range(j % 2, j, 2) if not (i >= QK_JOBS and (i - QK_JOBS) % VT == VT - 1))


def rows_before(j):
    return sum(1 for i in range(j % 2, j, 2) if i >= QK_JOBS // 2)


PARTS_STORED = [parts_before(QK_JOBS + V_JOBS), parts_before(QK_JOBS + V_JOBS + 1)]
ROWS_STORED = [rows_before(QK_JOBS + V_JOBS), rows_before(QK_JOBS + V_JOBS + 1)]


def fills():
    out = []
    for s in range(2 * KT):
        i = s % KT
        if i < 4:
            out.append((s, 0, i + 1))
        else:
            out += [(s, 0, 4), (s, 4, i - 3)]
    return [(s, 4 + f % 3, k0, n) for f, (s, k0, n) in enumerate(out)]


FILLS = fills()


def lagged(it, s):
    return it, (1 if s < 0 else 0), s % 16


def is_first(it, back):
    return isinstance(it, int) and it - back == 0


def in_range(s, first, last):
    return s >= 0 if first else s < 0 if last else True


def norstd_through(s):
    return sum(1 for i in range(s + 1) if (i % KT >= POOL_TILE) == (s % KT >= POOL_TILE))


def fills_through(s):
    return sum(1 for f in FILLS if f[0] <= s)


def score_blocks(i):
    n = P * (i + 1)
    return [(0, max(256, n))] if n <= 512 else [(0, 512), (1, max(256, n - 512))]


def weight_units(w_in, w_out, w_gate, w_up, w_down):
    def tile(w, c):
        return w[:, c:c + P].reshape(KT, P, P).transpose(1, 0, 2).reshape(P, 1024)

    def wide(w, c, half):
        return w[512 * half:512 * half + 512, c:c + 256].reshape(4, P, 256).transpose(1, 0, 2).reshape(P, 1024)

    def gates(g):
        return [tile(w_gate, 256 * g), tile(w_gate, 256 * g + P), tile(w_up, 256 * g), tile(w_up, 256 * g + P)]

    def downs(g):
        return [w_down[256 * g + P * f:256 * g + P * f + P, :] for f in range(2)]

    units = [tile(w_in, P * n) for n in range(8)]
    units += [wide(w_in, 2 * DA + 256 * vb, half) for vb in range(2) for half in range(2)]
    for p in range(4):
        units += [tile(w_in, 3 * DA + off + P * p) for off in (0, 2 * (D - DA), D - DA)]
    units += [tile(w_out, P * n) for n in range(KT)]
    units += gates(0)
    for g in range(1, GROUPS):
        units += gates(g) + downs(g - 1)
    units += downs(GROUPS - 1)
    return np.ascontiguousarray(np.stack(units))


def kernel(x_prompt, x_sample, state_attn_k, state_attn_v, state_conv, norm_mix_g, w_in, w_conv, w_out,
           norm_ffn_g, w_gate, w_up, w_down, norm_final_g):
    import concourse.bacc as bacc
    from concourse.bass_utils import run_bass_kernel_spmd

    a = np.ascontiguousarray
    x = np.concatenate([np.asarray(x_prompt)[0], np.asarray(x_sample).reshape(SAMP, D)])
    by_channel = lambda v: np.asarray(v).reshape(KT, P).T
    arrays = {
        "xT": a(x.T.reshape(KT, P, TOK).transpose(1, 0, 2)),
        "w": weight_units(*(np.asarray(m)[0] for m in (w_in, w_out, w_gate, w_up, w_down))),
        "gains": a(np.stack([by_channel(np.asarray(norm_mix_g)[0]), by_channel(np.asarray(norm_ffn_g)[0]),
                             by_channel(norm_final_g)], axis=1)),
        "taps": a(np.asarray(w_conv)[0].reshape(3, 4, P).transpose(2, 1, 0)),
        "conv_state": a(np.asarray(state_conv)[0].reshape(NB, 2, 4, P).transpose(3, 2, 0, 1)),
        "state_k": a(np.asarray(state_attn_k)[0].reshape(NB, PAST, DA)),
        "state_v": a(np.asarray(state_attn_v)[0].reshape(NB, PAST, DA)),
    }
    outs = {"yT": (P, KT, TOK), "kT": (4, P, TOK), "v": (TOK, DA), "conv_tail": (P, 4, 18)}
    nc = bacc.Bacc("TRN2", target_bir_lowering=False, num_devices=1, dynamic_dma_scratch_size=1024)
    args = [nc.dram_tensor(f"in_{n}", v.shape, F32, kind="ExternalInput").ap() for n, v in arrays.items()]
    args += [nc.dram_tensor(f"out_{n}", s, F32, kind="ExternalOutput").ap() for n, s in outs.items()]
    build(nc, *args)
    got = run_bass_kernel_spmd(nc, [{f"in_{n}": v for n, v in arrays.items()}], core_ids=[0]).results[0]
    y, k, v, tail = (np.asarray(got[f"out_{n}"]) for n in outs)

    y = y.transpose(2, 1, 0).reshape(TOK, D)
    k = k.transpose(2, 0, 1).reshape(TOK, HEADS, HD)
    v = v.reshape(TOK, HEADS, HD)
    tail = tail.transpose(2, 1, 0).reshape(18, D - DA)
    return (a(y[:PROMPT])[None], a(y[PROMPT:]).reshape(NB, NT, D),
            a(k[:PROMPT])[None, None], a(v[:PROMPT])[None, None], a(tail[:2])[None, None],
            a(k[PROMPT:]).reshape(1, NB, NT, HEADS, HD), a(v[PROMPT:]).reshape(1, NB, NT, HEADS, HD),
            a(tail[2:]).reshape(1, NB, 2, D - DA))
```
